# Optimizing a Trainium2 kernel written in Bass

```python
import jax, jax.numpy as jnp
from jax import lax
import numpy as np

D_MODEL = 1024
BATCH = 1
SEQ = 128
DEPTH = 2
DEC_BATCH = 1
DEC_SEQ = 512
PAST_LEN = 128

GRID_W = 64
GLA_HEADS = 4
GLA_DK = 128
GLA_DV = 256
GLA_LOWRANK = 16
GLA_TAU = 16.0
GLA_CHUNK = 64
FNET_GROUPS = 4
FNET_DG = 128
PEER_HEADS = 8
PEER_NKEYS = 128
PEER_DQ = 256
PEER_TOPK = 16
PEER_EXPERTS = PEER_NKEYS * PEER_NKEYS
PEER_BLOCK = 128
ROPE_THETA = 10000.0
EPS = 1e-6
QK_W = GLA_HEADS * GLA_DK
V_W = GLA_HEADS * GLA_DV
F_W = FNET_GROUPS * FNET_DG
IN_W = 2 * QK_W + 2 * V_W + 2 * GLA_LOWRANK + F_W + 2 * D_MODEL

kernel_name = "hybrid_gla_fnet_peer_diffusion_step"

def _rmsnorm(x, w):
    xf = x.astype(jnp.float32)
    y = xf * lax.rsqrt(jnp.mean(xf * xf, axis=-1, keepdims=True) + EPS)
    return (y * w).astype(x.dtype)

def _modulation(cond, w_mod, b_mod):
    m = jax.nn.silu(cond) @ w_mod + b_mod
    return jnp.split(m[:, None, :], 6, axis=-1)

def _heads(t, d):
    B, T, _ = t.shape
    return t.reshape(B, T, -1, d).transpose(0, 2, 1, 3)

def _rope_part(x, pos):
    half = x.shape[-1] // 2
    freqs = ROPE_THETA ** (-jnp.arange(half, dtype=jnp.float32) / half)
    ang = pos.astype(jnp.float32)[:, None] * freqs[None, :]
    cos = jnp.cos(ang).astype(x.dtype)
    sin = jnp.sin(ang).astype(x.dtype)
    x1, x2 = x[..., :half], x[..., half:]
    return jnp.concatenate([x1 * cos - x2 * sin, x1 * sin + x2 * cos], axis=-1)

def _rope_2d(x, row, col):
    d = x.shape[-1] // 2
    return jnp.concatenate([_rope_part(x[..., :d], row), _rope_part(x[..., d:], col)], axis=-1)

def _gla_chunked(q, k, v, g, s0):
    B, H, T, dk = q.shape
    dv = v.shape[-1]
    C = GLA_CHUNK
    N = T // C
    f32 = jnp.float32
    q = q.astype(f32).reshape(B, H, N, C, dk)
    k = k.astype(f32).reshape(B, H, N, C, dk)
    v = v.astype(f32).reshape(B, H, N, C, dv)
    g = g.astype(f32).reshape(B, H, N, C, dk)
    b = jnp.cumsum(g, axis=3)
    b_last = b[:, :, :, -1:, :]
    q_dec = q * jnp.exp(b)
    att = jnp.einsum('bhncd,bhnsd->bhncs', q_dec, k * jnp.exp(-b))
    att = jnp.where(jnp.tril(jnp.ones((C, C), bool)), att, 0.0)
    o_intra = jnp.einsum('bhncs,bhnse->bhnce', att, v)
    d_state = jnp.einsum('bhncd,bhnce->nbhde', k * jnp.exp(b_last - b), v)
    decay = jnp.exp(b_last[:, :, :, 0, :]).transpose(2, 0, 1, 3)

    def step(s, inp):
        dec, ds = inp
        return s * dec[..., None] + ds, s

    s_fin, s_prev = lax.scan(step, s0.astype(f32), (decay, d_state))
    o_inter = jnp.einsum('bhncd,nbhde->bhnce', q_dec, s_prev)
    return (o_intra + o_inter).reshape(B, H, T, dv), s_fin

def _bidir_gla(q, k, v, g_f, g_b, s_f0, s_b0):
    o_f, s_f = _gla_chunked(q, k, v, g_f, s_f0)
    flip = lambda t: t[:, :, ::-1]
    o_b, s_b = _gla_chunked(flip(q), flip(k), flip(v), flip(g_b), s_b0)
    return o_f + flip(o_b), s_f, s_b

def _token_mixer(h, rope_pos, s_f0, s_b0, w_in, w_af, b_af, w_ab, b_ab,
                 gla_norm, w_gla_out, w_four_out, w_out):
    B, T, _ = h.shape
    sizes = (QK_W, QK_W, V_W, V_W, GLA_LOWRANK, GLA_LOWRANK, F_W, D_MODEL, D_MODEL)
    cuts = np.cumsum(sizes)[:-1].tolist()
    q, k, v, r, lr_f, lr_b, u, z_gla, z_four = jnp.split(h @ w_in, cuts, axis=-1)
    q = _heads(q, GLA_DK) * (GLA_DK ** -0.5)
    k = _heads(k, GLA_DK)
    v = _heads(v, GLA_DV)
    if rope_pos is not None:
        row, col = rope_pos
        q = _rope_2d(q, row, col)
        k = _rope_2d(k, row, col)
    g_f = _heads(jax.nn.log_sigmoid((lr_f @ w_af + b_af).astype(jnp.float32)) / GLA_TAU, GLA_DK)
    g_b = _heads(jax.nn.log_sigmoid((lr_b @ w_ab + b_ab).astype(jnp.float32)) / GLA_TAU, GLA_DK)
    o, s_f, s_b = _bidir_gla(q, k, v, g_f, g_b, s_f0, s_b0)
    o = o * lax.rsqrt(jnp.mean(o * o, axis=-1, keepdims=True) + EPS)
    o = o.transpose(0, 2, 1, 3).reshape(B, T, V_W).astype(h.dtype) * gla_norm
    y_gla = (o * jax.nn.silu(r)) @ w_gla_out
    uf = u.reshape(B, T, FNET_GROUPS, FNET_DG).astype(jnp.float32)
    four = jnp.real(jnp.fft.fft2(uf, axes=(1, 3), norm='ortho')).reshape(B, T, F_W).astype(h.dtype)
    y_four = four @ w_four_out
    merged = jax.nn.sigmoid(z_gla) * y_gla + jax.nn.sigmoid(z_four) * y_four
    return merged @ w_out, s_f.astype(h.dtype), s_b.astype(h.dtype)

def _peer(h, w_query, sub_keys, expert_u, expert_v):
    B, T, D = h.shape
    n = B * T
    x = h.reshape(n, D)
    qry = (x @ w_query).reshape(n, PEER_HEADS, 2, PEER_DQ // 2)
    s = jnp.einsum('nhpd,hpkd->nhpk', qry, sub_keys).astype(jnp.float32)
    s1, i1 = lax.top_k(s[:, :, 0], PEER_TOPK)
    s2, i2 = lax.top_k(s[:, :, 1], PEER_TOPK)
    cand = (s1[..., :, None] + s2[..., None, :]).reshape(n, PEER_HEADS, PEER_TOPK * PEER_TOPK)
    cidx = (i1[..., :, None] * PEER_NKEYS + i2[..., None, :]).reshape(n, PEER_HEADS, PEER_TOPK * PEER_TOPK)
    top_s, sel = lax.top_k(cand, PEER_TOPK)
    idx = jnp.take_along_axis(cidx, sel, axis=-1)
    w = jax.nn.softmax(top_s, axis=-1)
    nblk = n // PEER_BLOCK

    def block(args):
        xb, ib, wb = args
        a = jax.nn.gelu(jnp.einsum('nd,nhkd->nhk', xb, expert_u[ib]).astype(jnp.float32))
        coef = (wb * a).astype(xb.dtype)
        return jnp.einsum('nhk,nhkd->nd', coef, expert_v[ib])

    out = lax.map(block, (x.reshape(nblk, PEER_BLOCK, D),
                          idx.reshape(nblk, PEER_BLOCK, PEER_HEADS, PEER_TOPK),
                          w.reshape(nblk, PEER_BLOCK, PEER_HEADS, PEER_TOPK)))
    return out.reshape(B, T, D)

def _trunk(x, cond, rope_pos, init_state, w_mod, b_mod, norm1, w_in, w_af, b_af, w_ab, b_ab,
           gla_norm, w_gla_out, w_four_out, w_out, norm2, w_query, sub_keys, expert_u,
           expert_v, final_norm):
    B = x.shape[0]
    finals = []
    for l in range(DEPTH):
        if init_state is None:
            s_f0 = jnp.zeros((B, GLA_HEADS, GLA_DK, GLA_DV), x.dtype)
            s_b0 = s_f0
        else:
            s_f0 = init_state[:, l, 0]
            s_b0 = init_state[:, l, 1]
        sh1, sc1, g1, sh2, sc2, g2 = _modulation(cond, w_mod[l], b_mod[l])
        h = _rmsnorm(x, norm1[l]) * (1 + sc1) + sh1
        mix, s_f, s_b = _token_mixer(h, rope_pos, s_f0, s_b0, w_in[l], w_af[l], b_af[l], w_ab[l],
                                     b_ab[l], gla_norm[l], w_gla_out[l], w_four_out[l], w_out[l])
        x = x + g1 * mix
        h = _rmsnorm(x, norm2[l]) * (1 + sc2) + sh2
        x = x + g2 * _peer(h, w_query[l], sub_keys[l], expert_u[l], expert_v[l])
        if init_state is None:
            finals.append(jnp.stack([s_f, s_b], axis=1))
    y = _rmsnorm(x, final_norm)
    if init_state is None:
        return y, jnp.stack(finals, axis=1)
    return y, None

def setup_inputs(seed: int = 0) -> dict:
    key = jax.random.key(seed)
    ks = jax.random.split(key, 24)
    f32 = jnp.float32
    nrm = lambda k, shape, s: jax.random.normal(k, shape, f32) * s
    D = D_MODEL
    return {
        "x_prompt": nrm(ks[0], (BATCH, SEQ, D), 1.0),
        "x_sample": nrm(ks[1], (DEC_BATCH, DEC_SEQ, D), 1.0),
        "state_gla": nrm(ks[2], (DEC_BATCH, DEPTH, 2, GLA_HEADS, GLA_DK, GLA_DV), 2.0),
        "c": nrm(ks[3], (DEC_BATCH, D), 1.0),
        "c_ctx": nrm(ks[4], (D,), 1.0),
        "w_mod": nrm(ks[5], (DEPTH, D, 6 * D), 0.5 * D ** -0.5),
        "b_mod": nrm(ks[6], (DEPTH, 6 * D), 0.02),
        "norm1": 1.0 + nrm(ks[7], (DEPTH, D), 0.02),
        "w_in": nrm(ks[8], (DEPTH, D, IN_W), D ** -0.5),
        "w_af": nrm(ks[9], (DEPTH, GLA_LOWRANK, QK_W), GLA_LOWRANK ** -0.5),
        "b_af": nrm(ks[10], (DEPTH, QK_W), 0.1),
        "w_ab": nrm(ks[11], (DEPTH, GLA_LOWRANK, QK_W), GLA_LOWRANK ** -0.5),
        "b_ab": nrm(ks[12], (DEPTH, QK_W), 0.1),
        "gla_norm": 1.0 + nrm(ks[13], (DEPTH, V_W), 0.02),
        "w_gla_out": nrm(ks[14], (DEPTH, V_W, D), V_W ** -0.5),
        "w_four_out": nrm(ks[15], (DEPTH, F_W, D), F_W ** -0.5),
        "w_out": nrm(ks[16], (DEPTH, D, D), D ** -0.5),
        "norm2": 1.0 + nrm(ks[17], (DEPTH, D), 0.02),
        "w_query": nrm(ks[18], (DEPTH, D, PEER_HEADS * PEER_DQ), D ** -0.5),
        "sub_keys": nrm(ks[19], (DEPTH, PEER_HEADS, 2, PEER_NKEYS, PEER_DQ // 2), (PEER_DQ // 2) ** -0.5),
        "expert_u": nrm(ks[20], (DEPTH, PEER_EXPERTS, D), D ** -0.5),
        "expert_v": nrm(ks[21], (DEPTH, PEER_EXPERTS, D), 1.0),
        "final_norm": 1.0 + nrm(ks[22], (D,), 0.02),
    }

def reference(x_prompt, x_sample, state_gla, c, c_ctx, w_mod, b_mod, norm1, w_in, w_af, b_af,
              w_ab, b_ab, gla_norm, w_gla_out, w_four_out, w_out, norm2, w_query, sub_keys,
              expert_u, expert_v, final_norm):
    weights = (w_mod, b_mod, norm1, w_in, w_af, b_af, w_ab, b_ab, gla_norm, w_gla_out,
               w_four_out, w_out, norm2, w_query, sub_keys, expert_u, expert_v, final_norm)
    y_prompt, new_state_gla = _trunk(x_prompt, c_ctx[None, :], None, None, *weights)
    T = x_sample.shape[1]
    rows = T // GRID_W
    row = jnp.repeat(jnp.arange(rows), GRID_W)
    col = jnp.tile(jnp.arange(GRID_W), rows)
    y_sample, _ = _trunk(x_sample, c, (row, col), state_gla, *weights)
    return (y_prompt, y_sample, new_state_gla)


_drawn_inputs = setup_inputs


def setup_inputs(seed=0):
    import zlib

    import numpy as np

    out = dict(_drawn_inputs(seed))
    spreads = {}
    factors = {'state_gla': 2.973, 'gla_norm': 3.782, 'final_norm': 2.822}
    for name, (base, spread) in spreads.items():
        noise = np.random.default_rng([zlib.crc32(name.encode()), seed]).standard_normal(out[name].shape)
        drawn = base * np.exp(spread * noise) if base else spread * noise
        out[name] = __import__('jax').numpy.asarray(drawn.astype(out[name].dtype))
    for name, factor in factors.items():
        out[name] = (out[name] * factor).astype(out[name].dtype)
    return out
```

```python
from contextlib import ExitStack

import concourse.bass as bass
import numpy as np
from concourse import mybir

F32 = mybir.dt.float32
U32 = mybir.dt.uint32
ALU = mybir.AluOpType
ACT = mybir.ActivationFunctionType
AX_X = mybir.AxisListType.X

P = 128
D = 1024
KC = D // P
DEPTH = 2
TP, TS = 128, 512
T = TP + TS
NT = T // P
GRID_W = 64
HEADS, DV = 4, 256
CHUNK = 64
NCH = T // CHUNK
LOWRANK = 16
TAU = 16.0
GROUPS = 4
QK_W, V_W, F_W = 512, 1024, 512
PH = 8
NKEYS = 128
TOPK = 16
EG = 4
EPS = 1e-6
ROPE_THETA = 10000.0
LOWEST = -3.0e38

Q0, K0, V0 = 0, QK_W, 2 * QK_W
R0 = V0 + V_W
L0 = R0 + V_W
U0 = L0 + 2 * LOWRANK
ZG0 = U0 + F_W
ZF0 = ZG0 + D

C_ID, C_ROT, C_IOTA, C_COS, C_SIN = 0, 128, 256, 384, 896
C_MF, C_MB, C_RESET, C_CDSD = 1408, 1536, 1664, 2304
C_W = 2560

START = 1
SLOTS = 6
WCOLS = 256
USES = [24, 12, 12, 9, 7, 6]
MOD_B = 6 * D // (SLOTS * WCOLS)
HEAD_N, UN, ZN = 4, 4, 8
ZN0, QN = 12, 16


def constants():
    c = np.zeros((P, C_W), np.float32)
    c[:, C_ID:C_ID + 128] = np.eye(128)
    rot = np.zeros((128, 128))
    for base in (0, 64):
        for i in range(32):
            rot[base + i, base + 32 + i] = -1.0
            rot[base + 32 + i, base + i] = 1.0
    c[:, C_ROT:C_ROT + 128] = rot.T
    c[:, C_IOTA:C_IOTA + 128] = np.arange(128)[None, :]
    freqs = (np.float32(ROPE_THETA) ** (-np.arange(32, dtype=np.float32) / np.float32(32))).astype(np.float32)
    tok = np.arange(TS)
    row, col = tok // GRID_W, tok % GRID_W
    for base, pos in ((0, row), (64, col)):
        ang = (pos.astype(np.float32)[None, :] * freqs[:, None]).astype(np.float32).astype(np.float64)
        for o in (0, 32):
            c[base + o:base + o + 32, C_COS:C_COS + TS] = np.cos(ang)
            c[base + o:base + o + 32, C_SIN:C_SIN + TS] = np.sin(ang)
    s, t = np.arange(128)[:, None], np.arange(128)[None, :]
    same = (s // CHUNK) == (t // CHUNK)
    c[:, C_MF:C_MF + 128] = same & (s <= t)
    c[:, C_MB:C_MB + 128] = same & (s >= t)
    c[:, C_RESET:C_RESET + T] = (np.arange(T) % CHUNK != 0)[None, :]
    a = 2 * np.pi * ((s * t) % 128) / 128
    c[:, C_CDSD:C_CDSD + 128] = np.cos(a) / np.sqrt(128)
    c[:, C_CDSD + 128:C_CDSD + 256] = np.sin(a) / np.sqrt(128)
    k, n = np.arange(TS)[:, None], np.arange(TS)[None, :]
    a5 = 2 * np.pi * ((k * n) % TS) / TS
    lat = np.stack([np.cos(a5), -np.sin(a5)], 1) / np.sqrt(TS)
    lat = lat.reshape(4, P, 2, TS).transpose(1, 0, 2, 3).reshape(P, -1)
    ctx = np.stack([np.cos(a), -np.sin(a)], 1).reshape(P, -1) / np.sqrt(TP)
    return c, np.concatenate([lat, ctx], 1).astype(np.float32)


TT_W = 4 * 2 * TS + 2 * TP


def build(nc, x_prompt, x_sample, state_gla, c, c_ctx, w_mod, b_mod, norm1, w_in, w_af, b_af, w_ab, b_ab,
          gla_norm, w_gla_out, w_four_out, w_out, norm2, w_query, sub_keys, expert_u, expert_v, final_norm,
          consts, fourier, y_prompt, y_sample, new_state):
    wd = nc.dram_tensor("expert_weights", [DEPTH, NKEYS, NKEYS, T], F32, kind="Internal").ap()

    cursor = [nc.sbuf_base + 31 & ~31]

    def place(name, shape, dt=F32, at=None):
        n = int(np.prod(shape[1:])) * 4
        off = cursor[0] if at is None else at[0]
        t = nc.alloc_sbuf_tensor_at(name, shape, dt, offset=off)
        nxt = (off + n + 31) & ~31
        if at is None:
            cursor[0] = nxt
        else:
            at[0] = nxt
        return t

    cst = place("cst", [P, C_W])
    xT = place("xT", [P, KC, T])
    hT = place("hT", [P, KC, T])
    ones = place("ones", [P, P])
    eps = place("eps", [P, 1])
    one = place("one", [P, 1])
    rows0 = place("rows0", [24, P])
    cols0 = place("cols0", [P, 24])
    scond = place("scond", [P, KC, 2])
    rows = place("rows", [80, P])
    cols = place("cols", [P, 80])
    modT = place("modT", [P, 48, 2])
    nscale = place("nscale", [P, 2, KC, 2])
    rs = place("rs", [P, T])
    base = cursor[0]

    m = [base]
    qk = place("qk", [P, 2, T], at=m)
    gx = place("gx", [P, 2, T], at=m)
    bx = place("bx", [P, 2, T], at=m)
    dx = place("dx", [P, 2, T], at=m)
    tmp = place("tmp", [P, 2, T], at=m)
    e2 = place("e2", [P, 2, T], at=m)
    kdT = place("kdT", [P, 2, NT, P], at=m)
    att = place("att", [P, 2, NT, P], at=m)
    hist = place("hist", [P, 2, 11, DV], at=m)
    v_sb = place("v_sb", [P, NT, DV], at=m)
    rsil = place("rsil", [P, 2, T], at=m)
    on = place("on", [P, NT, DV], at=m)
    tot = place("tot", [P, 2, NCH], at=m)
    dec = place("dec", [P, 2, NCH], at=m)
    oss = place("oss", [P, 8], at=m)
    ors = place("ors", [P, 8], at=m)
    wlr = place("wlr", [P, KC, 2 * LOWRANK], at=m)
    lrT = place("lrT", [2 * LOWRANK, T], at=m)
    wab = place("wab", [2 * LOWRANK, 2, P], at=m)
    oT = place("oT", [P, KC, T], at=m)
    ring0 = nc.sbuf_usable_end - SLOTS * KC * WCOLS * 4 & ~31
    assert m[0] <= ring0, (m[0], ring0)
    rg = [ring0]
    slot = [place(f"slot{i}", [P, KC, WCOLS], at=rg) for i in range(SLOTS)]
    f = [base]
    fourT = place("fourT", [P, GROUPS, T], at=f)
    uT = place("uT", [P, GROUPS, T], at=f)
    ab = place("ab", [P, NT, GROUPS, 2, P], at=f)
    table = place("table", [P, TT_W], at=f)
    assert f[0] <= base + 20 * T * 4 + 2 * 11 * DV * 4, f[0] - base
    f2 = [base + GROUPS * T * 4]
    mT = place("mT", [P, KC, T], at=f2)
    sg = place("sg", [P, 2, T], at=f2)
    mt = place("mt", [P, T], at=f2)

    p = [base]
    wsel = place("wsel", [P, 3, NT, P], at=p)
    wselT = place("wselT", [P, 3, T], at=p)
    onehot = place("onehot", [P, 2, 4, 2, P], at=p)
    pq = [p[0]]
    qryT = place("qryT", [P, 2, T], at=pq)
    skey = place("skey", [P, 2, P], at=pq)
    skT = place("skT", [P, 2, P], at=pq)
    sc = place("sc", [P, NT, 2, P], at=pq)
    top = place("top", [P, NT, 2, TOPK], at=pq)
    ti = place("ti", [P, NT, 2, TOPK], U32, at=pq)
    tif = place("tif", [P, NT, 2, TOPK], at=pq)
    cand = place("cand", [P, NT, TOPK, TOPK], at=pq)
    best = place("best", [P, NT, TOPK], at=pq)
    sel = place("sel", [P, NT, TOPK], U32, at=pq)
    selab = place("selab", [P, 2, NT, TOPK], U32, at=pq)
    self_ = place("self", [P, 2, NT, TOPK], at=pq)
    hot = place("hot", [P, 2, NT, TOPK, TOPK], at=pq)
    bsum = place("bsum", [P, NT], at=pq)
    assert pq[0] <= ring0
    wb = [p[0]]
    wbuf = [place(f"wbuf{i}", [P, NKEYS, P], at=wb) for i in range(2)]
    assert wb[0] <= nc.sbuf_usable_end, (wb[0], nc.sbuf_usable_end)
    e = [base]
    usb = [place(f"usb{i}", [P, D], at=e) for i in range(EG)]
    vsb = [place(f"vsb{i}", [P, D], at=e) for i in range(EG)]
    wex = [place(f"wex{i}", [P, T], at=e) for i in range(EG)]
    coef = [place(f"coef{i}", [P, T], at=e) for i in range(EG)]
    uTe = [place(f"uTe{i}", [P, KC, P], at=e) for i in range(2)]
    gel = [place(f"gel{i}", [P, T], at=e) for i in range(2)]
    accT = place("accT", [P, KC, T], at=e)
    assert e[0] <= ring0, (e[0], ring0)
    xnat = place("xnat", [P, NT, D], at=[base])
    ynat = place("ynat", [P, NT, D], at=[base])

    ident = cst[:, C_ID:C_ID + 128]
    rotT = cst[:, C_ROT:C_ROT + 128]
    iota = cst[:, C_IOTA:C_IOTA + 128]
    cos, sin = cst[:, C_COS:C_COS + TS], cst[:, C_SIN:C_SIN + TS]
    mask = [cst[:, C_MF:C_MF + 128].bitcast(U32), cst[:, C_MB:C_MB + 128].bitcast(U32)]
    reset = cst[:, C_RESET:C_RESET + T]
    cdsd = cst[:, C_CDSD:C_CDSD + 256]

    with ExitStack() as ctx:
        ps = [ctx.enter_context(nc.psum_tensor(f"bank{i}", [P, 512], F32)) for i in range(8)]

        semaphores = []

        def sem(name):
            semaphores.append(ctx.enter_context(nc.semaphore(name)))
            return semaphores[-1]

        def pool_load(name):
            return ctx.enter_context(nc.semaphore(name))

        s_const, s_x, s_rows = sem("const_loaded"), sem("x_loaded"), pool_load("rows_loaded")
        s_slot = [sem(f"slot{i}_loaded") for i in range(SLOTS)]
        s_wlr, s_wab, s_init, s_table = pool_load("wlr_loaded"), pool_load("wab_loaded"), pool_load("states_loaded"), sem("table_loaded")
        s_skey = pool_load("subkeys_loaded")
        s_u = [sem(f"expert_u{i}_loaded") for i in range(EG)]
        s_v = [sem(f"expert_v{i}_loaded") for i in range(EG)]
        s_w = [sem(f"expert_w{i}_loaded") for i in range(EG)]
        s_new, s_y = sem("new_state_stored"), sem("y_stored")
        s_wst = [sem(f"weights{i}_stored") for i in range(2)]
        s_set = sem("constants_set")
        s_xt, s_xc = sem("x_turned"), sem("x_copied")
        s_rowsT, s_cols = sem("rows_turned"), sem("cols_ready")
        s_econd, s_cond, s_mod, s_modT = sem("cond_exp"), sem("cond_ready"), sem("mod_mm"), sem("mod_ready")
        s_sq, s_ss, s_rs, s_h = sem("squares"), sem("square_sums"), sem("rstd"), sem("h_ready")
        s_lr, s_lrT = sem("lr_mm"), sem("lr_ready")
        s_qk, s_q, s_k = sem("qk_mm"), sem("q_copied"), sem("k_copied")
        s_gate, s_gx, s_gl, s_ex = sem("gate_mm"), sem("gate_x"), sem("gate_log"), sem("exponents")
        s_rot, s_dec = sem("rot_mm"), sem("decays_exp")
        s_vm, s_vc, s_rm, s_re, s_r = sem("v_mm"), sem("v_copied"), sem("r_mm"), sem("r_exp"), sem("r_silu")
        s_scal, s_kdm, s_kd = sem("qk_scaled"), sem("kd_turned"), sem("kd_copied")
        s_am, s_a, s_ds, s_st = sem("att_mm"), sem("att_masked"), sem("dstate_mm"), sem("state_step")
        s_om, s_on, s_ont, s_o = sem("o_mm"), sem("o_normed"), sem("o_turned"), sem("o_gated")
        s_um, s_uc, s_f1, s_f1c, s_f2, s_f2c = (sem("u_mm"), sem("u_copied"), sem("fourier_d"), sem("fourier_d_copied"),
                                               sem("fourier_t"), sem("fourier_ready"))
        s_zm, s_ym, s_ze, s_mg, s_out, s_x1 = (sem("z_mm"), sem("y_mm"), sem("z_exp"), sem("merged"), sem("out_mm"),
                                              sem("x_mixed"))
        s_qm, s_qc, s_kt, s_ktc, s_sm, s_sc = (sem("query_mm"), sem("query_copied"), sem("keys_turned"),
                                              sem("keys_copied"), sem("score_mm"), sem("scores_copied"))
        s_d, s_e, s_sel = sem("best_minus_max"), sem("best_exp"), sem("slots_chosen")
        s_tm, s_tc = sem("slots_turned"), sem("slots_ready")
        s_hot, s_wm, s_wc = sem("onehots"), sem("weights_mm"), sem("weights_copied")
        s_utm, s_utc, s_um2, s_gel, s_coef, s_vm2, s_acc, s_x2 = (
            sem("u_turned"), sem("uT_copied"), sem("expert_a"), sem("gelu_done"), sem("coef_ready"), sem("expert_out"),
            sem("expert_added"), sem("x_done"))
        s_yt, s_yc = sem("y_turned"), sem("y_copied")
        s_zero = sem("zeros_set")

        s_passed = sem("waits_passed")

        def hold(eng, semaphore, value):
            eng.wait_ge(semaphore, value)
            eng.sem_inc(s_passed, 1)

        for n, semaphore in enumerate(semaphores):
            (nc.sync, nc.scalar, nc.vector, nc.tensor)[n % 4].sem_inc(semaphore, START)
        nc.all_engine_barrier()

        block = ctx.enter_context(nc.Block())
        NWG = T // 4
        ZC, OC = KC, KC

        def wcols(w, l, c0):
            return w[l][:, c0:c0 + WCOLS].rearrange("(c p) n -> p c n", p=P)

        def wcols_at(w, l, c0):
            return w[l][:, bass.ds(c0, WCOLS)].rearrange("(c p) n -> p c n", p=P)

        @block.sync
        def _(sp):
            sp.dma_start(cst[:, :], consts).then_inc(s_const, 16)
            sp.dma_start(xnat[:, 0, :], x_prompt[0]).then_inc(s_x, 16)
            sp.dma_start(xnat[:, 1:NT, :], x_sample[0].rearrange("(t p) d -> p t d", p=P)).then_inc(s_x, 16)
            with sp.Fori(0, DEPTH) as l:
                hold(sp, s_out, l * OC + START)
                hold(sp, s_qm, l * PH + START)
                for i in range(2):
                    hold(sp, s_wst[i], l * (WST[i] * 16) + START)
                with sp.Fori(0, MOD_B) as b:
                    for s in range(SLOTS):
                        hold(sp, s_mod, l * (MOD_B * SLOTS) + b * SLOTS + START)
                        sp.dma_start(slot[s][:, :, :], wcols_at(w_mod, l, b * (SLOTS * WCOLS) + s * WCOLS)).then_inc(s_slot[s], 16)
                hold(sp, s_mod, l * (MOD_B * SLOTS) + MOD_B * SLOTS + START)
                with sp.Fori(0, HEADS) as h:
                    it = l * HEADS + h
                    hold(sp, s_qk, it + START)
                    sp.dma_start(slot[0][:, :, 0:P], w_in[l][:, bass.ds(h * P + Q0, P)].rearrange("(c p) n -> p c n", p=P)).then_inc(s_slot[0], 16)
                    sp.dma_start(slot[0][:, :, P:2 * P], w_in[l][:, bass.ds(h * P + K0, P)].rearrange("(c p) n -> p c n", p=P)).then_inc(s_slot[0], 16)
                    hold(sp, s_vm, it + START)
                    sp.dma_start(slot[1][:, :, :], wcols_at(w_in, l, h * DV + V0)).then_inc(s_slot[1], 16)
                    hold(sp, s_rm, it + START)
                    sp.dma_start(slot[2][:, :, :], wcols_at(w_in, l, h * DV + R0)).then_inc(s_slot[2], 16)
                sp.dma_start(slot[3][:, :, :], wcols(w_in, l, U0)).then_inc(s_slot[3], 16)
                sp.dma_start(slot[4][:, :, :], wcols(w_in, l, U0 + WCOLS)).then_inc(s_slot[4], 16)
                hold(sp, s_o, l * HEADS + HEADS + START)
                hold(sp, s_new, (l * HEADS + HEADS) * 32 + START)
                sp.dma_start(table[:, :], fourier).then_inc(s_table, 16)
                with sp.Fori(0, D // WCOLS) as z:
                    hold(sp, s_zm, l * ZC + z * 2 + START)
                    hold(sp, s_rm, l * HEADS + HEADS + START)
                    hold(sp, s_um, l + 1 + START)
                    sp.dma_start(slot[0][:, :, :], wcols_at(w_in, l, z * WCOLS + ZG0)).then_inc(s_slot[0], 16)
                    sp.dma_start(slot[1][:, :, :], wcols_at(w_in, l, z * WCOLS + ZF0)).then_inc(s_slot[1], 16)
                    hold(sp, s_ym, l * ZC + z * 2 + START)
                    sp.dma_start(slot[2][:, :, :], wcols_at(w_gla_out, l, z * WCOLS)).then_inc(s_slot[2], 16)
                    sp.dma_start(slot[3][:, 0:GROUPS, :], wcols_at(w_four_out, l, z * WCOLS)).then_inc(s_slot[3], 16)
                with sp.Fori(0, 2) as o:
                    hold(sp, s_out, l * OC + o * 4 + START)
                    sp.dma_start(slot[4][:, :, :], wcols_at(w_out, l, o * (2 * WCOLS))).then_inc(s_slot[4], 16)
                    sp.dma_start(slot[5][:, :, :], wcols_at(w_out, l, o * (2 * WCOLS) + WCOLS)).then_inc(s_slot[5], 16)
                hold(sp, s_zm, l * ZC + ZC + START)
                with sp.Fori(0, PH) as h:
                    hold(sp, s_qm, l * PH + h + START)
                    sp.dma_start(slot[0][:, :, :], wcols_at(w_query, l, h * WCOLS)).then_inc(s_slot[0], 16)
                for t in range(NT):
                    hold(sp, s_wc, l * NWG + (t + 1) * (P // 4) + START)
                    sp.dma_start(wd[l][:, :, t * P:(t + 1) * P].rearrange("i j n -> j i n"), wbuf[t % 2][:, :, :]).then_inc(s_wst[t % 2], 16)
                for i in range(2):
                    hold(sp, s_wst[i], (l + 1) * (WST[i] * 16) + START)
                with sp.Fori(0, NKEYS // EG) as n:
                    for g in range(EG):
                        i = n * EG + g
                        hold(sp, s_utm, l * NKEYS + n * EG + START)
                        sp.dma_start(usb[g][:, :], expert_u[l][bass.ds(i * P, P), :]).then_inc(s_u[g], 16)
                        hold(sp, s_coef, l * NKEYS + n * EG + START)
                        sp.dma_start(wex[g][:, :], wd[l][i]).then_inc(s_w[g], 16)
                    for g in range(EG):
                        hold(sp, s_vm2, l * (NKEYS // EG * KC) + n * KC + START)
                        sp.dma_start(vsb[g][:, :], expert_v[l][bass.ds((n * EG + g) * P, P), :]).then_inc(s_v[g], 16)
            hold(sp, s_yc, NT * 2 + START)
            sp.dma_start(y_prompt[0], ynat[:, 0, :]).then_inc(s_y, 16)
            sp.dma_start(y_sample[0].rearrange("(t p) d -> p t d", p=P), ynat[:, 1:NT, :]).then_inc(s_y, 16)
            hold(sp, s_y, 32 + START)

        @block.gpsimd
        def _(pool):
            pool.dma_start(rows0[0:8, :], c[0].rearrange("(r p) -> r p", p=P)).then_inc(s_rows, 16)
            pool.dma_start(rows0[8:16, :], c_ctx.rearrange("(r p) -> r p", p=P)).then_inc(s_rows, 16)
            pool.dma_start(rows0[16:24, :], final_norm.rearrange("(r p) -> r p", p=P)).then_inc(s_rows, 16)
            with pool.Fori(0, DEPTH) as l:
                hold(pool, s_rowsT, l * 1 + 1 + START)
                at = 0
                for w, n in ((b_mod, 48), (norm1, 8), (norm2, 8), (gla_norm, 8), (b_af, 4), (b_ab, 4)):
                    pool.dma_start(rows[at:at + n, :], w[l].rearrange("(r p) -> r p", p=P)).then_inc(s_rows, 16)
                    at += n
                hold(pool, s_x2, l * KC + START)
                hold(pool, s_xt, NT * 2 + START)
                hold(pool, s_set, 1 + START)
                pool.dma_start(wlr[:, :, :], w_in[l][:, L0:L0 + 2 * LOWRANK].rearrange("(c p) n -> p c n", p=P)).then_inc(s_wlr, 16)
                hold(pool, s_zero, l + 1 + START)
                with pool.Fori(0, HEADS) as h:
                    it = l * HEADS + h
                    hold(pool, s_gate, it + START)
                    pool.dma_start(wab[0:LOWRANK, 0, :], w_af[l][:, bass.ds(h * P, P)]).then_inc(s_wab, 16)
                    pool.dma_start(wab[LOWRANK:2 * LOWRANK, 1, :], w_ab[l][:, bass.ds(h * P, P)]).then_inc(s_wab, 16)
                    hold(pool, s_om, it * 3 + START)
                    for d in range(2):
                        pool.dma_start(hist[:, d, 3, :], state_gla[0, l, d, h]).then_inc(s_init, 16)
                hold(pool, s_x1, l * OC + OC + START)
                with pool.Fori(0, PH) as h:
                    hold(pool, s_kt, l * PH + h + START)
                    pool.dma_start(skey[:, :, :], sub_keys[l, h].rearrange("s k d -> k s d")).then_inc(s_skey, 16)

        @block.tensor
        def _(pe):
            def mm(out, lhsT, rhs, first, last):
                return pe.matmul(out, lhsT, rhs, start=first, stop=last)

            def both(big, small, lhsT, rhs, first, last):
                mm(big, lhsT, rhs[:, TP:T], first, last)
                return mm(small, lhsT, rhs[:, 0:TP], first, last)

            def sum_squares(n, l):
                for k in range(KC):
                    pe.wait_ge(s_sq, l * (2 * KC) + n * KC + k + 1 + START)
                    last = both(ps[0][:, :], ps[1][:, 0:TP], ones[:, :], hT[:, k, :], k == 0, k == KC - 1)
                last.then_inc(s_ss, 1)

            pe.wait_ge(s_const, 16 + START)
            pe.wait_ge(s_rows, 48)
            pe.transpose(ps[7][:, 0:24], rows0[:, :], ident[0:24, 0:24]).then_inc(s_rowsT, 1)
            pe.wait_ge(s_x, 32 + START)
            for t in range(NT):
                for j in range(2):
                    if t * 2 + j >= 2:
                        pe.wait_ge(s_xc, t * 2 + j - 1 + START)
                    for q in range(4):
                        k = j * 4 + q
                        last = pe.transpose(ps[j][:, q * P:(q + 1) * P], xnat[:, t, k * P:(k + 1) * P], ident)
                    last.then_inc(s_xt, 1)
            pe.wait_ge(s_xc, NT * 2 + START)
            hold(pe, s_cond, 1 + START)

            with pe.Fori(0, DEPTH) as l:
                pe.wait_ge(s_rows, l * 96 + 48 + 96)
                pe.wait_ge(s_cols, l + 1 + START)
                pe.transpose(ps[7][:, 0:80], rows[:, :], ident[0:80, 0:80]).then_inc(s_rowsT, 1)
                hold(pe, s_acc, l * (NKEYS // EG * KC) + START)
                with pe.Fori(0, MOD_B) as b:
                    for s in range(SLOTS):
                        pe.wait_ge(s_slot[s], 16 * USES_(s, l) + 16 * b + 16 + START)
                        for j in range(2):
                            n = b * (2 * SLOTS) + (2 * s + j)
                            for k in range(KC):
                                last = mm(ps[6][:, bass.ds(n * 2, 2)], slot[s][:, k, j * P:(j + 1) * P], scond[:, k, :],
                                          k == 0, k == KC - 1)
                        last.then_inc(s_mod, 1)
                sum_squares(0, l)
                pe.wait_ge(s_h, l * (2 * KC) + KC + START)
                pe.wait_ge(s_wlr, 16 * l + 16)
                for k in range(KC):
                    mm(ps[2][0:32, :], wlr[:, k, :], hT[:, k, TP:T], k == 0, k == KC - 1)
                    last = mm(ps[3][0:32, 0:TP], wlr[:, k, :], hT[:, k, 0:TP], k == 0, k == KC - 1)
                last.then_inc(s_lr, 1)
                hold(pe, s_lrT, l + 1 + START)

                with pe.Fori(0, HEADS) as h:
                    it = l * HEADS + h
                    pe.wait_ge(s_slot[0], 16 * (USES_(0, l) + HEAD_N) + h * 32 + 32 + START)
                    pe.wait_ge(s_o, it + START)
                    for j in range(2):
                        for k in range(KC):
                            last = both(ps[2 * j][:, :], ps[2 * j + 1][:, 0:TP], slot[0][:, k, j * P:(j + 1) * P],
                                        hT[:, k, :], k == 0, k == KC - 1)
                    last.then_inc(s_qk, 1)
                    pe.wait_ge(s_wab, 32 * it + 32)
                    for d in range(2):
                        last = both(ps[4 + 2 * d][:, :], ps[5 + 2 * d][:, 0:TP], wab[:, d, :], lrT[:, :], True, True)
                    last.then_inc(s_gate, 1)
                    pe.wait_ge(s_q, it + 1 + START)
                    mm(ps[0][:, :], rotT, qk[:, 0, TP:T], True, True)
                    pe.wait_ge(s_k, it + 1 + START)
                    mm(ps[2][:, :], rotT, qk[:, 1, TP:T], True, True).then_inc(s_rot, 1)
                    pe.wait_ge(s_slot[1], 16 * (USES_(1, l) + HEAD_N) + 16 * h + 16 + START)
                    pe.wait_ge(s_gx, it + 1 + START)
                    for t in range(NT):
                        for k in range(KC):
                            last = mm(ps[1 + 2 * (t // 2)][:, (t % 2) * DV:(t % 2 + 1) * DV], hT[:, k, t * P:(t + 1) * P],
                                      slot[1][:, k, :], k == 0, k == KC - 1)
                    last.then_inc(s_vm, 1)
                    pe.wait_ge(s_slot[2], 16 * (USES_(2, l) + HEAD_N) + 16 * h + 16 + START)
                    for j in range(2):
                        for k in range(KC):
                            last = both(ps[4 + 2 * j][:, :], ps[7][:, j * P:(j + 1) * P], slot[2][:, k, j * P:(j + 1) * P],
                                        hT[:, k, :], k == 0, k == KC - 1)
                    last.then_inc(s_rm, 1)
                    pe.wait_ge(s_scal, it + 1 + START)
                    pe.wait_ge(s_vc, it + 1 + START)
                    for d in range(2):
                        for t in range(NT):
                            dst = ps[1][:, d * P:(d + 1) * P] if t == 0 else ps[2 * d][:, (t - 1) * P:t * P]
                            last = pe.transpose(dst, dx[:, d, t * P:(t + 1) * P], ident)
                    last.then_inc(s_kdm, 1)
                    pe.wait_ge(s_r, it + 1 + START)
                    for d in range(2):
                        for t in range(NT):
                            dst = ps[5][:, d * P:(d + 1) * P] if t == 0 else ps[4 + 2 * d][:, (t - 1) * P:t * P]
                            tt = slice(t * P, (t + 1) * P)
                            last = mm(dst, e2[:, d, tt], bx[:, d, tt], True, True)
                    last.then_inc(s_am, 1)
                    pe.wait_ge(s_kd, it + 1 + START)
                    for i in range(9):
                        if i >= 2:
                            pe.wait_ge(s_st, it * 9 + i - 1 + START)
                        for d in range(2):
                            ch = step_chunk(i, d)
                            q = slice((ch % 2) * CHUNK, (ch % 2 + 1) * CHUNK)
                            last = mm(ps[STEP_BANKS[i % 2][d]][:, 0:DV], kdT[q, d, ch // 2, :], v_sb[q, ch // 2, :], True, True)
                        last.then_inc(s_ds, 1)
                    pe.wait_ge(s_a, it + 1 + START)
                    pe.wait_ge(s_st, it * 9 + 9 + START)
                    for t in range(NT):
                        bank, at = 4 + t // 2, (t % 2) * DV
                        for d in range(2):
                            pe.matmul(ps[bank][:, at:at + DV], att[:, d, t, :], v_sb[:, t, :], start=(d == 0), stop=False,
                                      skip_group_check=True)
                        for half in range(2):
                            ch = 2 * t + half
                            for d in range(2):
                                last = pe.matmul(ps[bank][half * CHUNK:(half + 1) * CHUNK, at:at + DV],
                                                 bx[:, d, ch * CHUNK:(ch + 1) * CHUNK], hist[:, d, prev_slot(ch, d), :],
                                                 start=False, stop=(d == 1), skip_group_check=True)
                        if t % 2 == 1 or t == NT - 1:
                            last.then_inc(s_om, 1)
                    pe.wait_ge(s_on, it + 1 + START)
                    for j in range(2):
                        for t in range(NT):
                            dst = ps[1][:, j * P:(j + 1) * P] if t == 0 else ps[2 * j][:, (t - 1) * P:t * P]
                            last = pe.transpose(dst, on[:, t, j * P:(j + 1) * P], ident)
                    last.then_inc(s_ont, 1)

                pe.wait_ge(s_o, l * HEADS + HEADS + START)
                for g in range(GROUPS):
                    s = 3 + g // 2
                    if g % 2 == 0:
                        pe.wait_ge(s_slot[s], 16 * (USES_(s, l) + UN) + 16 + START)
                    for k in range(KC):
                        last = both(ps[2 * g][:, :], ps[2 * g + 1][:, 0:TP], slot[s][:, k, (g % 2) * P:(g % 2 + 1) * P],
                                    hT[:, k, :], k == 0, k == KC - 1)
                last.then_inc(s_um, 1)
                pe.wait_ge(s_uc, l + 1 + START)
                for t in range(NT):
                    for g in range(GROUPS):
                        i = 2 * t + g // 2
                        if g % 2 == 0 and i >= 8:
                            pe.wait_ge(s_f1c, l * (2 * NT) + i - 7 + START)
                        last = mm(ps[i % 8][:, (g % 2) * 256:(g % 2 + 1) * 256], uT[:, g, t * P:(t + 1) * P], cdsd, True, True)
                        if g % 2 == 1:
                            last.then_inc(s_f1, 1)
                pe.wait_ge(s_f1c, l * (2 * NT) + 2 * NT + START)
                pe.wait_ge(s_table, 16 * l + 16 + START)
                for g in range(GROUPS):
                    for t in range(1, NT):
                        for q in range(2):
                            at = ((t - 1) * 2 + q) * TS
                            mm(ps[2 * g][:, :], ab[:, t, g, q, :], table[:, at:at + TS], t == 1 and q == 0, t == NT - 1 and q == 1)
                    for q in range(2):
                        at = 8 * TS + q * TP
                        last = mm(ps[2 * g + 1][:, 0:TP], ab[:, 0, g, q, :], table[:, at:at + TP], q == 0, q == 1)
                last.then_inc(s_f2, 1)
                hold(pe, s_f2c, l + 1 + START)

                with pe.Fori(0, D // WCOLS) as z:
                    for j in range(2):
                        cc = slice(j * P, (j + 1) * P)
                        n = l * ZC + z * 2 + j
                        if j == 0:
                            pe.wait_ge(s_slot[0], 16 * (USES_(0, l) + ZN0) + 16 * z + 16 + START)
                            pe.wait_ge(s_slot[1], 16 * (USES_(1, l) + ZN) + 16 * z + 16 + START)
                        pe.wait_ge(s_mg, n + START)
                        for k in range(KC):
                            both(ps[0][:, :], ps[1][:, 0:TP], slot[0][:, k, cc], hT[:, k, :], k == 0, k == KC - 1)
                        for k in range(KC):
                            last = both(ps[2][:, :], ps[3][:, 0:TP], slot[1][:, k, cc], hT[:, k, :], k == 0, k == KC - 1)
                        last.then_inc(s_zm, 1)
                        if j == 0:
                            pe.wait_ge(s_slot[2], 16 * (USES_(2, l) + ZN) + 16 * z + 16 + START)
                            pe.wait_ge(s_slot[3], 16 * (USES_(3, l) + UN + 1) + 16 * z + 16 + START)
                        for k in range(KC):
                            both(ps[4][:, :], ps[5][:, 0:TP], slot[2][:, k, cc], oT[:, k, :], k == 0, k == KC - 1)
                        for k in range(GROUPS):
                            last = both(ps[6][:, :], ps[7][:, 0:TP], slot[3][:, k, cc], fourT[:, k, :], k == 0, k == GROUPS - 1)
                        last.then_inc(s_ym, 1)
                hold(pe, s_mg, l * ZC + ZC + START)
                with pe.Fori(0, 2) as o:
                    for q in range(4):
                        s = 4 + q // 2
                        if q % 2 == 0:
                            pe.wait_ge(s_slot[s], 16 * (USES_(s, l) + (5 if s == 4 else 4)) + 16 * o + 16 + START)
                        pe.wait_ge(s_x1, l * OC + o * 4 + START)
                        for k in range(KC):
                            last = both(ps[2 * q][:, :], ps[2 * q + 1][:, 0:TP], slot[s][:, k, (q % 2) * P:(q % 2 + 1) * P],
                                        mT[:, k, :], k == 0, k == KC - 1)
                        last.then_inc(s_out, 1)
                pe.wait_ge(s_x1, l * OC + OC + START)
                sum_squares(1, l)

                hold(pe, s_h, l * (2 * KC) + 2 * KC + START)
                with pe.Fori(0, PH) as h:
                    it = l * PH + h
                    pe.wait_ge(s_slot[0], 16 * (USES_(0, l) + QN) + 16 * h + 16 + START)
                    for j in range(2):
                        for k in range(KC):
                            last = both(ps[2 * j][:, :], ps[2 * j + 1][:, 0:TP], slot[0][:, k, j * P:(j + 1) * P],
                                        hT[:, k, :], k == 0, k == KC - 1)
                    last.then_inc(s_qm, 1)
                    pe.wait_ge(s_skey, 16 * it + 16)
                    for j in range(2):
                        last = pe.transpose(ps[7][:, j * P:(j + 1) * P], skey[:, j, :], ident)
                    last.then_inc(s_kt, 1)
                    pe.wait_ge(s_ktc, it + 1 + START)
                    pe.wait_ge(s_qc, it + 1 + START)
                    for t in range(NT):
                        for j in range(2):
                            at = (t % 2) * 256 + j * P
                            last = mm(ps[4 + t // 2][:, at:at + P], qryT[:, j, t * P:(t + 1) * P], skT[:, j, :], True, True)
                    last.then_inc(s_sm, 1)
                    pe.wait_ge(s_sc, it + 1 + START)
                pe.wait_ge(s_sel, l * PH + PH + START)
                for a in range(3):
                    for t in range(NT):
                        dst = ps[3][:, a * P:(a + 1) * P] if t == NT - 1 else ps[a][:, t * P:(t + 1) * P]
                        last = pe.transpose(dst, wsel[:, a, t, :], ident)
                last.then_inc(s_tm, 1)
                hold(pe, s_tc, l + 1 + START)
                with pe.Fori(0, NWG // 2) as g:
                    for b in range(2):
                        n = l * NWG + g * 2 + b
                        pe.wait_ge(s_hot, n + 1 + START)
                        pe.wait_ge(s_wc, l * NWG + g * 2 + START)
                        for q in range(4):
                            last = mm(ps[4 + b][:, q * P:(q + 1) * P], onehot[:, b, q, 1, :], onehot[:, b, q, 0, :], True, True)
                        last.then_inc(s_wm, 1)

                with pe.Fori(0, NKEYS // EG) as n:
                    i0 = l * NKEYS + n * EG

                    def turn(g):
                        pe.wait_ge(s_u[g], 16 * (l * (NKEYS // EG) + n + 1) + START)
                        pe.wait_ge(s_utc, i0 + g + START)
                        for k in range(KC):
                            last = pe.transpose(ps[k // 4][:, (k % 4) * P:(k % 4 + 1) * P], usb[g][:, k * P:(k + 1) * P], ident)
                        last.then_inc(s_utm, 1)

                    turn(0)
                    for g in range(EG):
                        if g + 1 < EG:
                            turn(g + 1)
                        pe.wait_ge(s_utc, i0 + g + 1 + START)
                        b = 2 + 2 * (g % 2)
                        if g < 2:
                            pe.wait_ge(s_acc, (l * (NKEYS // EG) + n) * KC + START)
                        else:
                            pe.wait_ge(s_gel, i0 + g - 1 + START)
                        for k in range(KC):
                            last = both(ps[b][:, :], ps[b + 1][:, 0:TP], uTe[g % 2][:, k, :], hT[:, k, :], k == 0, k == KC - 1)
                        last.then_inc(s_um2, 1)
                    pe.wait_ge(s_gel, i0 + 3 + START)
                    pe.wait_ge(s_coef, i0 + EG + START)
                    for k in range(KC):
                        nn = (l * (NKEYS // EG) + n) * KC + k
                        if k >= 2:
                            pe.wait_ge(s_acc, nn - 1 + START)
                        b = 6 if k % 2 == 0 else 2
                        for g in range(EG):
                            if k == 0:
                                pe.wait_ge(s_v[g], 16 * (l * (NKEYS // EG) + n + 1) + START)
                            last = both(ps[b][:, :], ps[b + 1][:, 0:TP], vsb[g][:, k * P:(k + 1) * P], coef[g], g == 0, g == EG - 1)
                        last.then_inc(s_vm2, 1)
                pe.wait_ge(s_x2, l * KC + KC + START)
            for k in range(KC):
                pe.wait_ge(s_sq, DEPTH * 2 * KC + k + 1 + START)
                last = both(ps[0][:, :], ps[1][:, 0:TP], ones[:, :], hT[:, k, :], k == 0, k == KC - 1)
            last.then_inc(s_ss, 1)
            pe.wait_ge(s_h, (2 * DEPTH + 1) * KC + START)
            for t in range(NT):
                for j in range(2):
                    i = t * 2 + j
                    if i >= 2:
                        pe.wait_ge(s_yc, i - 1 + START)
                    for q in range(4):
                        k = j * 4 + q
                        last = pe.transpose(ps[4 + j][:, q * P:(q + 1) * P], hT[:, k, t * P:(t + 1) * P], ident)
                    last.then_inc(s_yt, 1)

        @block.scalar
        def _(act):
            def af(out, in_, fn, **kw):
                return nc.scalar.activation(out, in_, fn, **kw)

            def rstd(before):
                act.wait_ge(s_ss, before + 1 + START)
                af(rs[:, TP:T], ps[0][:, :], ACT.Ln, bias=eps[:, :], scale=1.0 / D)
                af(rs[:, 0:TP], ps[1][:, 0:TP], ACT.Ln, bias=eps[:, :], scale=1.0 / D)
                act.drain()
                af(rs[:, :], rs[:, :], ACT.Exp, scale=-0.5).then_inc(s_rs, 1)

            def squares(before):
                for k in range(KC):
                    af(hT[:, k, :], xT[:, k, :], ACT.Square).then_inc(s_sq, 1)
                rstd(before)

            act.wait_ge(s_set, 1 + START)
            act.wait_ge(s_cols, 1 + START)
            af(scond[:, :, 0], cols0[:, 8:16], ACT.Exp, scale=-1.0)
            af(scond[:, :, 1], cols0[:, 0:8], ACT.Exp, scale=-1.0).then_inc(s_econd, 1)
            hold(act, s_xc, NT * 2 + START)

            with act.Fori(0, DEPTH) as l:
                act.wait_ge(s_x2, l * KC + START)
                act.wait_ge(s_vm2, l * (NKEYS // EG * KC) + START)
                squares(2 * l)
                act.wait_ge(s_lr, l + 1 + START)
                af(lrT[:, TP:T], ps[2][0:32, :], ACT.Copy)
                af(lrT[:, 0:TP], ps[3][0:32, 0:TP], ACT.Copy).then_inc(s_lrT, 1)

                with act.Fori(0, HEADS) as h:
                    it = l * HEADS + h
                    act.wait_ge(s_qk, it + 1 + START)
                    af(qk[:, 0, TP:T], ps[0][:, :], ACT.Copy, scale=float(P) ** -0.5)
                    af(qk[:, 0, 0:TP], ps[1][:, 0:TP], ACT.Copy, scale=float(P) ** -0.5).then_inc(s_q, 1)
                    act.wait_ge(s_gx, it + 1 + START)
                    af(tmp[:, :, :], gx[:, :, :], ACT.Abs)
                    act.drain()
                    af(tmp[:, :, :], tmp[:, :, :], ACT.Exp, scale=-1.0)
                    act.drain()
                    af(tmp[:, :, :], tmp[:, :, :], ACT.Ln, bias=one[:, :]).then_inc(s_gl, 1)
                    act.wait_ge(s_vm, it + 1 + START)
                    af(v_sb[:, 0:2, :], ps[1][:, :], ACT.Copy)
                    af(v_sb[:, 2:4, :], ps[3][:, :], ACT.Copy)
                    af(v_sb[:, 4, :], ps[5][:, 0:DV], ACT.Copy).then_inc(s_vc, 1)
                    act.wait_ge(s_ex, it + 1 + START)
                    af(e2[:, :, :], bx[:, :, :], ACT.Exp, scale=-1.0 / TAU)
                    act.drain()
                    af(bx[:, :, :], bx[:, :, :], ACT.Exp, scale=1.0 / TAU)
                    af(dx[:, :, :], dx[:, :, :], ACT.Exp, scale=1.0 / TAU)
                    af(dec[:, :, :], tot[:, :, :], ACT.Exp, scale=1.0 / TAU).then_inc(s_dec, 1)
                    act.wait_ge(s_rm, it + 1 + START)
                    af(on[:, :, :].rearrange("p t e -> p (t e)")[:, 0:TS], ps[4][:, :], ACT.Exp, scale=-1.0)
                    af(on[:, :, :].rearrange("p t e -> p (t e)")[:, TS:2 * TS], ps[6][:, :], ACT.Exp, scale=-1.0)
                    af(on[:, :, :].rearrange("p t e -> p (t e)")[:, 2 * TS:2 * TS + 2 * TP], ps[7][:, 0:2 * TP], ACT.Exp,
                       scale=-1.0).then_inc(s_re, 1)
                    act.wait_ge(s_kdm, it + 1 + START)
                    af(kdT[:, 0, 1:NT, :], ps[0][:, :], ACT.Copy)
                    af(kdT[:, 1, 1:NT, :], ps[2][:, :], ACT.Copy)
                    af(kdT[:, :, 0, :], ps[1][:, 0:2 * P], ACT.Copy).then_inc(s_kd, 1)
                    hold(act, s_st, it * 9 + 2 + START)
                    for d in range(2):
                        act.dma_start(new_state[0, l, d, h], hist[:, d, 2, :]).then_inc(s_new, 16)
                    for t in range(NT):
                        if t % 2 == 0:
                            act.wait_ge(s_om, it * 3 + t // 2 + 1 + START)
                        af(on[:, t, :], ps[4 + t // 2][:, (t % 2) * DV:(t % 2 + 1) * DV], ACT.Square, accum_out=oss[:, t:t + 1])
                    act.drain()
                    af(ors[:, 0:NT], oss[:, 0:NT], ACT.Ln, bias=eps[:, :], scale=1.0 / DV)
                    act.drain()
                    af(ors[:, 0:NT], ors[:, 0:NT], ACT.Exp, scale=-0.5)
                    act.drain()
                    for t in range(NT):
                        last = af(on[:, t, :], ps[4 + t // 2][:, (t % 2) * DV:(t % 2 + 1) * DV], ACT.Copy, scale=ors[:, t:t + 1])
                    last.then_inc(s_on, 1)

                act.wait_ge(s_um, l + 1 + START)
                for g in range(GROUPS):
                    af(uT[:, g, TP:T], ps[2 * g][:, :], ACT.Copy)
                    last = af(uT[:, g, 0:TP], ps[2 * g + 1][:, 0:TP], ACT.Copy)
                last.then_inc(s_uc, 1)
                for i in range(2 * NT):
                    act.wait_ge(s_f1, l * (2 * NT) + i + 1 + START)
                    af(ab[:, i // 2, 2 * (i % 2):2 * (i % 2) + 2, :, :], ps[i % 8][:, :], ACT.Copy).then_inc(s_f1c, 1)
                act.wait_ge(s_f2, l + 1 + START)
                for g in range(GROUPS):
                    af(fourT[:, g, TP:T], ps[2 * g][:, :], ACT.Copy)
                    last = af(fourT[:, g, 0:TP], ps[2 * g + 1][:, 0:TP], ACT.Copy)
                last.then_inc(s_f2c, 1)
                with act.Fori(0, ZC) as z:
                    n = l * ZC + z
                    act.wait_ge(s_zm, n + 1 + START)
                    act.wait_ge(s_mg, n + START)
                    for a in range(2):
                        af(sg[:, a, TP:T], ps[2 * a][:, :], ACT.Exp, scale=-1.0)
                        last = af(sg[:, a, 0:TP], ps[2 * a + 1][:, 0:TP], ACT.Exp, scale=-1.0)
                    last.then_inc(s_ze, 1)
                act.wait_ge(s_x1, l * OC + OC + START)
                squares(2 * l + 1)

                with act.Fori(0, PH) as h:
                    it = l * PH + h
                    act.wait_ge(s_qm, it + 1 + START)
                    for j in range(2):
                        af(qryT[:, j, TP:T], ps[2 * j][:, :], ACT.Copy)
                        last = af(qryT[:, j, 0:TP], ps[2 * j + 1][:, 0:TP], ACT.Copy)
                    last.then_inc(s_qc, 1)
                    act.wait_ge(s_kt, it + 1 + START)
                    af(skT[:, :, :], ps[7][:, 0:2 * P], ACT.Copy).then_inc(s_ktc, 1)
                    act.wait_ge(s_sm, it + 1 + START)
                    act.wait_ge(s_sel, it + START)
                    af(sc[:, 0:2, :, :], ps[4][:, :], ACT.Copy)
                    af(sc[:, 2:4, :, :], ps[5][:, :], ACT.Copy)
                    af(sc[:, 4, :, :], ps[6][:, 0:2 * P], ACT.Copy).then_inc(s_sc, 1)
                    act.wait_ge(s_d, it + 1 + START)
                    af(best[:, :, :], best[:, :, :], ACT.Exp).then_inc(s_e, 1)
                act.wait_ge(s_tm, l + 1 + START)
                for a in range(3):
                    af(wselT[:, a, 0:TS], ps[a][:, :], ACT.Copy)
                    last = af(wselT[:, a, TS:T], ps[3][:, a * P:(a + 1) * P], ACT.Copy)
                last.then_inc(s_tc, 1)
                for t in range(NT):
                    if t >= 2:
                        hold(act, s_wst[t % 2], l * (WST[t % 2] * 16) + (t // 2) * 16 + START)
                    with act.Fori(0, P // 8) as g:
                        for b in range(2):
                            act.wait_ge(s_wm, l * NWG + t * (P // 4) + g * 2 + b + 1 + START)
                            af(wbuf[t % 2][:, :, bass.ds(g * 8 + b * 4, 4)].rearrange("p i n -> p n i"),
                               ps[4 + b][:, :].rearrange("p (n i) -> p n i", n=4), ACT.Copy).then_inc(s_wc, 1)

                for i in range(2):
                    hold(act, s_wst[i], (l + 1) * (WST[i] * 16) + START)
                with act.Fori(0, NKEYS // EG) as n:
                    i0 = l * NKEYS + n * EG

                    def copies(g):
                        act.wait_ge(s_utm, i0 + g + 1 + START)
                        if g < 2:
                            act.wait_ge(s_um2, i0 + START)
                        else:
                            act.wait_ge(s_um2, i0 + g - 1 + START)
                        af(uTe[g % 2][:, 0:4, :], ps[0][:, :], ACT.Copy)
                        af(uTe[g % 2][:, 4:8, :], ps[1][:, :], ACT.Copy).then_inc(s_utc, 1)

                    copies(0)
                    for g in range(EG):
                        if g + 1 < EG:
                            copies(g + 1)
                        act.wait_ge(s_um2, i0 + g + 1 + START)
                        if g >= 2:
                            act.wait_ge(s_coef, i0 + g - 1 + START)
                        else:
                            act.wait_ge(s_coef, i0 + START)
                        b = 2 + 2 * (g % 2)
                        af(gel[g % 2][:, TP:T], ps[b][:, :], ACT.Gelu_apprx_tanh)
                        af(gel[g % 2][:, 0:TP], ps[b + 1][:, 0:TP], ACT.Gelu_apprx_tanh).then_inc(s_gel, 1)
            act.wait_ge(s_x2, DEPTH * KC + START)
            act.wait_ge(s_vm2, DEPTH * (NKEYS // EG * KC) + START)
            squares(2 * DEPTH)
            act.wait_ge(s_new, DEPTH * HEADS * 2 * 16 + START)

        @block.vector
        def _(dve):
            v = nc.vector
            tt, ts, stt = v.tensor_tensor, v.tensor_scalar, v.scalar_tensor_tensor

            def norm(before, scale_of, shift_of):
                dve.wait_ge(s_rs, before + 1 + START)
                for k in range(KC):
                    tt(hT[:, k, :], xT[:, k, :], rs[:, :], ALU.mult)
                dve.drain()
                for k in range(KC):
                    for q, cols_ in ((0, slice(0, TP)), (1, slice(TP, T))):
                        a, b = scale_of(k, q), shift_of(k, q)
                        if b is None:
                            last = ts(hT[:, k, cols_], hT[:, k, cols_], a, None, ALU.mult)
                        else:
                            last = ts(hT[:, k, cols_], hT[:, k, cols_], a, b, ALU.mult, ALU.add)
                    last.then_inc(s_h, 1)

            v.memset(ones[:, :], 1.0)
            v.memset(eps[:, :], EPS)
            v.memset(one[:, :], 1.0).then_inc(s_set, 1)
            for i in range(2 * NT):
                dve.wait_ge(s_xt, i + 1 + START)
                t, j = i // 2, i % 2
                v.tensor_copy(xT[:, 4 * j:4 * j + 4, t * P:(t + 1) * P], ps[j][:, :].rearrange("p (a n) -> p a n", a=4)).then_inc(s_xc, 1)
            dve.wait_ge(s_rowsT, 1 + START)
            v.tensor_copy(cols0[:, :], ps[7][:, 0:24]).then_inc(s_cols, 1)
            dve.wait_ge(s_econd, 1 + START)
            ts(scond[:, :, :], scond[:, :, :], 1.0, None, ALU.add)
            dve.drain()
            v.reciprocal(scond[:, :, :], scond[:, :, :])
            dve.drain()
            tt(scond[:, :, 0], scond[:, :, 0], cols0[:, 8:16], ALU.mult)
            tt(scond[:, :, 1], scond[:, :, 1], cols0[:, 0:8], ALU.mult).then_inc(s_cond, 1)

            with dve.Fori(0, DEPTH) as l:
                dve.wait_ge(s_rowsT, l + 2 + START)
                v.tensor_copy(cols[:, :], ps[7][:, 0:80]).then_inc(s_cols, 1)
                v.memset(att[:, :, :, :], 0.0)
                v.memset(hist[:, :, 0, :], 0.0)
                v.memset(wab[:, :, :], 0.0)
                dve.drain()
                v.memset(tot[:, :, :], 0.0).then_inc(s_zero, 1)
                dve.wait_ge(s_mod, l * (MOD_B * SLOTS) + MOD_B * SLOTS + START)
                tt(modT[:, :, :], ps[6][:, 0:96].rearrange("p (n q) -> p n q", q=2),
                   cols[:, 0:48].unsqueeze(2).to_broadcast([P, 48, 2]), ALU.add)
                dve.drain()
                for a in range(2):
                    stt(nscale[:, a, :, :], modT[:, 8 + 24 * a:16 + 24 * a, :], 1.0,
                        cols[:, 48 + 8 * a:56 + 8 * a].unsqueeze(2).to_broadcast([P, KC, 2]), ALU.add, ALU.mult)
                dve.drain()
                norm(2 * l, lambda k, q: nscale[:, 0, k, q:q + 1], lambda k, q: modT[:, k, q:q + 1])

                with dve.Fori(0, HEADS) as h:
                    it = l * HEADS + h
                    dve.wait_ge(s_qk, it + 1 + START)
                    v.tensor_copy(qk[:, 1, TP:T], ps[2][:, :])
                    v.tensor_copy(qk[:, 1, 0:TP], ps[3][:, 0:TP]).then_inc(s_k, 1)
                    dve.wait_ge(s_gate, it + 1 + START)
                    for d in range(2):
                        bias = cols[:, bass.ds(h + (72 + 4 * d), 1)]
                        ts(gx[:, d, TP:T], ps[4 + 2 * d][:, :], bias, None, ALU.add)
                        last = ts(gx[:, d, 0:TP], ps[5 + 2 * d][:, 0:TP], bias, None, ALU.add)
                    last.then_inc(s_gx, 1)
                    dve.wait_ge(s_rot, it + 1 + START)
                    for a in range(2):
                        tt(qk[:, a, TP:T], qk[:, a, TP:T], cos, ALU.mult)
                        tt(e2[:, a, TP:T], ps[2 * a][:, :], sin, ALU.mult)
                    dve.drain()
                    for a in range(2):
                        tt(qk[:, a, TP:T], qk[:, a, TP:T], e2[:, a, TP:T], ALU.add)
                    dve.wait_ge(s_gl, it + 1 + START)
                    stt(gx[:, :, :], gx[:, :, :], 0.0, tmp[:, :, :], ALU.min, ALU.subtract)
                    dve.drain()
                    v.tensor_tensor_scan(bx[:, 0, :], reset, gx[:, 0, :], 0.0, ALU.mult, ALU.add)
                    v.tensor_tensor_scan(tmp[:, 0, :], reset, gx[:, 1, :], 0.0, ALU.mult, ALU.add)
                    dve.drain()
                    chunks = lambda ap: ap.rearrange("p (n c) -> p n c", c=CHUNK)
                    v.tensor_copy(tot[:, 0, :], chunks(bx[:, 0, :])[:, :, CHUNK - 1])
                    v.tensor_copy(tot[:, 1, :], chunks(tmp[:, 0, :])[:, :, CHUNK - 1])
                    dve.drain()
                    spread = lambda d: tot[:, d, :].unsqueeze(2).to_broadcast([P, NCH, CHUNK])
                    tt(chunks(dx[:, 0, :]), spread(0), chunks(bx[:, 0, :]), ALU.subtract)
                    tt(chunks(tmp[:, 1, :]), spread(1), chunks(tmp[:, 0, :]), ALU.subtract)
                    tt(dx[:, 1, :], tmp[:, 0, :], gx[:, 1, :], ALU.subtract)
                    dve.drain()
                    tt(bx[:, 1, :], tmp[:, 1, :], gx[:, 1, :], ALU.add).then_inc(s_ex, 1)
                    rr = on[:, :, :].rearrange("p t e -> p (t e)")
                    dve.wait_ge(s_re, it + 1 + START)
                    ts(rr, rr, 1.0, None, ALU.add)
                    dve.drain()
                    v.reciprocal(rr, rr)
                    dve.drain()
                    tt(rsil[:, 0, TP:T], ps[4][:, :], rr[:, 0:TS], ALU.mult)
                    tt(rsil[:, 1, TP:T], ps[6][:, :], rr[:, TS:2 * TS], ALU.mult)
                    tt(rsil[:, :, 0:TP], ps[7][:, 0:2 * TP].rearrange("p (j n) -> p j n", j=2),
                       rr[:, 2 * TS:2 * TS + 2 * TP].rearrange("p (j n) -> p j n", j=2), ALU.mult).then_inc(s_r, 1)
                    dve.wait_ge(s_dec, it + 1 + START)
                    qb = qk[:, 0, :].unsqueeze(1).to_broadcast([P, 2, T])
                    kb = qk[:, 1, :].unsqueeze(1).to_broadcast([P, 2, T])
                    tt(dx[:, :, :], dx[:, :, :], kb, ALU.mult)
                    tt(e2[:, :, :], e2[:, :, :], kb, ALU.mult)
                    tt(bx[:, :, :], bx[:, :, :], qb, ALU.mult).then_inc(s_scal, 1)
                    hold(dve, s_am, it + 1 + START)
                    for d in range(2):
                        v.copy_predicated(att[:, d, 1:NT, :], mask[d].unsqueeze(1).to_broadcast([P, 4, P]),
                                          ps[4 + 2 * d][:, :].rearrange("p (t n) -> p t n", n=P))
                    for d in range(2):
                        last = v.copy_predicated(att[:, d, 0, :], mask[d], ps[5][:, d * P:(d + 1) * P])
                    last.then_inc(s_a, 1)
                    dve.wait_ge(s_init, 32 * it + 32)
                    dve.wait_ge(s_new, 32 * it + START)
                    for i in range(9):
                        dve.wait_ge(s_ds, it * 9 + i + 1 + START)
                        src = i if i < 2 else i + 1
                        for d in range(2):
                            ch = step_chunk(i, d)
                            last = stt(hist[:, d, src + 1, :], hist[:, d, src, :], dec[:, d, ch:ch + 1],
                                       ps[STEP_BANKS[i % 2][d]][:, 0:DV], ALU.mult, ALU.add)
                        last.then_inc(s_st, 1)
                        dve.drain()
                    dve.wait_ge(s_ont, it + 1 + START)
                    for j in range(2):
                        gn = cols[:, bass.ds(h * 2 + (64 + j), 1)]
                        dst = oT[:, bass.ds(h * 2 + j, 1), :].rearrange("p a n -> p (a n)")
                        stt(dst[:, TP:T], ps[2 * j][:, :], gn, rsil[:, j, TP:T], ALU.mult, ALU.mult)
                        last = stt(dst[:, 0:TP], ps[1][:, j * P:(j + 1) * P], gn, rsil[:, j, 0:TP], ALU.mult, ALU.mult)
                    last.then_inc(s_o, 1)

                with dve.Fori(0, ZC) as z:
                    n = l * ZC + z
                    dve.wait_ge(s_ze, n + 1 + START)
                    ts(sg[:, :, :], sg[:, :, :], 1.0, None, ALU.add)
                    dve.drain()
                    v.reciprocal(sg[:, :, :], sg[:, :, :])
                    dve.drain()
                    dve.wait_ge(s_ym, n + 1 + START)
                    for a in range(2):
                        tt(sg[:, a, TP:T], sg[:, a, TP:T], ps[4 + 2 * a][:, :], ALU.mult)
                        tt(sg[:, a, 0:TP], sg[:, a, 0:TP], ps[5 + 2 * a][:, 0:TP], ALU.mult)
                    dve.drain()
                    tt(mT[:, bass.ds(z, 1), :].rearrange("p a n -> p (a n)"), sg[:, 0, :], sg[:, 1, :], ALU.add).then_inc(s_mg, 1)
                with dve.Fori(0, 2) as o:
                    for q in range(4):
                        dve.wait_ge(s_out, l * OC + o * 4 + q + 1 + START)
                        xs = xT[:, bass.ds(o * 4 + q, 1), :].rearrange("p a n -> p (a n)")
                        for a, cc, bank in ((1, slice(TP, T), ps[2 * q][:, :]), (0, slice(0, TP), ps[2 * q + 1][:, 0:TP])):
                            g1 = modT[:, bass.ds(o * 4 + (16 + q), 1), a]
                            last = stt(xs[:, cc], bank, g1, xs[:, cc], ALU.mult, ALU.add)
                        last.then_inc(s_x1, 1)
                norm(2 * l + 1, lambda k, q: nscale[:, 1, k, q:q + 1], lambda k, q: modT[:, 24 + k, q:q + 1])

                with dve.Fori(0, PH) as h:
                    it = l * PH + h
                    hold(dve, s_sc, it + 1 + START)
                    lists = [(t, s) for t in range(NT) for s in range(2)]
                    for rank in range(2):
                        r8 = slice(8 * rank, 8 * rank + 8)
                        for t, s in lists:
                            v.max(top[:, t, s, r8], sc[:, t, s, :])
                        dve.drain()
                        for t, s in lists:
                            v.max_index(ti[:, t, s, r8], top[:, t, s, r8], sc[:, t, s, :])
                        dve.drain()
                        if rank == 0:
                            for t, s in lists:
                                v.match_replace(sc[:, t, s, :], top[:, t, s, r8], sc[:, t, s, :], LOWEST)
                            dve.drain()
                    v.tensor_copy(tif[:, :, :, :], ti[:, :, :, :])
                    tt(cand[:, :, :, :], top[:, :, 0, :].unsqueeze(3).to_broadcast([P, NT, TOPK, TOPK]),
                       top[:, :, 1, :].unsqueeze(2).to_broadcast([P, NT, TOPK, TOPK]), ALU.add)
                    dve.drain()
                    flat = lambda t: cand[:, t, :, :].rearrange("p a b -> p (a b)")
                    for rank in range(2):
                        r8 = slice(8 * rank, 8 * rank + 8)
                        for t in range(NT):
                            v.max(best[:, t, r8], flat(t))
                        dve.drain()
                        for t in range(NT):
                            v.max_index(sel[:, t, r8], best[:, t, r8], flat(t))
                        dve.drain()
                        if rank == 0:
                            for t in range(NT):
                                v.match_replace(flat(t), best[:, t, r8], flat(t), LOWEST)
                            dve.drain()
                    v.tensor_copy(bsum[:, :], best[:, :, 0])
                    ts(selab[:, 0, :, :], sel[:, :, :], 4, None, ALU.logical_shift_right)
                    ts(selab[:, 1, :, :], sel[:, :, :], TOPK - 1, None, ALU.bitwise_and)
                    dve.drain()
                    tt(best[:, :, :], best[:, :, :], bsum[:, :].unsqueeze(2).to_broadcast([P, NT, TOPK]), ALU.subtract).then_inc(s_d, 1)
                    v.tensor_copy(self_[:, :, :, :], selab[:, :, :, :])
                    dve.drain()
                    for s in range(2):
                        tt(hot[:, s, :, :, :].rearrange("p t k a -> p (t k) a"),
                           self_[:, s, :, :].rearrange("p t k -> p (t k)").unsqueeze(2).to_broadcast([P, NT * TOPK, TOPK]),
                           iota[:, 0:TOPK].unsqueeze(1).to_broadcast([P, NT * TOPK, TOPK]), ALU.is_equal)
                    dve.drain()
                    for s in range(2):
                        tt(hot[:, s, :, :, :], hot[:, s, :, :, :],
                           tif[:, :, s, :].unsqueeze(2).to_broadcast([P, NT, TOPK, TOPK]), ALU.mult)
                    dve.drain()
                    for s in range(2):
                        v.tensor_reduce(wsel[:, 1 + s, :, bass.ds(h * TOPK, TOPK)], hot[:, s, :, :, :], AX_X, ALU.add)
                    dve.wait_ge(s_e, it + 1 + START)
                    v.tensor_reduce(bsum[:, :], best[:, :, :], AX_X, ALU.add)
                    dve.drain()
                    v.reciprocal(bsum[:, :], bsum[:, :])
                    dve.drain()
                    tt(wsel[:, 0, :, bass.ds(h * TOPK, TOPK)], best[:, :, :],
                       bsum[:, :].unsqueeze(2).to_broadcast([P, NT, TOPK]), ALU.mult).then_inc(s_sel, 1)
                hold(dve, s_tc, l + 1 + START)
                with dve.Fori(0, NWG // 2) as g:
                    for b in range(2):
                        dve.wait_ge(s_wm, l * NWG + g * 2 + START)
                        for q in range(4):
                            n = g * 8 + (b * 4 + q)
                            ts(onehot[:, b, q, 0, :], iota, wselT[:, 1, bass.ds(n, 1)], wselT[:, 0, bass.ds(n, 1)],
                               ALU.is_equal, ALU.mult)
                            last = ts(onehot[:, b, q, 1, :], iota, wselT[:, 2, bass.ds(n, 1)], None, ALU.is_equal)
                        last.then_inc(s_hot, 1)
                for i in range(2):
                    hold(dve, s_wst[i], (l + 1) * (WST[i] * 16) + START)
                v.memset(accT[:, :, :], 0.0)
                dve.drain()
                with dve.Fori(0, NKEYS // EG) as n:
                    i0 = l * NKEYS + n * EG
                    for g in range(EG):
                        dve.wait_ge(s_w[g], 16 * (l * (NKEYS // EG) + n + 1) + START)
                        dve.wait_ge(s_gel, i0 + g + 1 + START)
                        if g == 0:
                            dve.wait_ge(s_vm2, (l * (NKEYS // EG) + n) * KC + START)
                        tt(coef[g][:, :], gel[g % 2][:, :], wex[g][:, :], ALU.mult).then_inc(s_coef, 1)
                    for k in range(KC):
                        dve.wait_ge(s_vm2, (l * (NKEYS // EG) + n) * KC + k + 1 + START)
                        b = 6 if k % 2 == 0 else 2
                        tt(accT[:, k, TP:T], accT[:, k, TP:T], ps[b][:, :], ALU.add)
                        tt(accT[:, k, 0:TP], accT[:, k, 0:TP], ps[b + 1][:, 0:TP], ALU.add).then_inc(s_acc, 1)
                dve.drain()
                for k in range(KC):
                    stt(xT[:, k, 0:TP], accT[:, k, 0:TP], modT[:, 40 + k, 0:1], xT[:, k, 0:TP], ALU.mult, ALU.add)
                    stt(xT[:, k, TP:T], accT[:, k, TP:T], modT[:, 40 + k, 1:2], xT[:, k, TP:T], ALU.mult, ALU.add).then_inc(s_x2, 1)
            norm(2 * DEPTH, lambda k, q: cols0[:, 16 + k:17 + k], lambda k, q: None)
            for i in range(2 * NT):
                dve.wait_ge(s_yt, i + 1 + START)
                t, j = i // 2, i % 2
                v.tensor_copy(ynat[:, t, j * 512:(j + 1) * 512], ps[4 + j][:, :]).then_inc(s_yc, 1)


WST = [3, 2]


def USES_(s, l):
    return l * USES[s]


STEP_BANKS = [(3, 7), (1, 2)]


def step_chunk(i, d):
    if i < 2:
        return i if d == 0 else 1 - i
    return i if d == 0 else 11 - i


def prev_slot(ch, d):
    if ch < 2:
        return ch if d == 0 else 1 - ch
    return ch + 1 if d == 0 else 12 - ch


_INS = ["x_prompt", "x_sample", "state_gla", "c", "c_ctx", "w_mod", "b_mod", "norm1", "w_in", "w_af", "b_af", "w_ab",
        "b_ab", "gla_norm", "w_gla_out", "w_four_out", "w_out", "norm2", "w_query", "sub_keys", "expert_u",
        "expert_v", "final_norm"]
_OUTS = [(1, TP, D), (1, TS, D), (1, DEPTH, 2, HEADS, P, DV)]


def kernel(**inputs):
    import concourse.bacc as _bacc
    from concourse.bass_utils import run_bass_kernel_spmd as _run

    nc = _bacc.Bacc("TRN2", target_bir_lowering=False, num_devices=1)
    arrays, args = {}, []
    for name in _INS:
        a = np.ascontiguousarray(inputs[name])
        arrays[f"in_{name}"] = a
        args.append(nc.dram_tensor(f"in_{name}", a.shape, mybir.dt.from_np(a.dtype), kind="ExternalInput").ap())
    for name, a in zip(("consts", "fourier"), constants()):
        arrays[f"table_{name}"] = a
        args.append(nc.dram_tensor(f"table_{name}", a.shape, F32, kind="ExternalInput").ap())
    for i, shape in enumerate(_OUTS):
        args.append(nc.dram_tensor(f"out_{i}", shape, F32, kind="ExternalOutput").ap())
    build(nc, *args)
    r = _run(nc, [arrays], core_ids=[0])
    return tuple(r.results[0][f"out_{i}"] for i in range(len(_OUTS)))
```

```python
from contextlib import ExitStack

import concourse.bass as bass
import numpy as np
from concourse import mybir

F32 = mybir.dt.float32
F32R = mybir.dt.float32r
U32 = mybir.dt.uint32
ALU = mybir.AluOpType
ACT = mybir.ActivationFunctionType
AX_X = mybir.AxisListType.X

P = 128
D = 1024
KC = D // P
DEPTH = 2
TP, TS = 128, 512
T = TP + TS
NT = T // P
GRID_W = 64
HEADS, DV = 4, 256
CHUNK = 64
NCH = T // CHUNK
LOWRANK = 16
TAU = 16.0
GROUPS = 4
QK_W, V_W, F_W = 512, 1024, 512
PH = 8
NKEYS = 128
TOPK = 16
EG = 4
NG = NKEYS // EG
EPS = 1e-6
ROPE_THETA = 10000.0
LOWEST = -3.0e38

Q0, K0, V0 = 0, QK_W, 2 * QK_W
R0 = V0 + V_W
L0 = R0 + V_W
U0 = L0 + 2 * LOWRANK
ZG0 = U0 + F_W
ZF0 = ZG0 + D

C_ID, C_ROT, C_IOTA, C_COS, C_SIN = 0, 128, 256, 384, 896
C_MF, C_MB, C_RESET, C_CDSD = 1408, 1536, 1664, 2304
C_W = 2560

START = 4
SLOTS = 6
WCOLS = 256
USES = [24, 12, 12, 9, 7, 6]
MOD_B = 6 * D // (SLOTS * WCOLS)
HEAD_N, UN, ZN = 4, 4, 8
ZN0, QN = 12, 16


def constants():
    c = np.zeros((P, C_W), np.float32)
    c[:, C_ID:C_ID + 128] = np.eye(128)
    rot = np.zeros((128, 128))
    for base in (0, 64):
        for i in range(32):
            rot[base + i, base + 32 + i] = -1.0
            rot[base + 32 + i, base + i] = 1.0
    c[:, C_ROT:C_ROT + 128] = rot.T
    c[:, C_IOTA:C_IOTA + 128] = np.arange(128)[None, :]
    freqs = (np.float32(ROPE_THETA) ** (-np.arange(32, dtype=np.float32) / np.float32(32))).astype(np.float32)
    tok = np.arange(TS)
    row, col = tok // GRID_W, tok % GRID_W
    for base, pos in ((0, row), (64, col)):
        ang = (pos.astype(np.float32)[None, :] * freqs[:, None]).astype(np.float32).astype(np.float64)
        for o in (0, 32):
            c[base + o:base + o + 32, C_COS:C_COS + TS] = np.cos(ang)
            c[base + o:base + o + 32, C_SIN:C_SIN + TS] = np.sin(ang)
    s, t = np.arange(128)[:, None], np.arange(128)[None, :]
    same = (s // CHUNK) == (t // CHUNK)
    c[:, C_MF:C_MF + 128] = same & (s <= t)
    c[:, C_MB:C_MB + 128] = same & (s >= t)
    c[:, C_RESET:C_RESET + T] = (np.arange(T) % CHUNK != 0)[None, :]
    a = 2 * np.pi * ((s * t) % 128) / 128
    c[:, C_CDSD:C_CDSD + 128] = np.cos(a) / np.sqrt(128)
    c[:, C_CDSD + 128:C_CDSD + 256] = np.sin(a) / np.sqrt(128)
    k, n = np.arange(TS)[:, None], np.arange(TS)[None, :]
    a5 = 2 * np.pi * ((k * n) % TS) / TS
    lat = np.stack([np.cos(a5), -np.sin(a5)], 1) / np.sqrt(TS)
    lat = lat.reshape(4, P, 2, TS).transpose(1, 0, 2, 3).reshape(P, -1)
    ctx = np.stack([np.cos(a), -np.sin(a)], 1).reshape(P, -1) / np.sqrt(TP)
    return c, np.concatenate([lat, ctx], 1).astype(np.float32)


TT_W = 4 * 2 * TS + 2 * TP


def build(nc, x_prompt, x_sample, state_gla, c, c_ctx, w_mod, b_mod, norm1, w_in, w_af, b_af, w_ab, b_ab,
          gla_norm, w_gla_out, w_four_out, w_out, norm2, w_query, sub_keys, expert_u, expert_v, final_norm,
          consts, fourier, y_prompt, y_sample, new_state):
    wd = nc.dram_tensor("expert_weights", [DEPTH, NKEYS, NKEYS, T], F32, kind="Internal").ap()

    cursor = [nc.sbuf_base + 31 & ~31]

    def place(name, shape, dt=F32, at=None):
        n = int(np.prod(shape[1:])) * 4
        off = cursor[0] if at is None else at[0]
        t = nc.alloc_sbuf_tensor_at(name, shape, dt, offset=off)
        nxt = (off + n + 31) & ~31
        if at is None:
            cursor[0] = nxt
        else:
            at[0] = nxt
        return t

    cst = place("cst", [P, C_W])
    xT = place("xT", [P, KC, T])
    hL = place("hL", [P, KC, T], F32R, at=[cursor[0]])
    hT = place("hT", [P, KC, T])
    ones = place("ones", [P, P])
    eps = place("eps", [P, 1])
    one = place("one", [P, 1])
    rows0 = place("rows0", [24, P])
    cols0 = place("cols0", [P, 24])
    scond = place("scond", [P, KC, 2])
    rows = place("rows", [80, P])
    cols = place("cols", [P, 80])
    modT = place("modT", [P, 48, 2])
    nscale = place("nscale", [P, 2, KC, 2])
    rs = place("rs", [P, T])
    base = cursor[0]

    mr = [base]
    mrow = [place(f"mrow{i}", [2, WCOLS], at=mr) for i in range(SLOTS)]
    m = [base]
    qk = place("qk", [P, 2, T], at=m)
    gx = place("gx", [P, 2, T], at=m)
    bx = place("bx", [P, 2, T], at=m)
    dx = place("dx", [P, 2, T], at=m)
    tmp = place("tmp", [P, 2, T], at=m)
    e2 = place("e2", [P, 2, T], at=m)
    kdT = place("kdT", [P, 2, NT, P], at=m)
    att = place("att", [P, 2, NT, P], at=m)
    hist = place("hist", [P, 2, 11, DV], at=m)
    v_sb = place("v_sb", [P, NT, DV], at=m)
    rsil = place("rsil", [P, 2, T], at=m)
    on = place("on", [P, NT, DV], at=m)
    tot = place("tot", [P, 2, NCH], at=m)
    dec = place("dec", [P, 2, NCH], at=m)
    oss = place("oss", [P, 8], at=m)
    ors = place("ors", [P, 8], at=m)
    wlr = place("wlr", [P, KC, 2 * LOWRANK], at=m)
    lrT = place("lrT", [2 * LOWRANK, T], at=m)
    wab = place("wab", [2 * LOWRANK, 2, P], at=m)
    oT = place("oT", [P, KC, T], at=m)
    ring0 = nc.sbuf_usable_end - SLOTS * KC * WCOLS * 4 & ~31
    assert m[0] <= ring0, (m[0], ring0)
    rg = [ring0]
    slot = [place(f"slot{i}", [P, KC, WCOLS], at=rg) for i in range(SLOTS)]
    f = [base]
    fourT = place("fourT", [P, GROUPS, T], at=f)
    uT = place("uT", [P, GROUPS, T], at=f)
    ab = place("ab", [P, NT, GROUPS, 2, P], at=f)
    table = place("table", [P, TT_W], at=f)
    assert f[0] <= base + 20 * T * 4 + 2 * 11 * DV * 4, f[0] - base
    f2 = [base + GROUPS * T * 4]
    mT = place("mT", [P, KC, T], at=f2)
    sg = place("sg", [P, 2, T], at=f2)
    mt = place("mt", [P, T], at=f2)

    p = [base]
    wselT = place("wselT", [P, 3, T], at=p)
    pq = [p[0]]
    wsel = place("wsel", [P, 3, NT, P], at=pq)
    onehot = place("onehot", [P, 4, 4, 2, P], at=p)
    qryT = place("qryT", [P, 2, T], at=pq)
    skey = place("skey", [P, 2, P], at=pq)
    skT = place("skT", [P, 2, P], at=pq)
    sc = place("sc", [P, NT, 2, P], at=pq)
    top = place("top", [P, NT, 2, TOPK], at=pq)
    ti = place("ti", [P, NT, 2, TOPK], U32, at=pq)
    tif = place("tif", [P, NT, 2, TOPK], at=pq)
    cand = place("cand", [P, NT, TOPK, TOPK], at=pq)
    best = place("best", [P, NT, TOPK], at=pq)
    sel = place("sel", [P, NT, TOPK], U32, at=pq)
    selab = place("selab", [P, 2, NT, TOPK], U32, at=pq)
    self_ = place("self", [P, 2, NT, TOPK], at=pq)
    hot = place("hot", [P, 2, NT, TOPK, TOPK], at=pq)
    bsum = place("bsum", [P, NT], at=pq)
    assert pq[0] <= ring0
    wb = [p[0]]
    wbuf = [place(f"wbuf{i}", [P, NKEYS, P], at=wb) for i in range(2)]
    assert wb[0] <= nc.sbuf_usable_end, (wb[0], nc.sbuf_usable_end)
    e = [base]
    usb = [place(f"usb{i}", [P, D], at=e) for i in range(EG)]
    vraw = [place(f"vraw{i}", [P, D], at=e) for i in range(2)]
    vH = [place(f"vH{i}", [P, D], F32R, at=e) for i in range(EG)]
    vL = [place(f"vL{i}", [P, D], F32R, at=e) for i in range(EG)]
    wex = [place(f"wex{i}", [P, T], at=e) for i in range(2)]
    cH = [place(f"cH{i}", [P, T], F32R, at=e) for i in range(EG)]
    cL = [place(f"cL{i}", [P, T], F32R, at=e) for i in range(EG)]
    uH = [place(f"uH{i}", [P, KC, P], F32R, at=e) for i in range(2)]
    uL = [place(f"uL{i}", [P, KC, P], F32R, at=e) for i in range(2)]
    gel = [place(f"gel{i}", [P, T], at=e) for i in range(2)]
    accT = place("accT", [P, KC, T], at=e)
    hH = place("hH", [P, KC, T], F32R, at=e)
    assert e[0] <= nc.sbuf_usable_end
    xnat = place("xnat", [P, NT, D], at=[base])
    ynat = place("ynat", [P, NT, D], at=[base])

    ident = cst[:, C_ID:C_ID + 128]
    rotT = cst[:, C_ROT:C_ROT + 128]
    iota = cst[:, C_IOTA:C_IOTA + 128]
    cos, sin = cst[:, C_COS:C_COS + TS], cst[:, C_SIN:C_SIN + TS]
    mask = [cst[:, C_MF:C_MF + 128].bitcast(U32), cst[:, C_MB:C_MB + 128].bitcast(U32)]
    reset = cst[:, C_RESET:C_RESET + T]
    cdsd = cst[:, C_CDSD:C_CDSD + 256]

    with ExitStack() as ctx:
        ps = [ctx.enter_context(nc.psum_tensor(f"bank{i}", [P, 512], F32)) for i in range(8)]

        semaphores = []

        def sem(name):
            semaphores.append(ctx.enter_context(nc.semaphore(name)))
            return semaphores[-1]

        def pool_load(name):
            return ctx.enter_context(nc.semaphore(name))

        s_const, s_x, s_rows = sem("const_loaded"), sem("x_loaded"), pool_load("rows_loaded")
        s_slot = [sem(f"slot{i}_loaded") for i in range(SLOTS)]
        s_wlr, s_wab, s_init, s_table = pool_load("wlr_loaded"), pool_load("wab_loaded"), pool_load("states_loaded"), sem("table_loaded")
        s_skey = pool_load("subkeys_loaded")
        s_u = [sem(f"expert_u{i}_loaded") for i in range(EG)]
        s_v = [sem(f"expert_v{i}_loaded") for i in range(2)]
        s_w = [sem(f"expert_w{i}_loaded") for i in range(2)]
        s_new, s_y = sem("new_state_stored"), sem("y_stored")
        s_wst = [sem(f"weights{i}_stored") for i in range(2)]
        s_set = sem("constants_set")
        s_xt, s_xc = sem("x_turned"), sem("x_copied")
        s_rowsT, s_cols = sem("rows_turned"), sem("cols_ready")
        s_econd, s_cond, s_mod, s_modT = sem("cond_exp"), sem("cond_ready"), sem("mod_mm"), sem("mod_ready")
        s_sq, s_ss, s_rs, s_h = sem("squares"), sem("square_sums"), sem("rstd"), sem("h_ready")
        s_lr, s_lrT = sem("lr_mm"), sem("lr_ready")
        s_qk, s_q, s_k = sem("qk_mm"), sem("q_copied"), sem("k_copied")
        s_gate, s_gx, s_gl, s_ex = sem("gate_mm"), sem("gate_x"), sem("gate_log"), sem("exponents")
        s_rot, s_dec = sem("rot_mm"), sem("decays_exp")
        s_vm, s_vc, s_rm, s_re, s_r = sem("v_mm"), sem("v_copied"), sem("r_mm"), sem("r_exp"), sem("r_silu")
        s_scal, s_kdm, s_kd = sem("qk_scaled"), sem("kd_turned"), sem("kd_copied")
        s_am, s_a, s_ds, s_st = sem("att_mm"), sem("att_masked"), sem("dstate_mm"), sem("state_step")
        s_om, s_on, s_ont, s_o = sem("o_mm"), sem("o_normed"), sem("o_turned"), sem("o_gated")
        s_um, s_uc, s_f1, s_f1c, s_f2, s_f2c = (sem("u_mm"), sem("u_copied"), sem("fourier_d"), sem("fourier_d_copied"),
                                               sem("fourier_t"), sem("fourier_ready"))
        s_zm, s_ym, s_ze, s_mg, s_out, s_x1 = (sem("z_mm"), sem("y_mm"), sem("z_exp"), sem("merged"), sem("out_mm"),
                                              sem("x_mixed"))
        s_qm, s_qc, s_kt, s_ktc, s_sm, s_sc = (sem("query_mm"), sem("query_copied"), sem("keys_turned"),
                                              sem("keys_copied"), sem("score_mm"), sem("scores_copied"))
        s_d, s_e, s_sel = sem("best_minus_max"), sem("best_exp"), sem("slots_chosen")
        s_tm, s_tc = sem("slots_turned"), sem("slots_ready")
        s_hot, s_wm, s_wc = sem("onehots"), sem("weights_mm"), sem("weights_copied")
        s_utm, s_utc, s_um2, s_gel, s_coef, s_vm2, s_acc, s_x2 = (
            sem("u_turned"), sem("uT_copied"), sem("expert_a"), sem("gelu_done"), sem("coef_ready"), sem("expert_out"),
            sem("expert_added"), sem("x_done"))
        s_yt, s_yc = sem("y_turned"), sem("y_copied")
        s_zero = sem("zeros_set")
        s_hs, s_ul, s_vh, s_vl = sem("h_split"), sem("uT_split"), sem("v_high"), sem("v_split")
        s_mr, s_mt, s_scf = sem("mod_row_copied"), sem("mod_turned"), sem("scores_used")

        s_passed = sem("waits_passed")

        def hold(eng, semaphore, value):
            eng.wait_ge(semaphore, value)
            eng.sem_inc(s_passed, 1)

        for n, semaphore in enumerate(semaphores):
            (nc.sync, nc.scalar, nc.vector, nc.tensor)[n % 4].sem_inc(semaphore, START)
        nc.all_engine_barrier()

        block = ctx.enter_context(nc.Block())
        NWG = T // 4
        ZC, OC = KC, KC

        def wcols(w, l, c0):
            return w[l][:, c0:c0 + WCOLS].rearrange("(c p) n -> p c n", p=P)

        def wcols_at(w, l, c0):
            return w[l][:, bass.ds(c0, WCOLS)].rearrange("(c p) n -> p c n", p=P)

        @block.sync
        def _(sp):
            sp.dma_start(cst[:, :], consts).then_inc(s_const, 16)
            sp.dma_start(xnat[:, 0, :], x_prompt[0]).then_inc(s_x, 16)
            sp.dma_start(xnat[:, 1:NT, :], x_sample[0].rearrange("(t p) d -> p t d", p=P)).then_inc(s_x, 16)
            with sp.Fori(0, DEPTH) as l:
                hold(sp, s_x2, l * KC + START)
                hold(sp, s_vm2, l * (NG * KC) + START)
                hold(sp, s_out, l * OC + START)
                hold(sp, s_qm, l * PH + START)
                for i in range(2):
                    hold(sp, s_wst[i], l * (WST[i] * 16) + START)
                with sp.Fori(0, MOD_B) as b:
                    for s in range(SLOTS):
                        hold(sp, s_mod, l * (MOD_B * SLOTS) + b * SLOTS + START)
                        sp.dma_start(slot[s][:, :, :], wcols_at(w_mod, l, b * (SLOTS * WCOLS) + s * WCOLS)).then_inc(s_slot[s], 16)
                hold(sp, s_mod, l * (MOD_B * SLOTS) + MOD_B * SLOTS + START)
                with sp.Fori(0, HEADS) as h:
                    it = l * HEADS + h
                    hold(sp, s_qk, it + START)
                    sp.dma_start(slot[0][:, :, 0:P], w_in[l][:, bass.ds(h * P + Q0, P)].rearrange("(c p) n -> p c n", p=P)).then_inc(s_slot[0], 16)
                    sp.dma_start(slot[0][:, :, P:2 * P], w_in[l][:, bass.ds(h * P + K0, P)].rearrange("(c p) n -> p c n", p=P)).then_inc(s_slot[0], 16)
                    hold(sp, s_vm, it + START)
                    sp.dma_start(slot[1][:, :, :], wcols_at(w_in, l, h * DV + V0)).then_inc(s_slot[1], 16)
                    hold(sp, s_rm, it + START)
                    sp.dma_start(slot[2][:, :, :], wcols_at(w_in, l, h * DV + R0)).then_inc(s_slot[2], 16)
                sp.dma_start(slot[3][:, :, :], wcols(w_in, l, U0)).then_inc(s_slot[3], 16)
                sp.dma_start(slot[4][:, :, :], wcols(w_in, l, U0 + WCOLS)).then_inc(s_slot[4], 16)
                hold(sp, s_o, l * HEADS + HEADS + START)
                hold(sp, s_new, (l * HEADS + HEADS) * 32 + START)
                sp.dma_start(table[:, :], fourier).then_inc(s_table, 16)
                with sp.Fori(0, D // WCOLS) as z:
                    hold(sp, s_zm, l * ZC + z * 2 + START)
                    hold(sp, s_rm, l * HEADS + HEADS + START)
                    hold(sp, s_um, l + 1 + START)
                    sp.dma_start(slot[0][:, :, :], wcols_at(w_in, l, z * WCOLS + ZG0)).then_inc(s_slot[0], 16)
                    sp.dma_start(slot[1][:, :, :], wcols_at(w_in, l, z * WCOLS + ZF0)).then_inc(s_slot[1], 16)
                    hold(sp, s_ym, l * ZC + z * 2 + START)
                    sp.dma_start(slot[2][:, :, :], wcols_at(w_gla_out, l, z * WCOLS)).then_inc(s_slot[2], 16)
                    sp.dma_start(slot[3][:, 0:GROUPS, :], wcols_at(w_four_out, l, z * WCOLS)).then_inc(s_slot[3], 16)
                with sp.Fori(0, 2) as o:
                    hold(sp, s_out, l * OC + o * 4 + START)
                    sp.dma_start(slot[4][:, :, :], wcols_at(w_out, l, o * (2 * WCOLS))).then_inc(s_slot[4], 16)
                    sp.dma_start(slot[5][:, :, :], wcols_at(w_out, l, o * (2 * WCOLS) + WCOLS)).then_inc(s_slot[5], 16)
                hold(sp, s_zm, l * ZC + ZC + START)
                with sp.Fori(0, PH) as h:
                    hold(sp, s_qm, l * PH + h + START)
                    sp.dma_start(slot[0][:, :, :], wcols_at(w_query, l, h * WCOLS)).then_inc(s_slot[0], 16)
                for t in range(NT):
                    hold(sp, s_wc, l * NWG + (t + 1) * (P // 4) + START)
                    sp.dma_start(wd[l][:, :, t * P:(t + 1) * P].rearrange("i j n -> j i n"), wbuf[t % 2][:, :, :]).then_inc(s_wst[t % 2], 16)
                for i in range(2):
                    hold(sp, s_wst[i], (l + 1) * (WST[i] * 16) + START)
                def load_u(n, g):
                    hold(sp, s_utm, l * NKEYS + n * EG + (g - EG + 1) + START)
                    sp.dma_start(usb[g][:, :], expert_u[l][bass.ds((n * EG + g) * P, P), :]).then_inc(s_u[g], 16)

                def load_group(n, more):
                    i0 = l * NKEYS + n * EG
                    for g in range(EG):
                        b = g % 2
                        hold(sp, s_coef, i0 + g - 1 + START)
                        sp.dma_start(wex[b][:, :], wd[l][n * EG + g]).then_inc(s_w[b], 16)
                        hold(sp, s_vl, i0 + g - 1 + START)
                        sp.dma_start(vraw[b][:, :], expert_v[l][bass.ds((n * EG + g) * P, P), :]).then_inc(s_v[b], 16)
                        if more:
                            load_u(n + 1, g)

                for g in range(EG):
                    load_u(0, g)
                with sp.Fori(0, NG - 1) as n:
                    load_group(n, True)
                load_group(NG - 1, False)
            hold(sp, s_yc, NT * 2 + START)
            sp.dma_start(y_prompt[0], ynat[:, 0, :]).then_inc(s_y, 16)
            sp.dma_start(y_sample[0].rearrange("(t p) d -> p t d", p=P), ynat[:, 1:NT, :]).then_inc(s_y, 16)
            hold(sp, s_y, 32 + START)

        @block.gpsimd
        def _(pool):
            pool.dma_start(rows0[0:8, :], c[0].rearrange("(r p) -> r p", p=P)).then_inc(s_rows, 16)
            pool.dma_start(rows0[8:16, :], c_ctx.rearrange("(r p) -> r p", p=P)).then_inc(s_rows, 16)
            pool.dma_start(rows0[16:24, :], final_norm.rearrange("(r p) -> r p", p=P)).then_inc(s_rows, 16)
            with pool.Fori(0, DEPTH) as l:
                hold(pool, s_rowsT, l * 1 + 1 + START)
                at = 0
                for w, n in ((b_mod, 48), (norm1, 8), (norm2, 8), (gla_norm, 8), (b_af, 4), (b_ab, 4)):
                    pool.dma_start(rows[at:at + n, :], w[l].rearrange("(r p) -> r p", p=P)).then_inc(s_rows, 16)
                    at += n
                hold(pool, s_x2, l * KC + START)
                hold(pool, s_xt, NT * 2 + START)
                hold(pool, s_set, 1 + START)
                pool.dma_start(wlr[:, :, :], w_in[l][:, L0:L0 + 2 * LOWRANK].rearrange("(c p) n -> p c n", p=P)).then_inc(s_wlr, 16)
                hold(pool, s_zero, l + 1 + START)
                with pool.Fori(0, HEADS) as h:
                    it = l * HEADS + h
                    hold(pool, s_gate, it + START)
                    pool.dma_start(wab[0:LOWRANK, 0, :], w_af[l][:, bass.ds(h * P, P)]).then_inc(s_wab, 16)
                    pool.dma_start(wab[LOWRANK:2 * LOWRANK, 1, :], w_ab[l][:, bass.ds(h * P, P)]).then_inc(s_wab, 16)
                    hold(pool, s_om, it * 3 + START)
                    for d in range(2):
                        pool.dma_start(hist[:, d, 3, :], state_gla[0, l, d, h]).then_inc(s_init, 16)
                hold(pool, s_x1, l * OC + OC + START)
                with pool.Fori(0, PH) as h:
                    hold(pool, s_kt, l * PH + h + START)
                    pool.dma_start(skey[:, :, :], sub_keys[l, h].rearrange("s k d -> k s d")).then_inc(s_skey, 16)

        @block.tensor
        def _(pe):
            def mm(out, lhsT, rhs, first, last):
                return pe.matmul(out, lhsT, rhs, start=first, stop=last)

            def both(big, small, lhsT, rhs, first, last):
                mm(big, lhsT, rhs[:, TP:T], first, last)
                return mm(small, lhsT, rhs[:, 0:TP], first, last)

            def sum_squares(n, l):
                for k in range(KC):
                    pe.wait_ge(s_sq, l * (2 * KC) + n * KC + k + 1 + START)
                    last = both(ps[0][:, :], ps[1][:, 0:TP], ones[:, :], hT[:, k, :], k == 0, k == KC - 1)
                last.then_inc(s_ss, 1)

            pe.wait_ge(s_const, 16 + START)
            pe.wait_ge(s_rows, 48)
            pe.transpose(ps[7][:, 0:24], rows0[:, :], ident[0:24, 0:24]).then_inc(s_rowsT, 1)
            pe.wait_ge(s_x, 32 + START)
            for t in range(NT):
                for j in range(2):
                    if t * 2 + j >= 2:
                        pe.wait_ge(s_xc, t * 2 + j - 1 + START)
                    for q in range(4):
                        k = j * 4 + q
                        last = pe.transpose(ps[j][:, q * P:(q + 1) * P], xnat[:, t, k * P:(k + 1) * P], ident)
                    last.then_inc(s_xt, 1)
            pe.wait_ge(s_xc, NT * 2 + START)
            hold(pe, s_cond, 1 + START)

            with pe.Fori(0, DEPTH) as l:
                pe.wait_ge(s_rows, l * 96 + 48 + 96)
                pe.wait_ge(s_cols, l + 1 + START)
                pe.transpose(ps[7][:, 0:80], rows[:, :], ident[0:80, 0:80]).then_inc(s_rowsT, 1)
                pe.wait_ge(s_acc, l * (NG * KC) + START)
                hold(pe, s_cols, l + 2 + START)
                with pe.Fori(0, MOD_B) as b:
                    r0 = l * (MOD_B * SLOTS) + b * SLOTS

                    def turn_row(s):
                        if s == 0:
                            pe.wait_ge(s_modT, l * MOD_B + b + START)
                        hold(pe, s_mr, r0 + s + 1 + START)
                        for j in range(2):
                            q = 2 * s + j
                            last = pe.transpose(ps[6][:, 2 * q:2 * q + 2], mrow[s][:, j * P:(j + 1) * P], ident[0:2, 0:2])
                        if s == SLOTS - 1:
                            last.then_inc(s_mt, 1)

                    for s in range(SLOTS):
                        pe.wait_ge(s_slot[s], 16 * USES_(s, l) + 16 * b + 16 + START)
                        pe.wait_ge(s_mr, r0 + s - 1 + START)
                        for k in range(KC):
                            last = mm(ps[4 + s % 2][0:2, 0:WCOLS], scond[:, k, :], slot[s][:, k, :], k == 0, k == KC - 1)
                        last.then_inc(s_mod, 1)
                        if s >= 1:
                            turn_row(s - 1)
                    turn_row(SLOTS - 1)
                sum_squares(0, l)
                pe.wait_ge(s_h, l * (2 * KC) + KC + START)
                pe.wait_ge(s_wlr, 16 * l + 16)
                for k in range(KC):
                    mm(ps[2][0:32, :], wlr[:, k, :], hT[:, k, TP:T], k == 0, k == KC - 1)
                    last = mm(ps[3][0:32, 0:TP], wlr[:, k, :], hT[:, k, 0:TP], k == 0, k == KC - 1)
                last.then_inc(s_lr, 1)
                hold(pe, s_lrT, l + 1 + START)

                with pe.Fori(0, HEADS) as h:
                    it = l * HEADS + h
                    pe.wait_ge(s_slot[0], 16 * (USES_(0, l) + HEAD_N) + h * 32 + 32 + START)
                    pe.wait_ge(s_o, it + START)
                    for j in range(2):
                        for k in range(KC):
                            last = both(ps[2 * j][:, :], ps[2 * j + 1][:, 0:TP], slot[0][:, k, j * P:(j + 1) * P],
                                        hT[:, k, :], k == 0, k == KC - 1)
                    last.then_inc(s_qk, 1)
                    pe.wait_ge(s_wab, 32 * it + 32)
                    for d in range(2):
                        last = both(ps[4 + 2 * d][:, :], ps[5 + 2 * d][:, 0:TP], wab[:, d, :], lrT[:, :], True, True)
                    last.then_inc(s_gate, 1)
                    pe.wait_ge(s_q, it + 1 + START)
                    mm(ps[0][:, :], rotT, qk[:, 0, TP:T], True, True)
                    pe.wait_ge(s_k, it + 1 + START)
                    mm(ps[2][:, :], rotT, qk[:, 1, TP:T], True, True).then_inc(s_rot, 1)
                    pe.wait_ge(s_slot[1], 16 * (USES_(1, l) + HEAD_N) + 16 * h + 16 + START)
                    pe.wait_ge(s_gx, it + 1 + START)
                    for t in range(NT):
                        for k in range(KC):
                            last = mm(ps[1 + 2 * (t // 2)][:, (t % 2) * DV:(t % 2 + 1) * DV], hT[:, k, t * P:(t + 1) * P],
                                      slot[1][:, k, :], k == 0, k == KC - 1)
                    last.then_inc(s_vm, 1)
                    pe.wait_ge(s_slot[2], 16 * (USES_(2, l) + HEAD_N) + 16 * h + 16 + START)
                    for j in range(2):
                        for k in range(KC):
                            last = both(ps[4 + 2 * j][:, :], ps[7][:, j * P:(j + 1) * P], slot[2][:, k, j * P:(j + 1) * P],
                                        hT[:, k, :], k == 0, k == KC - 1)
                    last.then_inc(s_rm, 1)
                    pe.wait_ge(s_scal, it + 1 + START)
                    pe.wait_ge(s_vc, it + 1 + START)
                    for d in range(2):
                        for t in range(NT):
                            dst = ps[1][:, d * P:(d + 1) * P] if t == 0 else ps[2 * d][:, (t - 1) * P:t * P]
                            last = pe.transpose(dst, dx[:, d, t * P:(t + 1) * P], ident)
                    last.then_inc(s_kdm, 1)
                    pe.wait_ge(s_r, it + 1 + START)
                    for d in range(2):
                        for t in range(NT):
                            dst = ps[5][:, d * P:(d + 1) * P] if t == 0 else ps[4 + 2 * d][:, (t - 1) * P:t * P]
                            tt = slice(t * P, (t + 1) * P)
                            last = mm(dst, e2[:, d, tt], bx[:, d, tt], True, True)
                    last.then_inc(s_am, 1)
                    pe.wait_ge(s_kd, it + 1 + START)
                    for i in range(9):
                        if i >= 2:
                            pe.wait_ge(s_st, it * 9 + i - 1 + START)
                        for d in range(2):
                            ch = step_chunk(i, d)
                            q = slice((ch % 2) * CHUNK, (ch % 2 + 1) * CHUNK)
                            last = mm(ps[STEP_BANKS[i % 2][d]][:, 0:DV], kdT[q, d, ch // 2, :], v_sb[q, ch // 2, :], True, True)
                        last.then_inc(s_ds, 1)
                    pe.wait_ge(s_a, it + 1 + START)
                    pe.wait_ge(s_st, it * 9 + 9 + START)
                    for t in range(NT):
                        bank, at = 4 + t // 2, (t % 2) * DV
                        for d in range(2):
                            pe.matmul(ps[bank][:, at:at + DV], att[:, d, t, :], v_sb[:, t, :], start=(d == 0), stop=False,
                                      skip_group_check=True)
                        for half in range(2):
                            ch = 2 * t + half
                            for d in range(2):
                                last = pe.matmul(ps[bank][half * CHUNK:(half + 1) * CHUNK, at:at + DV],
                                                 bx[:, d, ch * CHUNK:(ch + 1) * CHUNK], hist[:, d, prev_slot(ch, d), :],
                                                 start=False, stop=(d == 1), skip_group_check=True)
                        if t % 2 == 1 or t == NT - 1:
                            last.then_inc(s_om, 1)
                    pe.wait_ge(s_on, it + 1 + START)
                    for j in range(2):
                        for t in range(NT):
                            dst = ps[1][:, j * P:(j + 1) * P] if t == 0 else ps[2 * j][:, (t - 1) * P:t * P]
                            last = pe.transpose(dst, on[:, t, j * P:(j + 1) * P], ident)
                    last.then_inc(s_ont, 1)

                pe.wait_ge(s_o, l * HEADS + HEADS + START)
                for g in range(GROUPS):
                    s = 3 + g // 2
                    if g % 2 == 0:
                        pe.wait_ge(s_slot[s], 16 * (USES_(s, l) + UN) + 16 + START)
                    for k in range(KC):
                        last = both(ps[2 * g][:, :], ps[2 * g + 1][:, 0:TP], slot[s][:, k, (g % 2) * P:(g % 2 + 1) * P],
                                    hT[:, k, :], k == 0, k == KC - 1)
                last.then_inc(s_um, 1)
                pe.wait_ge(s_uc, l + 1 + START)
                for t in range(NT):
                    for g in range(GROUPS):
                        i = 2 * t + g // 2
                        if g % 2 == 0 and i >= 8:
                            pe.wait_ge(s_f1c, l * (2 * NT) + i - 7 + START)
                        last = mm(ps[i % 8][:, (g % 2) * 256:(g % 2 + 1) * 256], uT[:, g, t * P:(t + 1) * P], cdsd, True, True)
                        if g % 2 == 1:
                            last.then_inc(s_f1, 1)
                pe.wait_ge(s_f1c, l * (2 * NT) + 2 * NT + START)
                pe.wait_ge(s_table, 16 * l + 16 + START)
                for g in range(GROUPS):
                    for t in range(1, NT):
                        for q in range(2):
                            at = ((t - 1) * 2 + q) * TS
                            mm(ps[2 * g][:, :], ab[:, t, g, q, :], table[:, at:at + TS], t == 1 and q == 0, t == NT - 1 and q == 1)
                    for q in range(2):
                        at = 8 * TS + q * TP
                        last = mm(ps[2 * g + 1][:, 0:TP], ab[:, 0, g, q, :], table[:, at:at + TP], q == 0, q == 1)
                last.then_inc(s_f2, 1)
                hold(pe, s_f2c, l + 1 + START)

                with pe.Fori(0, D // WCOLS) as z:
                    for j in range(2):
                        cc = slice(j * P, (j + 1) * P)
                        n = l * ZC + z * 2 + j
                        if j == 0:
                            pe.wait_ge(s_slot[0], 16 * (USES_(0, l) + ZN0) + 16 * z + 16 + START)
                            pe.wait_ge(s_slot[1], 16 * (USES_(1, l) + ZN) + 16 * z + 16 + START)
                        pe.wait_ge(s_mg, n + START)
                        for k in range(KC):
                            both(ps[0][:, :], ps[1][:, 0:TP], slot[0][:, k, cc], hT[:, k, :], k == 0, k == KC - 1)
                        for k in range(KC):
                            last = both(ps[2][:, :], ps[3][:, 0:TP], slot[1][:, k, cc], hT[:, k, :], k == 0, k == KC - 1)
                        last.then_inc(s_zm, 1)
                        if j == 0:
                            pe.wait_ge(s_slot[2], 16 * (USES_(2, l) + ZN) + 16 * z + 16 + START)
                            pe.wait_ge(s_slot[3], 16 * (USES_(3, l) + UN + 1) + 16 * z + 16 + START)
                        for k in range(KC):
                            both(ps[4][:, :], ps[5][:, 0:TP], slot[2][:, k, cc], oT[:, k, :], k == 0, k == KC - 1)
                        for k in range(GROUPS):
                            last = both(ps[6][:, :], ps[7][:, 0:TP], slot[3][:, k, cc], fourT[:, k, :], k == 0, k == GROUPS - 1)
                        last.then_inc(s_ym, 1)
                hold(pe, s_mg, l * ZC + ZC + START)
                with pe.Fori(0, 2) as o:
                    for q in range(4):
                        s = 4 + q // 2
                        if q % 2 == 0:
                            pe.wait_ge(s_slot[s], 16 * (USES_(s, l) + (5 if s == 4 else 4)) + 16 * o + 16 + START)
                        pe.wait_ge(s_x1, l * OC + o * 4 + START)
                        for k in range(KC):
                            last = both(ps[2 * q][:, :], ps[2 * q + 1][:, 0:TP], slot[s][:, k, (q % 2) * P:(q % 2 + 1) * P],
                                        mT[:, k, :], k == 0, k == KC - 1)
                        last.then_inc(s_out, 1)
                pe.wait_ge(s_x1, l * OC + OC + START)
                sum_squares(1, l)

                hold(pe, s_h, l * (2 * KC) + 2 * KC + START)
                def queries(h, it):
                    pe.wait_ge(s_slot[0], 16 * (USES_(0, l) + QN) + 16 * h + 16 + START)
                    pe.wait_ge(s_qc, it + START)
                    for j in range(2):
                        for k in range(KC):
                            last = both(ps[2 * j][:, :], ps[2 * j + 1][:, 0:TP], slot[0][:, k, j * P:(j + 1) * P],
                                        hT[:, k, :], k == 0, k == KC - 1)
                    last.then_inc(s_qm, 1)
                    pe.wait_ge(s_skey, 16 * it + 16)
                    pe.wait_ge(s_ktc, it + START)
                    for j in range(2):
                        last = pe.transpose(ps[7][:, j * P:(j + 1) * P], skey[:, j, :], ident)
                    last.then_inc(s_kt, 1)

                def scores(it):
                    pe.wait_ge(s_ktc, it + 1 + START)
                    pe.wait_ge(s_qc, it + 1 + START)
                    pe.wait_ge(s_sc, it + START)
                    for t in range(NT):
                        for j in range(2):
                            at = (t % 2) * 256 + j * P
                            last = mm(ps[4 + t // 2][:, at:at + P], qryT[:, j, t * P:(t + 1) * P], skT[:, j, :], True, True)
                    last.then_inc(s_sm, 1)

                queries(0, l * PH)
                with pe.Fori(0, PH - 1) as h:
                    scores(l * PH + h)
                    queries(h + 1, l * PH + h + 1)
                scores(l * PH + PH - 1)
                pe.wait_ge(s_sc, l * PH + PH + START)
                pe.wait_ge(s_sel, l * PH + PH + START)
                for a in range(3):
                    for t in range(NT):
                        dst = ps[3][:, a * P:(a + 1) * P] if t == NT - 1 else ps[a][:, t * P:(t + 1) * P]
                        last = pe.transpose(dst, wsel[:, a, t, :], ident)
                last.then_inc(s_tm, 1)
                hold(pe, s_tc, l + 1 + START)
                with pe.Fori(0, NWG // 4) as g:
                    for b in range(4):
                        n = l * NWG + g * 4 + b
                        pe.wait_ge(s_hot, n + 1 + START)
                        pe.wait_ge(s_wc, n - 3 + START)
                        for q in range(4):
                            last = mm(ps[4 + b][:, q * P:(q + 1) * P], onehot[:, b, q, 1, :], onehot[:, b, q, 0, :], True, True)
                        last.then_inc(s_wm, 1)

                HALF = T // 2
                halves = [slice(0, HALF), slice(HALF, T)]

                def three(bank, high, low, mov_high, mov_low, first, last_one):
                    for q in range(2):
                        mm(ps[bank + q][:, 0:HALF], high, mov_high[:, halves[q]], first, False)
                    for q in range(2):
                        mm(ps[bank + q][:, 0:HALF], high, mov_low[:, halves[q]], False, False)
                    for q in range(2):
                        ins = mm(ps[bank + q][:, 0:HALF], low, mov_high[:, halves[q]], False, last_one)
                    return ins

                def turn(n, g):
                    i = l * NKEYS + n * EG + g
                    pe.wait_ge(s_u[g], 16 * (l * NG + n + 1) + START)
                    pe.wait_ge(s_ul, i + START)
                    for k in range(KC):
                        last = pe.transpose(ps[k // 4][:, (k % 4) * P:(k % 4 + 1) * P], usb[g][:, k * P:(k + 1) * P], ident)
                    last.then_inc(s_utm, 1)

                def group(n, more):
                    i0 = l * NKEYS + n * EG
                    k0 = (l * NG + n) * KC
                    for g in range(EG):
                        if g + 1 < EG:
                            turn(n, g + 1)
                        pe.wait_ge(s_ul, i0 + g + 1 + START)
                        if g == 0:
                            pe.wait_ge(s_acc, k0 + START)
                        else:
                            pe.wait_ge(s_gel, i0 + g - 1 + START)
                        for k in range(KC):
                            last = three(2 + 2 * (g % 2), uH[g % 2][:, k, :], uL[g % 2][:, k, :], hH[:, k, :], hL[:, k, :],
                                         k == 0, k == KC - 1)
                        last.then_inc(s_um2, 1)
                    def out_part(k, g):
                        kk = slice(k * P, (k + 1) * P)
                        return three(6 if k % 2 == 0 else 2, vH[g][:, kk], vL[g][:, kk], cH[g][:, :], cL[g][:, :],
                                     g == 0, g == EG - 1)

                    for k in range(2):
                        if k == 1:
                            pe.wait_ge(s_gel, i0 + EG - 1 + START)
                        for g in range(EG - 1):
                            if k == 0:
                                pe.wait_ge(s_vl, i0 + g + 1 + START)
                                pe.wait_ge(s_coef, i0 + g + 1 + START)
                            out_part(k, g)
                    if more:
                        turn(n + 1, 0)
                    pe.wait_ge(s_vl, i0 + EG + START)
                    pe.wait_ge(s_coef, i0 + EG + START)
                    for k in range(2):
                        out_part(k, EG - 1).then_inc(s_vm2, 1)
                    for k in range(2, KC):
                        pe.wait_ge(s_acc, k0 + k - 1 + START)
                        for g in range(EG):
                            last = out_part(k, g)
                        last.then_inc(s_vm2, 1)

                pe.wait_ge(s_hs, l + 1 + START)
                turn(0, 0)
                with pe.Fori(0, NG - 1) as n:
                    group(n, True)
                group(NG - 1, False)
                pe.wait_ge(s_x2, l * KC + KC + START)
            for k in range(KC):
                pe.wait_ge(s_sq, DEPTH * 2 * KC + k + 1 + START)
                last = both(ps[0][:, :], ps[1][:, 0:TP], ones[:, :], hT[:, k, :], k == 0, k == KC - 1)
            last.then_inc(s_ss, 1)
            pe.wait_ge(s_h, (2 * DEPTH + 1) * KC + START)
            for t in range(NT):
                for j in range(2):
                    i = t * 2 + j
                    if i >= 2:
                        pe.wait_ge(s_yc, i - 1 + START)
                    for q in range(4):
                        k = j * 4 + q
                        last = pe.transpose(ps[4 + j][:, q * P:(q + 1) * P], hT[:, k, t * P:(t + 1) * P], ident)
                    last.then_inc(s_yt, 1)

        @block.scalar
        def _(act):
            def af(out, in_, fn, **kw):
                return nc.scalar.activation(out, in_, fn, **kw)

            def rstd(before):
                act.wait_ge(s_ss, before + 1 + START)
                af(rs[:, TP:T], ps[0][:, :], ACT.Ln, bias=eps[:, :], scale=1.0 / D)
                af(rs[:, 0:TP], ps[1][:, 0:TP], ACT.Ln, bias=eps[:, :], scale=1.0 / D)
                act.drain()
                af(rs[:, :], rs[:, :], ACT.Exp, scale=-0.5).then_inc(s_rs, 1)

            def squares(before):
                for k in range(KC):
                    af(hT[:, k, :], xT[:, k, :], ACT.Square).then_inc(s_sq, 1)
                rstd(before)

            act.wait_ge(s_set, 1 + START)
            act.wait_ge(s_cols, 1 + START)
            af(scond[:, :, 0], cols0[:, 8:16], ACT.Exp, scale=-1.0)
            af(scond[:, :, 1], cols0[:, 0:8], ACT.Exp, scale=-1.0).then_inc(s_econd, 1)
            hold(act, s_xc, NT * 2 + START)

            with act.Fori(0, DEPTH) as l:
                with act.Fori(0, MOD_B) as b:
                    for s in range(SLOTS):
                        act.wait_ge(s_mod, l * (MOD_B * SLOTS) + b * SLOTS + s + 1 + START)
                        act.wait_ge(s_mt, l * MOD_B + b + START)
                        af(mrow[s][:, :], ps[4 + s % 2][0:2, 0:WCOLS], ACT.Copy).then_inc(s_mr, 1)
                act.wait_ge(s_x2, l * KC + START)
                act.wait_ge(s_vm2, l * (NG * KC) + START)
                squares(2 * l)
                act.wait_ge(s_lr, l + 1 + START)
                af(lrT[:, TP:T], ps[2][0:32, :], ACT.Copy)
                af(lrT[:, 0:TP], ps[3][0:32, 0:TP], ACT.Copy).then_inc(s_lrT, 1)

                with act.Fori(0, HEADS) as h:
                    it = l * HEADS + h
                    act.wait_ge(s_qk, it + 1 + START)
                    af(qk[:, 0, TP:T], ps[0][:, :], ACT.Copy, scale=float(P) ** -0.5)
                    af(qk[:, 0, 0:TP], ps[1][:, 0:TP], ACT.Copy, scale=float(P) ** -0.5).then_inc(s_q, 1)
                    act.wait_ge(s_gx, it + 1 + START)
                    af(tmp[:, :, :], gx[:, :, :], ACT.Abs)
                    act.drain()
                    af(tmp[:, :, :], tmp[:, :, :], ACT.Exp, scale=-1.0)
                    act.drain()
                    af(tmp[:, :, :], tmp[:, :, :], ACT.Ln, bias=one[:, :]).then_inc(s_gl, 1)
                    act.wait_ge(s_vm, it + 1 + START)
                    af(v_sb[:, 0:2, :], ps[1][:, :], ACT.Copy)
                    af(v_sb[:, 2:4, :], ps[3][:, :], ACT.Copy)
                    af(v_sb[:, 4, :], ps[5][:, 0:DV], ACT.Copy).then_inc(s_vc, 1)
                    act.wait_ge(s_ex, it + 1 + START)
                    af(e2[:, :, :], bx[:, :, :], ACT.Exp, scale=-1.0 / TAU)
                    act.drain()
                    af(bx[:, :, :], bx[:, :, :], ACT.Exp, scale=1.0 / TAU)
                    af(dx[:, :, :], dx[:, :, :], ACT.Exp, scale=1.0 / TAU)
                    af(dec[:, :, :], tot[:, :, :], ACT.Exp, scale=1.0 / TAU).then_inc(s_dec, 1)
                    act.wait_ge(s_rm, it + 1 + START)
                    af(on[:, :, :].rearrange("p t e -> p (t e)")[:, 0:TS], ps[4][:, :], ACT.Exp, scale=-1.0)
                    af(on[:, :, :].rearrange("p t e -> p (t e)")[:, TS:2 * TS], ps[6][:, :], ACT.Exp, scale=-1.0)
                    af(on[:, :, :].rearrange("p t e -> p (t e)")[:, 2 * TS:2 * TS + 2 * TP], ps[7][:, 0:2 * TP], ACT.Exp,
                       scale=-1.0).then_inc(s_re, 1)
                    act.wait_ge(s_kdm, it + 1 + START)
                    af(kdT[:, 0, 1:NT, :], ps[0][:, :], ACT.Copy)
                    af(kdT[:, 1, 1:NT, :], ps[2][:, :], ACT.Copy)
                    af(kdT[:, :, 0, :], ps[1][:, 0:2 * P], ACT.Copy).then_inc(s_kd, 1)
                    hold(act, s_st, it * 9 + 2 + START)
                    for d in range(2):
                        act.dma_start(new_state[0, l, d, h], hist[:, d, 2, :]).then_inc(s_new, 16)
                    for t in range(NT):
                        if t % 2 == 0:
                            act.wait_ge(s_om, it * 3 + t // 2 + 1 + START)
                        af(on[:, t, :], ps[4 + t // 2][:, (t % 2) * DV:(t % 2 + 1) * DV], ACT.Square, accum_out=oss[:, t:t + 1])
                    act.drain()
                    af(ors[:, 0:NT], oss[:, 0:NT], ACT.Ln, bias=eps[:, :], scale=1.0 / DV)
                    act.drain()
                    af(ors[:, 0:NT], ors[:, 0:NT], ACT.Exp, scale=-0.5)
                    act.drain()
                    for t in range(NT):
                        last = af(on[:, t, :], ps[4 + t // 2][:, (t % 2) * DV:(t % 2 + 1) * DV], ACT.Copy, scale=ors[:, t:t + 1])
                    last.then_inc(s_on, 1)

                act.wait_ge(s_um, l + 1 + START)
                for g in range(GROUPS):
                    af(uT[:, g, TP:T], ps[2 * g][:, :], ACT.Copy)
                    last = af(uT[:, g, 0:TP], ps[2 * g + 1][:, 0:TP], ACT.Copy)
                last.then_inc(s_uc, 1)
                for i in range(2 * NT):
                    act.wait_ge(s_f1, l * (2 * NT) + i + 1 + START)
                    af(ab[:, i // 2, 2 * (i % 2):2 * (i % 2) + 2, :, :], ps[i % 8][:, :], ACT.Copy).then_inc(s_f1c, 1)
                act.wait_ge(s_f2, l + 1 + START)
                for g in range(GROUPS):
                    af(fourT[:, g, TP:T], ps[2 * g][:, :], ACT.Copy)
                    last = af(fourT[:, g, 0:TP], ps[2 * g + 1][:, 0:TP], ACT.Copy)
                last.then_inc(s_f2c, 1)
                with act.Fori(0, ZC) as z:
                    n = l * ZC + z
                    act.wait_ge(s_zm, n + 1 + START)
                    act.wait_ge(s_mg, n + START)
                    for a in range(2):
                        af(sg[:, a, TP:T], ps[2 * a][:, :], ACT.Exp, scale=-1.0)
                        last = af(sg[:, a, 0:TP], ps[2 * a + 1][:, 0:TP], ACT.Exp, scale=-1.0)
                    last.then_inc(s_ze, 1)
                act.wait_ge(s_x1, l * OC + OC + START)
                squares(2 * l + 1)

                def query_copies(it):
                    act.wait_ge(s_qm, it + 1 + START)
                    act.wait_ge(s_sm, it + START)
                    for j in range(2):
                        af(qryT[:, j, TP:T], ps[2 * j][:, :], ACT.Copy)
                        last = af(qryT[:, j, 0:TP], ps[2 * j + 1][:, 0:TP], ACT.Copy)
                    last.then_inc(s_qc, 1)
                    act.wait_ge(s_kt, it + 1 + START)
                    af(skT[:, :, :], ps[7][:, 0:2 * P], ACT.Copy).then_inc(s_ktc, 1)

                def select_head(it, more):
                    act.wait_ge(s_sm, it + 1 + START)
                    act.wait_ge(s_scf, it + START)
                    af(sc[:, 0:2, :, :], ps[4][:, :], ACT.Copy)
                    af(sc[:, 2:4, :, :], ps[5][:, :], ACT.Copy)
                    af(sc[:, 4, :, :], ps[6][:, 0:2 * P], ACT.Copy).then_inc(s_sc, 1)
                    if more:
                        query_copies(it + 1)
                    act.wait_ge(s_d, it + 1 + START)
                    af(best[:, :, :], best[:, :, :], ACT.Exp).then_inc(s_e, 1)

                query_copies(l * PH)
                with act.Fori(0, PH - 1) as h:
                    select_head(l * PH + h, True)
                select_head(l * PH + PH - 1, False)
                act.wait_ge(s_tm, l + 1 + START)
                for a in range(3):
                    af(wselT[:, a, 0:TS], ps[a][:, :], ACT.Copy)
                    last = af(wselT[:, a, TS:T], ps[3][:, a * P:(a + 1) * P], ACT.Copy)
                last.then_inc(s_tc, 1)
                for t in range(NT):
                    if t >= 2:
                        hold(act, s_wst[t % 2], l * (WST[t % 2] * 16) + (t // 2) * 16 + START)
                    with act.Fori(0, P // 16) as g:
                        for b in range(4):
                            act.wait_ge(s_wm, l * NWG + t * (P // 4) + g * 4 + b + 1 + START)
                            af(wbuf[t % 2][:, :, bass.ds(g * 16 + b * 4, 4)].rearrange("p i n -> p n i"),
                               ps[4 + b][:, :].rearrange("p (n i) -> p n i", n=4), ACT.Copy).then_inc(s_wc, 1)

                for i in range(2):
                    hold(act, s_wst[i], (l + 1) * (WST[i] * 16) + START)
                def high_u(i, b):
                    act.wait_ge(s_utm, i + 1 + START)
                    act.wait_ge(s_um2, i - 1 + START)
                    af(uH[b][:, 0:4, :], ps[0][:, :], ACT.Copy)
                    af(uH[b][:, 4:8, :], ps[1][:, :], ACT.Copy).then_inc(s_utc, 1)

                def group(n, more):
                    i0 = l * NKEYS + n * EG
                    for g in range(EG):
                        if g + 1 < EG:
                            high_u(i0 + g + 1, (g + 1) % 2)
                        act.wait_ge(s_um2, i0 + g + 1 + START)
                        act.wait_ge(s_coef, i0 + g - 1 + START)
                        b = 2 + 2 * (g % 2)
                        af(gel[g % 2][:, 0:T // 2], ps[b][:, 0:T // 2], ACT.Gelu_apprx_tanh)
                        af(gel[g % 2][:, T // 2:T], ps[b + 1][:, 0:T // 2], ACT.Gelu_apprx_tanh).then_inc(s_gel, 1)
                        act.wait_ge(s_v[g % 2], 16 * (l * (NKEYS // 2) + n * (EG // 2) + g // 2 + 1) + START)
                        if g == 0:
                            act.wait_ge(s_vm2, (l * NG + n) * KC + START)
                        af(vH[g][:, :], vraw[g % 2][:, :], ACT.Copy).then_inc(s_vh, 1)
                    if more:
                        high_u(i0 + EG, 0)

                high_u(l * NKEYS, 0)
                with act.Fori(0, NG - 1) as n:
                    group(n, True)
                group(NG - 1, False)
            act.wait_ge(s_x2, DEPTH * KC + START)
            act.wait_ge(s_vm2, DEPTH * (NG * KC) + START)
            squares(2 * DEPTH)
            act.wait_ge(s_new, DEPTH * HEADS * 2 * 16 + START)

        @block.vector
        def _(dve):
            v = nc.vector
            tt, ts, stt = v.tensor_tensor, v.tensor_scalar, v.scalar_tensor_tensor

            def norm(before, scale_of, shift_of):
                dve.wait_ge(s_rs, before + 1 + START)
                for k in range(KC):
                    tt(hT[:, k, :], xT[:, k, :], rs[:, :], ALU.mult)
                dve.drain()
                for k in range(KC):
                    for q, cols_ in ((0, slice(0, TP)), (1, slice(TP, T))):
                        a, b = scale_of(k, q), shift_of(k, q)
                        if b is None:
                            last = ts(hT[:, k, cols_], hT[:, k, cols_], a, None, ALU.mult)
                        else:
                            last = ts(hT[:, k, cols_], hT[:, k, cols_], a, b, ALU.mult, ALU.add)
                    last.then_inc(s_h, 1)

            v.memset(ones[:, :], 1.0)
            v.memset(eps[:, :], EPS)
            v.memset(one[:, :], 1.0).then_inc(s_set, 1)
            for i in range(2 * NT):
                dve.wait_ge(s_xt, i + 1 + START)
                t, j = i // 2, i % 2
                v.tensor_copy(xT[:, 4 * j:4 * j + 4, t * P:(t + 1) * P], ps[j][:, :].rearrange("p (a n) -> p a n", a=4)).then_inc(s_xc, 1)
            dve.wait_ge(s_rowsT, 1 + START)
            v.tensor_copy(cols0[:, :], ps[7][:, 0:24]).then_inc(s_cols, 1)
            dve.wait_ge(s_econd, 1 + START)
            ts(scond[:, :, :], scond[:, :, :], 1.0, None, ALU.add)
            dve.drain()
            v.reciprocal(scond[:, :, :], scond[:, :, :])
            dve.drain()
            tt(scond[:, :, 0], scond[:, :, 0], cols0[:, 8:16], ALU.mult)
            tt(scond[:, :, 1], scond[:, :, 1], cols0[:, 0:8], ALU.mult).then_inc(s_cond, 1)

            with dve.Fori(0, DEPTH) as l:
                dve.wait_ge(s_rowsT, l + 2 + START)
                v.tensor_copy(cols[:, :], ps[7][:, 0:80]).then_inc(s_cols, 1)
                v.memset(att[:, :, :, :], 0.0)
                v.memset(hist[:, :, 0, :], 0.0)
                v.memset(wab[:, :, :], 0.0)
                dve.drain()
                v.memset(tot[:, :, :], 0.0).then_inc(s_zero, 1)
                with dve.Fori(0, MOD_B) as b:
                    dve.wait_ge(s_mt, l * MOD_B + b + 1 + START)
                    tt(modT[:, bass.ds(b * (2 * SLOTS), 2 * SLOTS), :], ps[6][:, 0:4 * SLOTS].rearrange("p (n q) -> p n q", q=2),
                       cols[:, bass.ds(b * (2 * SLOTS), 2 * SLOTS)].unsqueeze(2).to_broadcast([P, 2 * SLOTS, 2]),
                       ALU.add).then_inc(s_modT, 1)
                dve.drain()
                for a in range(2):
                    stt(nscale[:, a, :, :], modT[:, 8 + 24 * a:16 + 24 * a, :], 1.0,
                        cols[:, 48 + 8 * a:56 + 8 * a].unsqueeze(2).to_broadcast([P, KC, 2]), ALU.add, ALU.mult)
                dve.drain()
                norm(2 * l, lambda k, q: nscale[:, 0, k, q:q + 1], lambda k, q: modT[:, k, q:q + 1])

                with dve.Fori(0, HEADS) as h:
                    it = l * HEADS + h
                    dve.wait_ge(s_qk, it + 1 + START)
                    v.tensor_copy(qk[:, 1, TP:T], ps[2][:, :])
                    v.tensor_copy(qk[:, 1, 0:TP], ps[3][:, 0:TP]).then_inc(s_k, 1)
                    dve.wait_ge(s_gate, it + 1 + START)
                    for d in range(2):
                        bias = cols[:, bass.ds(h + (72 + 4 * d), 1)]
                        ts(gx[:, d, TP:T], ps[4 + 2 * d][:, :], bias, None, ALU.add)
                        last = ts(gx[:, d, 0:TP], ps[5 + 2 * d][:, 0:TP], bias, None, ALU.add)
                    last.then_inc(s_gx, 1)
                    dve.wait_ge(s_rot, it + 1 + START)
                    for a in range(2):
                        tt(qk[:, a, TP:T], qk[:, a, TP:T], cos, ALU.mult)
                        tt(e2[:, a, TP:T], ps[2 * a][:, :], sin, ALU.mult)
                    dve.drain()
                    for a in range(2):
                        tt(qk[:, a, TP:T], qk[:, a, TP:T], e2[:, a, TP:T], ALU.add)
                    dve.wait_ge(s_gl, it + 1 + START)
                    stt(gx[:, :, :], gx[:, :, :], 0.0, tmp[:, :, :], ALU.min, ALU.subtract)
                    dve.drain()
                    v.tensor_tensor_scan(bx[:, 0, :], reset, gx[:, 0, :], 0.0, ALU.mult, ALU.add)
                    v.tensor_tensor_scan(tmp[:, 0, :], reset, gx[:, 1, :], 0.0, ALU.mult, ALU.add)
                    dve.drain()
                    chunks = lambda ap: ap.rearrange("p (n c) -> p n c", c=CHUNK)
                    v.tensor_copy(tot[:, 0, :], chunks(bx[:, 0, :])[:, :, CHUNK - 1])
                    v.tensor_copy(tot[:, 1, :], chunks(tmp[:, 0, :])[:, :, CHUNK - 1])
                    dve.drain()
                    spread = lambda d: tot[:, d, :].unsqueeze(2).to_broadcast([P, NCH, CHUNK])
                    tt(chunks(dx[:, 0, :]), spread(0), chunks(bx[:, 0, :]), ALU.subtract)
                    tt(chunks(tmp[:, 1, :]), spread(1), chunks(tmp[:, 0, :]), ALU.subtract)
                    tt(dx[:, 1, :], tmp[:, 0, :], gx[:, 1, :], ALU.subtract)
                    dve.drain()
                    tt(bx[:, 1, :], tmp[:, 1, :], gx[:, 1, :], ALU.add).then_inc(s_ex, 1)
                    rr = on[:, :, :].rearrange("p t e -> p (t e)")
                    dve.wait_ge(s_re, it + 1 + START)
                    ts(rr, rr, 1.0, None, ALU.add)
                    dve.drain()
                    v.reciprocal(rr, rr)
                    dve.drain()
                    tt(rsil[:, 0, TP:T], ps[4][:, :], rr[:, 0:TS], ALU.mult)
                    tt(rsil[:, 1, TP:T], ps[6][:, :], rr[:, TS:2 * TS], ALU.mult)
                    tt(rsil[:, :, 0:TP], ps[7][:, 0:2 * TP].rearrange("p (j n) -> p j n", j=2),
                       rr[:, 2 * TS:2 * TS + 2 * TP].rearrange("p (j n) -> p j n", j=2), ALU.mult).then_inc(s_r, 1)
                    dve.wait_ge(s_dec, it + 1 + START)
                    qb = qk[:, 0, :].unsqueeze(1).to_broadcast([P, 2, T])
                    kb = qk[:, 1, :].unsqueeze(1).to_broadcast([P, 2, T])
                    tt(dx[:, :, :], dx[:, :, :], kb, ALU.mult)
                    tt(e2[:, :, :], e2[:, :, :], kb, ALU.mult)
                    tt(bx[:, :, :], bx[:, :, :], qb, ALU.mult).then_inc(s_scal, 1)
                    hold(dve, s_am, it + 1 + START)
                    for d in range(2):
                        v.copy_predicated(att[:, d, 1:NT, :], mask[d].unsqueeze(1).to_broadcast([P, 4, P]),
                                          ps[4 + 2 * d][:, :].rearrange("p (t n) -> p t n", n=P))
                    for d in range(2):
                        last = v.copy_predicated(att[:, d, 0, :], mask[d], ps[5][:, d * P:(d + 1) * P])
                    last.then_inc(s_a, 1)
                    dve.wait_ge(s_init, 32 * it + 32)
                    dve.wait_ge(s_new, 32 * it + START)
                    for i in range(9):
                        dve.wait_ge(s_ds, it * 9 + i + 1 + START)
                        src = i if i < 2 else i + 1
                        for d in range(2):
                            ch = step_chunk(i, d)
                            last = stt(hist[:, d, src + 1, :], hist[:, d, src, :], dec[:, d, ch:ch + 1],
                                       ps[STEP_BANKS[i % 2][d]][:, 0:DV], ALU.mult, ALU.add)
                        last.then_inc(s_st, 1)
                        dve.drain()
                    dve.wait_ge(s_ont, it + 1 + START)
                    for j in range(2):
                        gn = cols[:, bass.ds(h * 2 + (64 + j), 1)]
                        dst = oT[:, bass.ds(h * 2 + j, 1), :].rearrange("p a n -> p (a n)")
                        stt(dst[:, TP:T], ps[2 * j][:, :], gn, rsil[:, j, TP:T], ALU.mult, ALU.mult)
                        last = stt(dst[:, 0:TP], ps[1][:, j * P:(j + 1) * P], gn, rsil[:, j, 0:TP], ALU.mult, ALU.mult)
                    last.then_inc(s_o, 1)

                with dve.Fori(0, ZC) as z:
                    n = l * ZC + z
                    dve.wait_ge(s_ze, n + 1 + START)
                    ts(sg[:, :, :], sg[:, :, :], 1.0, None, ALU.add)
                    dve.drain()
                    v.reciprocal(sg[:, :, :], sg[:, :, :])
                    dve.drain()
                    dve.wait_ge(s_ym, n + 1 + START)
                    for a in range(2):
                        tt(sg[:, a, TP:T], sg[:, a, TP:T], ps[4 + 2 * a][:, :], ALU.mult)
                        tt(sg[:, a, 0:TP], sg[:, a, 0:TP], ps[5 + 2 * a][:, 0:TP], ALU.mult)
                    dve.drain()
                    tt(mT[:, bass.ds(z, 1), :].rearrange("p a n -> p (a n)"), sg[:, 0, :], sg[:, 1, :], ALU.add).then_inc(s_mg, 1)
                with dve.Fori(0, 2) as o:
                    for q in range(4):
                        dve.wait_ge(s_out, l * OC + o * 4 + q + 1 + START)
                        xs = xT[:, bass.ds(o * 4 + q, 1), :].rearrange("p a n -> p (a n)")
                        for a, cc, bank in ((1, slice(TP, T), ps[2 * q][:, :]), (0, slice(0, TP), ps[2 * q + 1][:, 0:TP])):
                            g1 = modT[:, bass.ds(o * 4 + (16 + q), 1), a]
                            last = stt(xs[:, cc], bank, g1, xs[:, cc], ALU.mult, ALU.add)
                        last.then_inc(s_x1, 1)
                norm(2 * l + 1, lambda k, q: nscale[:, 1, k, q:q + 1], lambda k, q: modT[:, 24 + k, q:q + 1])

                with dve.Fori(0, PH) as h:
                    it = l * PH + h
                    hold(dve, s_sc, it + 1 + START)
                    lists = [(t, s) for t in range(NT) for s in range(2)]
                    for rank in range(2):
                        r8 = slice(8 * rank, 8 * rank + 8)
                        for t, s in lists:
                            v.max(top[:, t, s, r8], sc[:, t, s, :])
                        dve.drain()
                        for t, s in lists:
                            v.max_index(ti[:, t, s, r8], top[:, t, s, r8], sc[:, t, s, :])
                        dve.drain()
                        if rank == 0:
                            for t, s in lists:
                                v.match_replace(sc[:, t, s, :], top[:, t, s, r8], sc[:, t, s, :], LOWEST)
                            dve.drain()
                    v.tensor_copy(tif[:, :, :, :], ti[:, :, :, :]).then_inc(s_scf, 1)
                    tt(cand[:, :, :, :], top[:, :, 0, :].unsqueeze(3).to_broadcast([P, NT, TOPK, TOPK]),
                       top[:, :, 1, :].unsqueeze(2).to_broadcast([P, NT, TOPK, TOPK]), ALU.add)
                    dve.drain()
                    flat = lambda t: cand[:, t, :, :].rearrange("p a b -> p (a b)")
                    for rank in range(2):
                        r8 = slice(8 * rank, 8 * rank + 8)
                        for t in range(NT):
                            v.max(best[:, t, r8], flat(t))
                        dve.drain()
                        for t in range(NT):
                            v.max_index(sel[:, t, r8], best[:, t, r8], flat(t))
                        dve.drain()
                        if rank == 0:
                            for t in range(NT):
                                v.match_replace(flat(t), best[:, t, r8], flat(t), LOWEST)
                            dve.drain()
                    v.tensor_copy(bsum[:, :], best[:, :, 0])
                    ts(selab[:, 0, :, :], sel[:, :, :], 4, None, ALU.logical_shift_right)
                    ts(selab[:, 1, :, :], sel[:, :, :], TOPK - 1, None, ALU.bitwise_and)
                    dve.drain()
                    tt(best[:, :, :], best[:, :, :], bsum[:, :].unsqueeze(2).to_broadcast([P, NT, TOPK]), ALU.subtract).then_inc(s_d, 1)
                    v.tensor_copy(self_[:, :, :, :], selab[:, :, :, :])
                    dve.drain()
                    for s in range(2):
                        tt(hot[:, s, :, :, :].rearrange("p t k a -> p (t k) a"),
                           self_[:, s, :, :].rearrange("p t k -> p (t k)").unsqueeze(2).to_broadcast([P, NT * TOPK, TOPK]),
                           iota[:, 0:TOPK].unsqueeze(1).to_broadcast([P, NT * TOPK, TOPK]), ALU.is_equal)
                    dve.drain()
                    for s in range(2):
                        tt(hot[:, s, :, :, :], hot[:, s, :, :, :],
                           tif[:, :, s, :].unsqueeze(2).to_broadcast([P, NT, TOPK, TOPK]), ALU.mult)
                    dve.drain()
                    for s in range(2):
                        v.tensor_reduce(wsel[:, 1 + s, :, bass.ds(h * TOPK, TOPK)], hot[:, s, :, :, :], AX_X, ALU.add)
                    dve.wait_ge(s_e, it + 1 + START)
                    v.tensor_reduce(bsum[:, :], best[:, :, :], AX_X, ALU.add)
                    dve.drain()
                    v.reciprocal(bsum[:, :], bsum[:, :])
                    dve.drain()
                    tt(wsel[:, 0, :, bass.ds(h * TOPK, TOPK)], best[:, :, :],
                       bsum[:, :].unsqueeze(2).to_broadcast([P, NT, TOPK]), ALU.mult).then_inc(s_sel, 1)
                hold(dve, s_tc, l + 1 + START)
                with dve.Fori(0, NWG // 4) as g:
                    for b in range(4):
                        dve.wait_ge(s_wm, l * NWG + g * 4 + (b - 3) + START)
                        for q in range(4):
                            n = g * 16 + (b * 4 + q)
                            ts(onehot[:, b, q, 0, :], iota, wselT[:, 1, bass.ds(n, 1)], wselT[:, 0, bass.ds(n, 1)],
                               ALU.is_equal, ALU.mult)
                            last = ts(onehot[:, b, q, 1, :], iota, wselT[:, 2, bass.ds(n, 1)], None, ALU.is_equal)
                        last.then_inc(s_hot, 1)
                for i in range(2):
                    hold(dve, s_wst[i], (l + 1) * (WST[i] * 16) + START)
                v.memset(accT[:, :, :], 0.0)
                v.tensor_copy(hH[:, :, :], hT[:, :, :])
                dve.drain()
                tt(hL[:, :, :], hT[:, :, :], hH[:, :, :].bitcast(F32), ALU.subtract).then_inc(s_hs, 1)

                def low_u(i, b):
                    dve.wait_ge(s_utc, i + 1 + START)
                    for q in range(2):
                        last = tt(uL[b][:, 4 * q:4 * q + 4, :], ps[q][:, :].rearrange("p (k n) -> p k n", k=4),
                                  uH[b][:, 4 * q:4 * q + 4, :].bitcast(F32), ALU.subtract)
                    last.then_inc(s_ul, 1)

                def group(n, more):
                    i0 = l * NKEYS + n * EG
                    k0 = (l * NG + n) * KC
                    for g in range(EG):
                        if g + 1 < EG:
                            low_u(i0 + g + 1, (g + 1) % 2)
                        b = g % 2
                        dve.wait_ge(s_w[b], 16 * (l * (NKEYS // 2) + n * (EG // 2) + g // 2 + 1) + START)
                        dve.wait_ge(s_gel, i0 + g + 1 + START)
                        if g == 0:
                            dve.wait_ge(s_vm2, k0 + START)
                        tt(gel[b][:, :], gel[b][:, :], wex[b][:, :], ALU.mult)
                        dve.drain()
                        v.tensor_copy(cH[g][:, :], gel[b][:, :])
                        dve.drain()
                        tt(cL[g][:, :], gel[b][:, :], cH[g][:, :].bitcast(F32), ALU.subtract).then_inc(s_coef, 1)
                        dve.wait_ge(s_vh, i0 + g + 1 + START)
                        tt(vL[g][:, :], vraw[b][:, :], vH[g][:, :].bitcast(F32), ALU.subtract).then_inc(s_vl, 1)
                    if more:
                        low_u(i0 + EG, 0)
                    for k in range(KC):
                        dve.wait_ge(s_vm2, k0 + k + 1 + START)
                        bank = 6 if k % 2 == 0 else 2
                        for q in range(2):
                            half = slice(q * (T // 2), (q + 1) * (T // 2))
                            last = tt(accT[:, k, half], accT[:, k, half], ps[bank + q][:, 0:T // 2], ALU.add)
                        last.then_inc(s_acc, 1)

                low_u(l * NKEYS, 0)
                with dve.Fori(0, NG - 1) as n:
                    group(n, True)
                group(NG - 1, False)
                dve.drain()
                for k in range(KC):
                    stt(xT[:, k, 0:TP], accT[:, k, 0:TP], modT[:, 40 + k, 0:1], xT[:, k, 0:TP], ALU.mult, ALU.add)
                    stt(xT[:, k, TP:T], accT[:, k, TP:T], modT[:, 40 + k, 1:2], xT[:, k, TP:T], ALU.mult, ALU.add).then_inc(s_x2, 1)
            norm(2 * DEPTH, lambda k, q: cols0[:, 16 + k:17 + k], lambda k, q: None)
            for i in range(2 * NT):
                dve.wait_ge(s_yt, i + 1 + START)
                t, j = i // 2, i % 2
                v.tensor_copy(ynat[:, t, j * 512:(j + 1) * 512], ps[4 + j][:, :]).then_inc(s_yc, 1)


WST = [3, 2]


def USES_(s, l):
    return l * USES[s]


STEP_BANKS = [(3, 7), (1, 2)]


def step_chunk(i, d):
    if i < 2:
        return i if d == 0 else 1 - i
    return i if d == 0 else 11 - i


def prev_slot(ch, d):
    if ch < 2:
        return ch if d == 0 else 1 - ch
    return ch + 1 if d == 0 else 12 - ch


_INS = ["x_prompt", "x_sample", "state_gla", "c", "c_ctx", "w_mod", "b_mod", "norm1", "w_in", "w_af", "b_af", "w_ab",
        "b_ab", "gla_norm", "w_gla_out", "w_four_out", "w_out", "norm2", "w_query", "sub_keys", "expert_u",
        "expert_v", "final_norm"]
_OUTS = [(1, TP, D), (1, TS, D), (1, DEPTH, 2, HEADS, P, DV)]


def kernel(**inputs):
    import concourse.bacc as _bacc
    from concourse.bass_utils import run_bass_kernel_spmd as _run

    nc = _bacc.Bacc("TRN2", target_bir_lowering=False, num_devices=1)
    arrays, args = {}, []
    for name in _INS:
        a = np.ascontiguousarray(inputs[name])
        arrays[f"in_{name}"] = a
        args.append(nc.dram_tensor(f"in_{name}", a.shape, mybir.dt.from_np(a.dtype), kind="ExternalInput").ap())
    for name, a in zip(("consts", "fourier"), constants()):
        arrays[f"table_{name}"] = a
        args.append(nc.dram_tensor(f"table_{name}", a.shape, F32, kind="ExternalInput").ap())
    for i, shape in enumerate(_OUTS):
        args.append(nc.dram_tensor(f"out_{i}", shape, F32, kind="ExternalOutput").ap())
    build(nc, *args)
    r = _run(nc, [arrays], core_ids=[0])
    return tuple(r.results[0][f"out_{i}"] for i in range(len(_OUTS)))
```

```python
from contextlib import ExitStack

import concourse.bass as bass
import numpy as np
from concourse import mybir

F32 = mybir.dt.float32
F32R = mybir.dt.float32r
U32 = mybir.dt.uint32
ALU = mybir.AluOpType
ACT = mybir.ActivationFunctionType
AX_X = mybir.AxisListType.X

P = 128
D = 1024
KC = D // P
DEPTH = 2
TP, TS = 128, 512
T = TP + TS
NT = T // P
GRID_W = 64
HEADS, DV = 4, 256
CHUNK = 64
NCH = T // CHUNK
LOWRANK = 16
TAU = 16.0
GROUPS = 4
QK_W, V_W, F_W = 512, 1024, 512
PH = 8
NKEYS = 128
TOPK = 16
WIDE, NARROW = 4, 4
NWIDE = WIDE * TOPK
NCAND = NWIDE + (TOPK - WIDE) * NARROW
EG = 4
NG = NKEYS // EG
NB = 8
EPS = 1e-6
ROPE_THETA = 10000.0
LOWEST = -3.0e38

Q0, K0, V0 = 0, QK_W, 2 * QK_W
R0 = V0 + V_W
L0 = R0 + V_W
U0 = L0 + 2 * LOWRANK
ZG0 = U0 + F_W
ZF0 = ZG0 + D

C_ID, C_IOTA, C_ROT, C_COS, C_SIN = 0, 128, 256, 384, 896
C_MF, C_MB, C_RESET, C_CDSD = 1408, 1536, 1664, 2304
C_W = 2560

START = 4
SLOTS = 6
WCOLS = 256
MOD_B = 6 * D // (SLOTS * WCOLS)
OUT_SLOTS = [4, 5, 0, 1]
HEAD_FILLS = MOD_B
MERGE_FILLS = [HEAD_FILLS + 2 * HEADS] + 3 * [HEAD_FILLS + HEADS]
OUT_FILLS = [MOD_B, MOD_B, MERGE_FILLS[0] + KC, MERGE_FILLS[1] + KC]
QUERY_FILLS = OUT_FILLS[2] + 2
FILLS = [QUERY_FILLS + PH, OUT_FILLS[3] + 2, MERGE_FILLS[2] + KC, MERGE_FILLS[3] + KC, MOD_B + 2, MOD_B + 2]


def constants():
    c = np.zeros((P, C_W), np.float32)
    c[:, C_ID:C_ID + 128] = np.eye(128)
    rot = np.zeros((128, 128))
    for base in (0, 64):
        for i in range(32):
            rot[base + i, base + 32 + i] = -1.0
            rot[base + 32 + i, base + i] = 1.0
    c[:, C_ROT:C_ROT + 128] = rot.T
    c[:, C_IOTA:C_IOTA + 128] = np.arange(128)[None, :]
    freqs = (np.float32(ROPE_THETA) ** (-np.arange(32, dtype=np.float32) / np.float32(32))).astype(np.float32)
    tok = np.arange(TS)
    row, col = tok // GRID_W, tok % GRID_W
    for base, pos in ((0, row), (64, col)):
        ang = (pos.astype(np.float32)[None, :] * freqs[:, None]).astype(np.float32).astype(np.float64)
        for o in (0, 32):
            c[base + o:base + o + 32, C_COS:C_COS + TS] = np.cos(ang)
            c[base + o:base + o + 32, C_SIN:C_SIN + TS] = np.sin(ang)
    s, t = np.arange(128)[:, None], np.arange(128)[None, :]
    same = (s // CHUNK) == (t // CHUNK)
    c[:, C_MF:C_MF + 128] = same & (s <= t)
    c[:, C_MB:C_MB + 128] = same & (s >= t)
    c[:, C_RESET:C_RESET + T] = (np.arange(T) % CHUNK != 0)[None, :]
    a = 2 * np.pi * ((s * t) % 128) / 128
    c[:, C_CDSD:C_CDSD + 128] = np.cos(a) / np.sqrt(128)
    c[:, C_CDSD + 128:C_CDSD + 256] = np.sin(a) / np.sqrt(128)
    k, n = np.arange(TS)[:, None], np.arange(TS)[None, :]
    a5 = 2 * np.pi * ((k * n) % TS) / TS
    lat = np.stack([np.cos(a5), -np.sin(a5)], 1) / np.sqrt(TS)
    lat = lat.reshape(4, P, 2, TS).transpose(1, 0, 2, 3).reshape(P, -1)
    ctx = np.stack([np.cos(a), -np.sin(a)], 1).reshape(P, -1) / np.sqrt(TP)
    return c, np.concatenate([lat, ctx], 1).astype(np.float32)


TT_W = 4 * 2 * TS + 2 * TP


def build(nc, x_prompt, x_sample, state_gla, c, c_ctx, w_mod, b_mod, norm1, w_in, w_af, b_af, w_ab, b_ab,
          gla_norm, w_gla_out, w_four_out, w_out, norm2, w_query, sub_keys, expert_u, expert_v, final_norm,
          consts, fourier, y_prompt, y_sample, new_state):
    wd = nc.dram_tensor("expert_weights", [DEPTH, NT, NKEYS, NKEYS, P], F32, kind="Internal").ap()

    cursor = [nc.sbuf_base + 31 & ~31]

    def place(name, shape, dt=F32, at=None):
        n = int(np.prod(shape[1:])) * 4
        off = cursor[0] if at is None else at[0]
        t = nc.alloc_sbuf_tensor_at(name, shape, dt, offset=off)
        nxt = (off + n + 31) & ~31
        if at is None:
            cursor[0] = nxt
        else:
            at[0] = nxt
        return t

    cst_at = cursor[0]
    cst = place("cst", [P, C_W])
    xT = place("xT", [P, KC, T])
    hL = place("hL", [P, KC, T], F32R, at=[cursor[0]])
    hT = place("hT", [P, KC, T])
    ones = place("ones", [P, P])
    eps = place("eps", [P, 1])
    one = place("one", [P, 1])
    rows0 = place("rows0", [24, P])
    cols0 = place("cols0", [P, 24])
    scond = place("scond", [P, KC, 2])
    rows = place("rows", [80, P])
    cols = place("cols", [P, 80])
    modT = place("modT", [P, 48, 2])
    nscale = place("nscale", [P, 2, KC, 2])
    rs_at = cursor[0]
    rs = place("rs", [P, T])
    base = cursor[0]

    mr = [base]
    mrow = [place(f"mrow{i}", [2, WCOLS], at=mr) for i in range(SLOTS)]
    m = [base]
    qk = place("qk", [P, 2, T], at=m)
    gx = place("gx", [P, 2, T], at=m)
    bx = place("bx", [P, 2, T], at=m)
    dx = place("dx", [P, 2, T], at=m)
    tmp = place("tmp", [P, 2, T], at=m)
    e2 = place("e2", [P, 2, T], at=m)
    kdT = place("kdT", [P, 2, NT, P], at=m)
    att = place("att", [P, 2, NT, P], at=m)
    hist = place("hist", [P, 2, 11, DV], at=m)
    v_sb = place("v_sb", [P, NT, DV], at=m)
    rsil = place("rsil", [P, 2, T], at=m)
    on = place("on", [P, NT, DV], at=m)
    tot = place("tot", [P, 2, NCH], at=m)
    dec = place("dec", [P, 2, NCH], at=m)
    oss = place("oss", [P, 8], at=m)
    ors = place("ors", [P, 8], at=m)
    wlr = place("wlr", [P, KC, 2 * LOWRANK], at=m)
    lrT = place("lrT", [2 * LOWRANK, T], at=m)
    wab = place("wab", [2 * LOWRANK, 2, P], at=m)
    oT_at = m[0]
    oT = place("oT", [P, KC, T], at=m)
    ring0 = nc.sbuf_usable_end - SLOTS * KC * WCOLS * 4 & ~31
    assert m[0] <= ring0, (m[0], ring0)
    uT_at = m[0]
    uT = place("uT", [P, GROUPS, T], at=m)
    assert m[0] <= ring0 + KC * WCOLS * 4
    rg = [ring0]
    last_slot = place(f"slot{SLOTS - 1}", [P, KC, WCOLS], at=rg)
    slot = [place(f"slot{i}", [P, KC, WCOLS], at=rg) for i in range(SLOTS - 1)] + [last_slot]
    f = [base]
    fourT = place("fourT", [P, GROUPS, T], at=f)
    ab = place("ab", [P, NT, GROUPS, 2, P], at=f)
    table = place("table", [P, TT_W], at=f)
    assert f[0] <= base + 20 * T * 4 + 2 * 11 * DV * 4, f[0] - base
    f2 = [base]
    fourL = place("fourL", [P, GROUPS, T], F32R, at=f2)
    mT_at = f2[0]
    mT = place("mT", [P, KC, T], at=f2)
    fourH = place("fourH", [P, GROUPS, T], F32R, at=f2)
    oH = place("oH", [P, KC, T], F32R, at=f2)
    hmH_at = oT_at - KC * T * 4
    assert f[0] <= hmH_at and f2[0] <= hmH_at
    hmH = place("hmH", [P, KC, T], F32R, at=[hmH_at])
    oL = place("oL", [P, KC, T], F32R, at=[oT_at])
    wraw, wH, wL, sg = [], [], [], []
    for i in range(4):
        n, at = (KC if i < 3 else GROUPS), ring0 + (i + 1) * KC * WCOLS * 4
        wraw.append(place(f"wraw{i}", [P, n, P], at=[at]))
        wL.append(place(f"wL{i}", [P, n, P], F32R, at=[at]))
        wH.append(place(f"wH{i}", [P, n, P], F32R, at=[at + n * P * 4]))
    mH = place("mH", [P, KC, T], F32R, at=[hmH_at])
    mL = place("mL", [P, KC, T], F32R, at=[mT_at])
    oraw, owH, owL = [], [], []
    for i, number in enumerate(OUT_SLOTS):
        at = ring0 + (number + 1) % SLOTS * KC * WCOLS * 4
        oraw.append(place(f"oraw{i}", [P, KC, P], at=[at]))
        owL.append(place(f"owL{i}", [P, KC, P], F32R, at=[at]))
        owH.append(place(f"owH{i}", [P, KC, P], F32R, at=[at + KC * P * 4]))
    sg.append(place("sg0", [P, T], at=[ring0 + 4 * KC * WCOLS * 4 + 2 * GROUPS * P * 4]))
    sg.append(place("sg1", [P, T], at=[uT_at]))
    assert uT_at + T * 4 <= ring0

    p = [base]
    wselT = place("wselT", [P, 3, T], at=p)
    pq = [p[0]]
    wsel = place("wsel", [P, 3, NT, P], at=pq)
    hotA = place("hotA", [P, 2, NB, P], at=p)
    hotB = place("hotB", [P, 2, NB, P], at=p)
    qryT = place("qryT", [P, 2, T], at=pq)
    dg = [cst_at + C_ROT * 4]
    hot16 = place("hot16", [P, 2, 2, 2 * NB, NKEYS // 8], at=dg)
    hot8 = place("hot8", [P, 2, 2, 2 * NB, 8], at=dg)
    low_int = place("low_int", [P, 2, P], U32, at=dg)
    low_digit = place("low_digit", [P, 2, P], at=dg)
    assert dg[0] <= cst_at + C_W * 4
    dg = [rs_at]
    key_int = place("key_int", [P, 2, P], U32, at=dg)
    high_int = place("high_int", [P, 2, P], U32, at=dg)
    high_digit = place("high_digit", [P, 2, P], at=[rs_at])
    skey = place("skey", [P, 2, P], at=pq)
    skT = place("skT", [P, 2, P], at=pq)
    sc = place("sc", [P, NT, 2, P], at=pq)
    top = place("top", [P, NT, 2, TOPK], at=pq)
    ti = place("ti", [P, NT, 2, TOPK], U32, at=pq)
    tif = place("tif", [P, 2, NT, TOPK], at=pq)
    cand = place("cand", [P, NT, NCAND], at=pq)
    best = place("best", [P, NT, TOPK], at=pq)
    sel = place("sel", [P, NT, TOPK], U32, at=pq)
    parts_int = place("parts_int", [P, 4, NT, TOPK], U32, at=pq)
    parts = place("parts", [P, 4, NT, TOPK], at=pq)
    place_no = place("place_no", [P, NT, TOPK], at=pq)
    step = place("step", [P, 2, NT, TOPK], at=pq)
    rank_ab = place("rank_ab", [P, 2, NT, TOPK], at=pq)
    hot = place("hot", [P, 2, NT, TOPK, TOPK], at=pq)
    bsum = place("bsum", [P, NT], at=pq)
    assert pq[0] <= ring0
    wb = [p[0]]
    wbuf = [place(f"wbuf{i}", [P, NKEYS, P], at=wb) for i in range(2)]
    assert wb[0] <= nc.sbuf_usable_end, (wb[0], nc.sbuf_usable_end)
    e = [base]
    uH = [place(f"uH{i}", [P, KC, P], F32R, at=e) for i in range(2)]
    uL = [place(f"uL{i}", [P, KC, P], F32R, at=e) for i in range(2)]
    gel = [place(f"gel{i}", [P, T], at=e) for i in range(2)]
    assert e[0] <= p[0]
    vraw = [place(f"vraw{i}", [P, D], at=e) for i in range(2)]
    vH = [place(f"vH{i}", [P, D], F32R, at=e) for i in range(EG)]
    vL = [place(f"vL{i}", [P, D], F32R, at=e) for i in range(EG)]
    wex = [place(f"wex{i}", [P, T], at=e) for i in range(2)]
    cH = [place(f"cH{i}", [P, T], F32R, at=e) for i in range(EG)]
    cL = [place(f"cL{i}", [P, T], F32R, at=e) for i in range(EG)]
    assert e[0] <= p[0] + NKEYS * P * 4
    e = [p[0] + NKEYS * P * 4]
    usb = [place(f"usb{i}", [P, D], at=e) for i in range(EG)]
    accT = place("accT", [P, KC, T], at=e)
    hH = place("hH", [P, KC, T], F32R, at=e)
    assert e[0] <= nc.sbuf_usable_end
    xnat = place("xnat", [P, NT, D], at=[base])
    ynat = place("ynat", [P, NT, D], at=[base])

    ident = cst[:, C_ID:C_ID + 128]
    rotT = cst[:, C_ROT:C_ROT + 128]
    iota = cst[:, C_IOTA:C_IOTA + 128]
    cos, sin = cst[:, C_COS:C_COS + TS], cst[:, C_SIN:C_SIN + TS]
    mask = [cst[:, C_MF:C_MF + 128].bitcast(U32), cst[:, C_MB:C_MB + 128].bitcast(U32)]
    reset = cst[:, C_RESET:C_RESET + T]
    cdsd = cst[:, C_CDSD:C_CDSD + 256]

    with ExitStack() as ctx:
        ps = [ctx.enter_context(nc.psum_tensor(f"bank{i}", [P, 512], F32)) for i in range(8)]

        semaphores = []

        def sem(name):
            semaphores.append(ctx.enter_context(nc.semaphore(name)))
            return semaphores[-1]

        def pool_load(name):
            return ctx.enter_context(nc.semaphore(name))

        s_const, s_x, s_rows = sem("const_loaded"), sem("x_loaded"), pool_load("rows_loaded")
        s_slot = [sem(f"slot{i}_loaded") for i in range(SLOTS)]
        s_wlr, s_wab, s_init, s_table = pool_load("wlr_loaded"), pool_load("wab_loaded"), pool_load("states_loaded"), sem("table_loaded")
        s_skey = pool_load("subkeys_loaded")
        s_u = [sem(f"expert_u{i}_loaded") for i in range(EG)]
        s_v = [sem(f"expert_v{i}_loaded") for i in range(2)]
        s_w = [sem(f"expert_w{i}_loaded") for i in range(2)]
        s_new, s_y = sem("new_state_stored"), sem("y_stored")
        s_wst = [sem(f"weights{i}_stored") for i in range(2)]
        s_set = sem("constants_set")
        s_xt, s_xc = sem("x_turned"), sem("x_copied")
        s_rowsT, s_cols = sem("rows_turned"), sem("cols_ready")
        s_econd, s_cond, s_mod, s_modT = sem("cond_exp"), sem("cond_ready"), sem("mod_mm"), sem("mod_ready")
        s_sq, s_ss, s_rs, s_h = sem("squares"), sem("square_sums"), sem("rstd"), sem("h_ready")
        s_lr, s_lrT = sem("lr_mm"), sem("lr_ready")
        s_qk, s_q, s_k = sem("qk_mm"), sem("q_copied"), sem("k_copied")
        s_gate, s_gx, s_gl, s_ex = sem("gate_mm"), sem("gate_x"), sem("gate_log"), sem("exponents")
        s_rot, s_dec = sem("rot_mm"), sem("decays_exp")
        s_vm, s_vc, s_rm, s_re, s_r = sem("v_mm"), sem("v_copied"), sem("r_mm"), sem("r_exp"), sem("r_silu")
        s_scal, s_kdm, s_kd = sem("qk_scaled"), sem("kd_turned"), sem("kd_copied")
        s_am, s_a, s_ds, s_st = sem("att_mm"), sem("att_masked"), sem("dstate_mm"), sem("state_step")
        s_om, s_on, s_ont, s_o = sem("o_mm"), sem("o_normed"), sem("o_turned"), sem("o_gated")
        s_um, s_uc, s_f1, s_f1c, s_f2, s_f2c = (sem("u_mm"), sem("u_copied"), sem("fourier_d"), sem("fourier_d_copied"),
                                               sem("fourier_t"), sem("fourier_ready"))
        s_zm, s_ym, s_ze, s_mg, s_out, s_x1 = (sem("z_mm"), sem("y_mm"), sem("z_exp"), sem("merged"), sem("out_mm"),
                                              sem("x_mixed"))
        s_zgm, s_glm, s_sg = sem("z_gla_mm"), sem("gla_out_mm"), sem("gates_ready")
        s_part = [s_zgm, s_zm, s_glm, s_ym]
        s_wh = [sem(f"weights{i}_high") for i in range(4)]
        s_wl = [sem(f"weights{i}_low") for i in range(4)]
        s_ms, s_owh, s_owl = sem("merged_split"), sem("w_out_high"), sem("w_out_low")
        s_hms, s_os, s_fs = sem("mixer_h_split"), sem("o_split"), sem("fourier_split")
        s_qm, s_qc, s_kt, s_ktc, s_sm, s_sc = (sem("query_mm"), sem("query_copied"), sem("keys_turned"),
                                              sem("keys_copied"), sem("score_mm"), sem("scores_copied"))
        s_eq, s_key = sem("rank_onehots"), sem("keys_resolved")
        s_d, s_e, s_sel = sem("best_minus_max"), sem("best_exp"), sem("slots_chosen")
        s_tm, s_tc = sem("slots_turned"), sem("slots_ready")
        s_tab = sem("tables_loaded")
        s_digit = sem("digit_onehots")
        s_hotA, s_hotB, s_wm, s_wc = sem("key1_onehots"), sem("key2_onehots"), sem("weights_mm"), sem("weights_copied")
        s_utm, s_utc, s_um2, s_gel, s_coef, s_vm2, s_acc, s_x2 = (
            sem("u_turned"), sem("uT_copied"), sem("expert_a"), sem("gelu_done"), sem("coef_ready"), sem("expert_out"),
            sem("expert_added"), sem("x_done"))
        s_yt, s_yc = sem("y_turned"), sem("y_copied")
        s_zero = sem("zeros_set")
        s_hs, s_ul, s_vh, s_vl = sem("h_split"), sem("uT_split"), sem("v_high"), sem("v_split")
        s_mr, s_mt, s_scf = sem("mod_row_copied"), sem("mod_turned"), sem("scores_used")

        s_passed = sem("waits_passed")

        def hold(eng, semaphore, value):
            eng.wait_ge(semaphore, value)
            eng.sem_inc(s_passed, 1)

        for n, semaphore in enumerate(semaphores):
            (nc.sync, nc.scalar, nc.vector, nc.tensor)[n % 4].sem_inc(semaphore, START)
        nc.all_engine_barrier()

        block = ctx.enter_context(nc.Block())
        NWG = T // 4
        ZC, OC = KC, KC

        def wcols_at(w, l, c0):
            return w[l][:, bass.ds(c0, WCOLS)].rearrange("(c p) n -> p c n", p=P)

        def digit_product(engine, hot, b, a, q):
            tok = slice(q * NB, (q + 1) * NB)
            return engine.tensor_tensor(
                hot[:, q, :, :].rearrange("p n (u v) -> p n u v", v=8),
                hot16[:, b, a, tok, :].unsqueeze(3).to_broadcast([P, NB, NKEYS // 8, 8]),
                hot8[:, b, a, tok, :].unsqueeze(2).to_broadcast([P, NB, NKEYS // 8, 8]), ALU.mult)

        @block.sync
        def _(sp):
            sp.dma_start(cst[:, 0:C_ROT], consts[:, 0:C_ROT]).then_inc(s_const, 16)
            sp.dma_start(xnat[:, 0, :], x_prompt[0]).then_inc(s_x, 16)
            sp.dma_start(xnat[:, 1:NT, :], x_sample[0].rearrange("(t p) d -> p t d", p=P)).then_inc(s_x, 16)
            with sp.Fori(0, DEPTH) as l:
                hold(sp, s_x2, l * KC + START)
                hold(sp, s_vm2, l * (NG * KC) + START)
                hold(sp, s_out, l * OC + START)
                hold(sp, s_qm, l * PH + START)
                for i in range(2):
                    hold(sp, s_wst[i], l * (WST[i] * 16) + START)
                with sp.Fori(0, MOD_B) as b:
                    for s in range(SLOTS):
                        hold(sp, s_mod, l * (MOD_B * SLOTS) + b * SLOTS + START)
                        sp.dma_start(slot[s][:, :, :], wcols_at(w_mod, l, b * (SLOTS * WCOLS) + s * WCOLS)).then_inc(s_slot[s], 16)
                hold(sp, s_wm, l * NWG + START)
                sp.dma_start(cst[:, C_ROT:C_W], consts[:, C_ROT:C_W]).then_inc(s_tab, 16)
                hold(sp, s_mod, l * (MOD_B * SLOTS) + MOD_B * SLOTS + START)
                with sp.Fori(0, HEADS) as h:
                    it = l * HEADS + h
                    hold(sp, s_qk, it + START)
                    sp.dma_start(slot[0][:, :, 0:P], w_in[l][:, bass.ds(h * P + Q0, P)].rearrange("(c p) n -> p c n", p=P)).then_inc(s_slot[0], 16)
                    sp.dma_start(slot[0][:, :, P:2 * P], w_in[l][:, bass.ds(h * P + K0, P)].rearrange("(c p) n -> p c n", p=P)).then_inc(s_slot[0], 16)
                    hold(sp, s_vm, it + START)
                    sp.dma_start(slot[1][:, :, :], wcols_at(w_in, l, h * DV + V0)).then_inc(s_slot[1], 16)
                    hold(sp, s_rm, it + START)
                    sp.dma_start(slot[2][:, :, :], wcols_at(w_in, l, h * DV + R0)).then_inc(s_slot[2], 16)
                    hold(sp, s_um, it + START)
                    sp.dma_start(slot[3][:, :, 0:P], w_in[l][:, bass.ds(h * P + U0, P)].rearrange("(c p) n -> p c n", p=P)).then_inc(s_slot[3], 16)
                hold(sp, s_o, l * HEADS + HEADS + START)
                hold(sp, s_new, (l * HEADS + HEADS) * 32 + START)
                sp.dma_start(table[:, :], fourier).then_inc(s_table, 16)
                hold(sp, s_rm, l * HEADS + HEADS + START)
                hold(sp, s_um, l * HEADS + HEADS + START)
                with sp.Fori(0, ZC) as z:
                    n = l * ZC + z
                    for i in range(4):
                        hold(sp, s_part[i], n + START)
                        w, c0 = ((w_in, ZG0), (w_in, ZF0), (w_gla_out, 0), (w_four_out, 0))[i]
                        sp.dma_start(wraw[i][:, :, :], w[l][:, bass.ds(z * P + c0, P)].rearrange("(c p) n -> p c n", p=P)).then_inc(s_slot[i], 16)
                hold(sp, s_f1, (l + 1) * (2 * NT) + START)
                for chunk in range(OC):
                    i = chunk % 4
                    if chunk >= 4:
                        hold(sp, s_out, l * OC + (chunk - 3) + START)
                    elif i >= 2:
                        hold(sp, s_part[i - 2], l * ZC + ZC + START)
                    sp.dma_start(oraw[i][:, :, :], w_out[l][:, chunk * P:(chunk + 1) * P].rearrange("(c p) n -> p c n", p=P)).then_inc(s_slot[OUT_SLOTS[i]], 16)
                hold(sp, s_out, l * OC + (OC - 1) + START)
                with sp.Fori(0, PH) as h:
                    hold(sp, s_qm, l * PH + h + START)
                    sp.dma_start(slot[0][:, :, :], wcols_at(w_query, l, h * WCOLS)).then_inc(s_slot[0], 16)
                def load_u(n, g):
                    hold(sp, s_utm, l * NKEYS + n * EG + (g - EG + 1) + START)
                    sp.dma_start(usb[g][:, :], expert_u[l][bass.ds((n * EG + g) * P, P), :]).then_inc(s_u[g], 16)

                for t in range(NT):
                    if t == NT - 1:
                        hold(sp, s_wst[1], (l + 1) * (WST[1] * 16) + START)
                        for g in range(EG):
                            load_u(0, g)
                    hold(sp, s_wc, l * NWG + (t + 1) * (P // 4) + START)
                    sp.dma_start(wd[l][t], wbuf[t % 2][:, :, :]).then_inc(s_wst[t % 2], 16)
                def load_group(n, more):
                    i0 = l * NKEYS + n * EG
                    for g in range(EG):
                        b = g % 2
                        hold(sp, s_coef, i0 + g - 1 + START)
                        sp.dma_start(wex[b][:, :].rearrange("p (t n) -> p t n", n=P),
                                     wd[l][:, :, bass.ds(n * EG + g, 1), :].rearrange("t j a n -> j t (a n)")).then_inc(s_w[b], 16)
                        hold(sp, s_vl, i0 + g - 1 + START)
                        sp.dma_start(vraw[b][:, :], expert_v[l][bass.ds((n * EG + g) * P, P), :]).then_inc(s_v[b], 16)
                        if more:
                            load_u(n + 1, g)

                for i in range(2):
                    hold(sp, s_wst[i], (l + 1) * (WST[i] * 16) + START)
                with sp.Fori(0, NG - 1) as n:
                    load_group(n, True)
                load_group(NG - 1, False)
            hold(sp, s_yc, NT * 2 + START)
            sp.dma_start(y_prompt[0], ynat[:, 0, :]).then_inc(s_y, 16)
            sp.dma_start(y_sample[0].rearrange("(t p) d -> p t d", p=P), ynat[:, 1:NT, :]).then_inc(s_y, 16)
            hold(sp, s_y, 32 + START)

        @block.gpsimd
        def _(pool):
            pool.dma_start(rows0[0:8, :], c[0].rearrange("(r p) -> r p", p=P)).then_inc(s_rows, 16)
            pool.dma_start(rows0[8:16, :], c_ctx.rearrange("(r p) -> r p", p=P)).then_inc(s_rows, 16)
            pool.dma_start(rows0[16:24, :], final_norm.rearrange("(r p) -> r p", p=P)).then_inc(s_rows, 16)
            with pool.Fori(0, DEPTH) as l:
                hold(pool, s_rowsT, l * 1 + 1 + START)
                at = 0
                for w, n in ((b_mod, 48), (norm1, 8), (norm2, 8), (gla_norm, 8), (b_af, 4), (b_ab, 4)):
                    pool.dma_start(rows[at:at + n, :], w[l].rearrange("(r p) -> r p", p=P)).then_inc(s_rows, 16)
                    at += n
                hold(pool, s_x2, l * KC + START)
                hold(pool, s_xt, NT * 2 + START)
                hold(pool, s_set, 1 + START)
                pool.dma_start(wlr[:, :, :], w_in[l][:, L0:L0 + 2 * LOWRANK].rearrange("(c p) n -> p c n", p=P)).then_inc(s_wlr, 16)
                hold(pool, s_zero, l + 1 + START)
                with pool.Fori(0, HEADS) as h:
                    it = l * HEADS + h
                    hold(pool, s_gate, it + START)
                    pool.dma_start(wab[0:LOWRANK, 0, :], w_af[l][:, bass.ds(h * P, P)]).then_inc(s_wab, 16)
                    pool.dma_start(wab[LOWRANK:2 * LOWRANK, 1, :], w_ab[l][:, bass.ds(h * P, P)]).then_inc(s_wab, 16)
                    hold(pool, s_om, it * 3 + START)
                    for d in range(2):
                        pool.dma_start(hist[:, d, 3, :], state_gla[0, l, d, h]).then_inc(s_init, 16)
                hold(pool, s_x1, l * OC + OC + START)

                def load_keys(h):
                    hold(pool, s_kt, l * PH + h + START)
                    pool.dma_start(skey[:, :, :], sub_keys[l, h].rearrange("s k d -> k s d")).then_inc(s_skey, 16)

                def resolve(h, sides):
                    hold(pool, s_eq, l * PH + h + 1 + START)
                    flat = hot[:, 0:sides, :, :, :].rearrange("p s t k a -> p (s t) k a")
                    keys = tif[:, 0:sides, :, :].rearrange("p s t a -> p (s t) a")
                    nc.gpsimd.tensor_tensor(flat, flat, keys.unsqueeze(2).to_broadcast([P, sides * NT, TOPK, TOPK]), ALU.mult)
                    n = TOPK // 2
                    while n > 1:
                        pool.drain()
                        nc.gpsimd.tensor_tensor(flat[:, :, :, 0:n], flat[:, :, :, 0:n], flat[:, :, :, n:2 * n], ALU.add)
                        n //= 2
                    pool.drain()
                    nc.gpsimd.tensor_tensor(wsel[:, 1:1 + sides, :, bass.ds(h * TOPK, TOPK)], hot[:, 0:sides, :, :, 0],
                                            hot[:, 0:sides, :, :, 1],
                                            ALU.add).then_inc(s_key, 1)

                load_keys(0)
                with pool.Fori(0, PH - 1) as h:
                    load_keys(h + 1)
                    resolve(h, 2)
                resolve(PH - 1, 1)
                with pool.Fori(0, T // (2 * NB * 2)) as g2:
                    for b in range(2):
                        g = l * (T // (2 * NB)) + g2 * 2 + b
                        hold(pool, s_digit, g + 1 + START)
                        for q in range(2):
                            hold(pool, s_wm, g * 4 + (q * 2 - 2) + START)
                            digit_product(nc.gpsimd, hotB, b, 1, q).then_inc(s_hotB, 1)

        @block.tensor
        def _(pe):
            def mm(out, lhsT, rhs, first, last):
                return pe.matmul(out, lhsT, rhs, start=first, stop=last)

            def both(big, small, lhsT, rhs, first, last):
                mm(big, lhsT, rhs[:, TP:T], first, last)
                return mm(small, lhsT, rhs[:, 0:TP], first, last)

            HALF = T // 2
            halves = [slice(0, HALF), slice(HALF, T)]

            def three(bank, high, low, mov_high, mov_low, first, last_one):
                for q in range(2):
                    mm(ps[bank + q][:, 0:HALF], high, mov_high[:, halves[q]], first, False)
                for q in range(2):
                    mm(ps[bank + q][:, 0:HALF], high, mov_low[:, halves[q]], False, False)
                for q in range(2):
                    ins = mm(ps[bank + q][:, 0:HALF], low, mov_high[:, halves[q]], False, last_one)
                return ins

            def sum_squares(norm_index):
                for k in range(KC):
                    pe.wait_ge(s_sq, norm_index * KC + k + 1 + START)
                    last = both(ps[0][:, :], ps[1][:, 0:TP], ones[:, :], hT[:, k, :], k == 0, k == KC - 1)
                last.then_inc(s_ss, 1)

            pe.wait_ge(s_const, 16 + START)
            pe.wait_ge(s_rows, 48)
            pe.transpose(ps[7][:, 0:24], rows0[:, :], ident[0:24, 0:24]).then_inc(s_rowsT, 1)
            pe.wait_ge(s_x, 32 + START)
            for t in range(NT):
                for j in range(2):
                    if t * 2 + j >= 2:
                        pe.wait_ge(s_xc, t * 2 + j - 1 + START)
                    for q in range(4):
                        k = j * 4 + q
                        last = pe.transpose(ps[j][:, q * P:(q + 1) * P], xnat[:, t, k * P:(k + 1) * P], ident)
                    last.then_inc(s_xt, 1)
            pe.wait_ge(s_xc, NT * 2 + START)
            sum_squares(0)
            hold(pe, s_cond, 1 + START)

            with pe.Fori(0, DEPTH) as l:
                pe.wait_ge(s_rows, l * 96 + 48 + 96)
                pe.wait_ge(s_cols, l + 1 + START)
                pe.transpose(ps[7][:, 0:80], rows[:, :], ident[0:80, 0:80]).then_inc(s_rowsT, 1)
                pe.wait_ge(s_acc, l * (NG * KC) + START)
                hold(pe, s_cols, l + 2 + START)
                with pe.Fori(0, MOD_B) as b:
                    r0 = l * (MOD_B * SLOTS) + b * SLOTS

                    def turn_row(s):
                        if s == 0:
                            pe.wait_ge(s_modT, l * MOD_B + b + START)
                        hold(pe, s_mr, r0 + s + 1 + START)
                        for j in range(2):
                            q = 2 * s + j
                            last = pe.transpose(ps[6][:, 2 * q:2 * q + 2], mrow[s][:, j * P:(j + 1) * P], ident[0:2, 0:2])
                        if s == SLOTS - 1:
                            last.then_inc(s_mt, 1)

                    for s in range(SLOTS):
                        pe.wait_ge(s_slot[s], 16 * fills_before(s, l) + 16 * b + 16 + START)
                        pe.wait_ge(s_mr, r0 + s - 1 + START)
                        for k in range(KC):
                            last = mm(ps[4 + s % 2][0:2, 0:WCOLS], scond[:, k, :], slot[s][:, k, :], k == 0, k == KC - 1)
                        last.then_inc(s_mod, 1)
                        if s >= 1:
                            turn_row(s - 1)
                    turn_row(SLOTS - 1)
                pe.wait_ge(s_tab, 16 * l + 16 + START)
                pe.wait_ge(s_wlr, 16 * l + 16)
                for k in range(KC):
                    pe.wait_ge(s_h, l * (2 * KC) + k + 1 + START)
                    mm(ps[6][0:32, :], wlr[:, k, :], hT[:, k, TP:T], k == 0, k == KC - 1)
                    last = mm(ps[7][0:32, 0:TP], wlr[:, k, :], hT[:, k, 0:TP], k == 0, k == KC - 1)
                last.then_inc(s_lr, 1)
                def query_key(h, it):
                    pe.wait_ge(s_slot[0], 16 * (fills_before(0, l) + HEAD_FILLS) + h * 32 + 32 + START)
                    for j in range(2):
                        for k in range(KC):
                            last = both(ps[2 * j][:, :], ps[2 * j + 1][:, 0:TP], slot[0][:, k, j * P:(j + 1) * P],
                                        hT[:, k, :], k == 0, k == KC - 1)
                    last.then_inc(s_qk, 1)

                def rope_partners(it):
                    pe.wait_ge(s_q, it + 1 + START)
                    pe.wait_ge(s_k, it + 1 + START)
                    mm(ps[0][:, :], rotT, qk[:, 0, TP:T], True, True)
                    mm(ps[2][:, :], rotT, qk[:, 1, TP:T], True, True).then_inc(s_rot, 1)

                def head(h, more):
                    it = l * HEADS + h
                    pe.wait_ge(s_wab, 32 * it + 32)
                    pe.wait_ge(s_o, it + START)
                    for d in range(2):
                        last = both(ps[4 + 2 * d][:, :], ps[5 + 2 * d][:, 0:TP], wab[:, d, :], lrT[:, :], True, True)
                    last.then_inc(s_gate, 1)
                    pe.wait_ge(s_slot[1], 16 * (fills_before(1, l) + HEAD_FILLS) + 16 * h + 16 + START)
                    pe.wait_ge(s_gx, it + 1 + START)
                    for t in range(NT):
                        for k in range(KC):
                            last = mm(ps[1 + 2 * (t // 2)][:, (t % 2) * DV:(t % 2 + 1) * DV], hT[:, k, t * P:(t + 1) * P],
                                      slot[1][:, k, :], k == 0, k == KC - 1)
                    last.then_inc(s_vm, 1)
                    pe.wait_ge(s_slot[2], 16 * (fills_before(2, l) + HEAD_FILLS) + 16 * h + 16 + START)
                    for j in range(2):
                        for k in range(KC):
                            last = both(ps[4 + 2 * j][:, :], ps[7][:, j * P:(j + 1) * P], slot[2][:, k, j * P:(j + 1) * P],
                                        hT[:, k, :], k == 0, k == KC - 1)
                    last.then_inc(s_rm, 1)
                    pe.wait_ge(s_slot[3], 16 * (fills_before(3, l) + HEAD_FILLS) + 16 * h + 16 + START)
                    pe.wait_ge(s_vc, it + 1 + START)
                    for k in range(KC):
                        last = both(ps[3][:, :], ps[1][:, 0:TP], slot[3][:, k, 0:P], hT[:, k, :], k == 0, k == KC - 1)
                    last.then_inc(s_um, 1)
                    pe.wait_ge(s_uc, it + 1 + START)
                    pe.wait_ge(s_scal, it + 1 + START)
                    for d in range(2):
                        for t in range(NT):
                            dst = ps[1][:, d * P:(d + 1) * P] if t == 0 else ps[2 * d][:, (t - 1) * P:t * P]
                            last = pe.transpose(dst, dx[:, d, t * P:(t + 1) * P], ident)
                    last.then_inc(s_kdm, 1)
                    pe.wait_ge(s_r, it + 1 + START)
                    for d in range(2):
                        for t in range(NT):
                            dst = ps[5][:, d * P:(d + 1) * P] if t == 0 else ps[4 + 2 * d][:, (t - 1) * P:t * P]
                            tt = slice(t * P, (t + 1) * P)
                            last = mm(dst, e2[:, d, tt], bx[:, d, tt], True, True)
                    last.then_inc(s_am, 1)
                    pe.wait_ge(s_kd, it + 1 + START)
                    for i in range(9):
                        if i >= 2:
                            pe.wait_ge(s_st, it * 9 + i - 1 + START)
                        for d in range(2):
                            ch = step_chunk(i, d)
                            q = slice((ch % 2) * CHUNK, (ch % 2 + 1) * CHUNK)
                            last = mm(ps[STEP_BANKS[i % 2][d]][:, 0:DV], kdT[q, d, ch // 2, :], v_sb[q, ch // 2, :], True, True)
                        last.then_inc(s_ds, 1)
                    pe.wait_ge(s_a, it + 1 + START)
                    pe.wait_ge(s_st, it * 9 + 9 + START)
                    for t in range(NT):
                        bank, at = 4 + t // 2, (t % 2) * DV
                        for d in range(2):
                            pe.matmul(ps[bank][:, at:at + DV], att[:, d, t, :], v_sb[:, t, :], start=(d == 0), stop=False,
                                      skip_group_check=True)
                        for half in range(2):
                            ch = 2 * t + half
                            for d in range(2):
                                last = pe.matmul(ps[bank][half * CHUNK:(half + 1) * CHUNK, at:at + DV],
                                                 bx[:, d, ch * CHUNK:(ch + 1) * CHUNK], hist[:, d, prev_slot(ch, d), :],
                                                 start=False, stop=(d == 1), skip_group_check=True)
                        if t % 2 == 1 or t == NT - 1:
                            last.then_inc(s_om, 1)
                    if more:
                        query_key(h + 1, it + 1)
                    pe.wait_ge(s_on, it + 1 + START)
                    for j in range(2):
                        for t in range(NT):
                            dst = ps[5][:, j * P:(j + 1) * P] if t == 0 else ps[4 + 2 * j][:, (t - 1) * P:t * P]
                            last = pe.transpose(dst, on[:, t, j * P:(j + 1) * P], ident)
                    last.then_inc(s_ont, 1)
                    if more:
                        rope_partners(it + 1)

                query_key(0, l * HEADS)
                rope_partners(l * HEADS)
                hold(pe, s_lrT, l + 1 + START)
                with pe.Fori(0, HEADS - 1) as h:
                    head(h, True)
                head(HEADS - 1, False)

                pe.wait_ge(s_o, l * HEADS + HEADS + START)
                pe.wait_ge(s_uc, l * HEADS + HEADS + START)
                for t in range(NT):
                    for g in range(GROUPS):
                        i = 2 * t + g // 2
                        if g % 2 == 0 and i >= 8:
                            pe.wait_ge(s_f1c, l * (2 * NT) + i - 7 + START)
                        last = mm(ps[i % 8][:, (g % 2) * 256:(g % 2 + 1) * 256], uT[:, g, t * P:(t + 1) * P], cdsd, True, True)
                        if g % 2 == 1:
                            last.then_inc(s_f1, 1)
                pe.wait_ge(s_f1c, l * (2 * NT) + 2 * NT + START)
                pe.wait_ge(s_table, 16 * l + 16 + START)
                for g in range(GROUPS):
                    for t in range(1, NT):
                        for q in range(2):
                            at = ((t - 1) * 2 + q) * TS
                            mm(ps[2 * g][:, :], ab[:, t, g, q, :], table[:, at:at + TS], t == 1 and q == 0, t == NT - 1 and q == 1)
                    for q in range(2):
                        at = 8 * TS + q * TP
                        last = mm(ps[2 * g + 1][:, 0:TP], ab[:, 0, g, q, :], table[:, at:at + TP], q == 0, q == 1)
                last.then_inc(s_f2, 1)
                hold(pe, s_f2c, l + 1 + START)
                hold(pe, s_hms, l + 1 + START)

                with pe.Fori(0, ZC) as z:
                    n = l * ZC + z
                    for i in range(4):
                        pe.wait_ge(s_wl[i], n + 1 + START)
                        if i == 0:
                            pe.wait_ge(s_ze, n + START)
                        elif i == 2:
                            pe.wait_ge(s_mg, n + START)
                            pe.wait_ge(s_os, l + 1 + START)
                        elif i == 3:
                            pe.wait_ge(s_fs, l + 1 + START)
                        high, low = ((hmH, hL), (hmH, hL), (oH, oL), (fourH, fourL))[i]
                        depth = GROUPS if i == 3 else KC
                        for k in range(depth):
                            last = three(2 * i, wH[i][:, k, :], wL[i][:, k, :], high[:, k, :], low[:, k, :], k == 0, k == depth - 1)
                        last.then_inc(s_part[i], 1)
                for chunk in range(OC):
                    i = chunk % 4
                    pe.wait_ge(s_owl, l * OC + chunk + 1 + START)
                    if chunk >= 4:
                        pe.wait_ge(s_x1, l * OC + (chunk - 3) + START)
                    for k in range(KC):
                        if chunk == 0 and k == 0:
                            pe.wait_ge(s_ze, l * ZC + ZC + START)
                            pe.wait_ge(s_ms, l * 2 + 1 + START)
                        if chunk == 0 and k == KC - 1:
                            pe.wait_ge(s_ms, l * 2 + 2 + START)
                        last = three(2 * i, owH[i][:, k, :], owL[i][:, k, :], mH[:, k, :], mL[:, k, :], k == 0, k == KC - 1)
                    last.then_inc(s_out, 1)
                pe.wait_ge(s_x1, l * OC + OC + START)
                sum_squares(2 * l + 1)

                def queries(h, it, first=False):
                    pe.wait_ge(s_slot[0], 16 * (fills_before(0, l) + QUERY_FILLS) + 16 * h + 16 + START)
                    pe.wait_ge(s_qc, it + START)
                    for j in range(2):
                        for k in range(KC):
                            if first and j == 0:
                                pe.wait_ge(s_h, l * (2 * KC) + KC + k + 1 + START)
                            last = both(ps[2 * j][:, :], ps[2 * j + 1][:, 0:TP], slot[0][:, k, j * P:(j + 1) * P],
                                        hT[:, k, :], k == 0, k == KC - 1)
                    last.then_inc(s_qm, 1)
                    pe.wait_ge(s_skey, 16 * it + 16)
                    pe.wait_ge(s_ktc, it + START)
                    for j in range(2):
                        last = pe.transpose(ps[7][:, j * P:(j + 1) * P], skey[:, j, :], ident)
                    last.then_inc(s_kt, 1)

                def scores(it):
                    pe.wait_ge(s_ktc, it + 1 + START)
                    pe.wait_ge(s_qc, it + 1 + START)
                    pe.wait_ge(s_sc, it + START)
                    for t in range(NT):
                        for j in range(2):
                            at = (t % 2) * 256 + j * P
                            last = mm(ps[4 + t // 2][:, at:at + P], qryT[:, j, t * P:(t + 1) * P], skT[:, j, :], True, True)
                    last.then_inc(s_sm, 1)

                queries(0, l * PH, first=True)
                with pe.Fori(0, PH - 1) as h:
                    scores(l * PH + h)
                    queries(h + 1, l * PH + h + 1)
                scores(l * PH + PH - 1)
                pe.wait_ge(s_sc, l * PH + PH + START)
                pe.wait_ge(s_sel, l * PH + PH + START)
                pe.wait_ge(s_key, l * PH + PH + START)
                for a in range(3):
                    for t in range(NT):
                        dst = ps[3][:, a * P:(a + 1) * P] if t == NT - 1 else ps[a][:, t * P:(t + 1) * P]
                        last = pe.transpose(dst, wsel[:, a, t, :], ident)
                last.then_inc(s_tm, 1)
                hold(pe, s_tc, l + 1 + START)
                with pe.Fori(0, NWG // 4) as g:
                    for b in range(4):
                        n = l * NWG + g * 4 + b
                        if b % 2 == 0:
                            pe.wait_ge(s_hotA, l * (T // NB) + g * 2 + b // 2 + 1 + START)
                            pe.wait_ge(s_hotB, l * (T // NB) + g * 2 + b // 2 + 1 + START)
                        pe.wait_ge(s_wc, n - 3 + START)
                        for q in range(4):
                            at = b // 2, (b % 2) * 4 + q
                            last = mm(ps[4 + b][:, q * P:(q + 1) * P], hotB[:, at[0], at[1], :], hotA[:, at[0], at[1], :], True, True)
                        last.then_inc(s_wm, 1)

                def turn(n, g):
                    i = l * NKEYS + n * EG + g
                    pe.wait_ge(s_u[g], 16 * (l * NG + n + 1) + START)
                    pe.wait_ge(s_ul, i + START)
                    for k in range(KC):
                        last = pe.transpose(ps[k // 4][:, (k % 4) * P:(k % 4 + 1) * P], usb[g][:, k * P:(k + 1) * P], ident)
                    last.then_inc(s_utm, 1)

                def group(n, more):
                    i0 = l * NKEYS + n * EG
                    k0 = (l * NG + n) * KC
                    for g in range(EG):
                        if g + 1 < EG:
                            turn(n, g + 1)
                        pe.wait_ge(s_ul, i0 + g + 1 + START)
                        if g == 1:
                            pe.wait_ge(s_acc, k0 - 1 + START)
                        if g >= 1:
                            pe.wait_ge(s_gel, i0 + g - 1 + START)
                        for k in range(KC):
                            if g == 0 and k % (KC // 2) == 0:
                                pe.wait_ge(s_hs, l * 2 + k // (KC // 2) + 1 + START)
                            last = three(2 + 2 * (g % 2), uH[g % 2][:, k, :], uL[g % 2][:, k, :], hH[:, k, :], hL[:, k, :],
                                         k == 0, k == KC - 1)
                        last.then_inc(s_um2, 1)
                    def out_part(k, g):
                        kk = slice(k * P, (k + 1) * P)
                        return three(OUT_BANKS[k], vH[g][:, kk], vL[g][:, kk], cH[g][:, :], cL[g][:, :],
                                     g == 0, g == EG - 1)

                    for k in range(2):
                        if k == 0:
                            pe.wait_ge(s_acc, k0 + START)
                        else:
                            pe.wait_ge(s_gel, i0 + EG - 1 + START)
                        for g in range(EG - 1):
                            if k == 0:
                                pe.wait_ge(s_vl, i0 + g + 1 + START)
                                pe.wait_ge(s_coef, i0 + g + 1 + START)
                            out_part(k, g)
                    if more:
                        turn(n + 1, 0)
                    pe.wait_ge(s_vl, i0 + EG + START)
                    pe.wait_ge(s_coef, i0 + EG + START)
                    for k in range(2):
                        out_part(k, EG - 1).then_inc(s_vm2, 1)
                    for k in range(2, KC):
                        if k > 2:
                            pe.wait_ge(s_acc, k0 + (1 if k == 3 else k - 1) + START)
                        for g in range(EG):
                            last = out_part(k, g)
                        last.then_inc(s_vm2, 1)

                turn(0, 0)
                with pe.Fori(0, NG - 1) as n:
                    group(n, True)
                group(NG - 1, False)
                sum_squares(2 * l + 2)
            pe.wait_ge(s_h, (2 * DEPTH + 1) * KC + START)
            for t in range(NT):
                for j in range(2):
                    i = t * 2 + j
                    if i >= 2:
                        pe.wait_ge(s_yc, i - 1 + START)
                    for q in range(4):
                        k = j * 4 + q
                        last = pe.transpose(ps[4 + j][:, q * P:(q + 1) * P], hT[:, k, t * P:(t + 1) * P], ident)
                    last.then_inc(s_yt, 1)

        @block.scalar
        def _(act):
            def af(out, in_, fn, **kw):
                return nc.scalar.activation(out, in_, fn, **kw)

            def rstd(before):
                act.wait_ge(s_ss, before + 1 + START)
                af(rs[:, TP:T], ps[0][:, :], ACT.Ln, bias=eps[:, :], scale=1.0 / D)
                af(rs[:, 0:TP], ps[1][:, 0:TP], ACT.Ln, bias=eps[:, :], scale=1.0 / D)
                act.drain()
                af(rs[:, :], rs[:, :], ACT.Exp, scale=-0.5).then_inc(s_rs, 1)

            def squares(before, chunk_ready=None, after_chunk=None):
                for k in range(KC):
                    if chunk_ready is not None:
                        act.wait_ge(chunk_ready[0], chunk_ready[1] + k + 1 + START)
                    af(hT[:, k, :], xT[:, k, :], ACT.Square).then_inc(s_sq, 1)
                    if after_chunk is not None:
                        after_chunk(k)
                rstd(before)

            act.wait_ge(s_set, 1 + START)
            act.wait_ge(s_cols, 1 + START)
            af(scond[:, :, 0], cols0[:, 8:16], ACT.Exp, scale=-1.0)
            af(scond[:, :, 1], cols0[:, 0:8], ACT.Exp, scale=-1.0).then_inc(s_econd, 1)
            act.wait_ge(s_xc, NT * 2 + START)
            squares(0)

            with act.Fori(0, DEPTH) as l:
                with act.Fori(0, MOD_B) as b:
                    for s in range(SLOTS):
                        act.wait_ge(s_mod, l * (MOD_B * SLOTS) + b * SLOTS + s + 1 + START)
                        act.wait_ge(s_mt, l * MOD_B + b + START)
                        af(mrow[s][:, :], ps[4 + s % 2][0:2, 0:WCOLS], ACT.Copy).then_inc(s_mr, 1)
                act.wait_ge(s_lr, l + 1 + START)
                af(lrT[:, TP:T], ps[6][0:32, :], ACT.Copy)
                af(lrT[:, 0:TP], ps[7][0:32, 0:TP], ACT.Copy).then_inc(s_lrT, 1)

                def copy_query(it):
                    act.wait_ge(s_qk, it + 1 + START)
                    af(qk[:, 0, TP:T], ps[0][:, :], ACT.Copy, scale=float(P) ** -0.5)
                    af(qk[:, 0, 0:TP], ps[1][:, 0:TP], ACT.Copy, scale=float(P) ** -0.5).then_inc(s_q, 1)

                def head(h, more):
                    it = l * HEADS + h
                    act.wait_ge(s_gx, it + 1 + START)
                    af(tmp[:, :, :], gx[:, :, :], ACT.Abs)
                    act.drain()
                    af(tmp[:, :, :], tmp[:, :, :], ACT.Exp, scale=-1.0)
                    act.drain()
                    af(tmp[:, :, :], tmp[:, :, :], ACT.Ln, bias=one[:, :]).then_inc(s_gl, 1)
                    act.wait_ge(s_vm, it + 1 + START)
                    af(v_sb[:, 0:2, :], ps[1][:, :], ACT.Copy)
                    af(v_sb[:, 2:4, :], ps[3][:, :], ACT.Copy)
                    af(v_sb[:, 4, :], ps[5][:, 0:DV], ACT.Copy).then_inc(s_vc, 1)
                    act.wait_ge(s_ex, it + 1 + START)
                    af(e2[:, :, :], bx[:, :, :], ACT.Exp, scale=-1.0 / TAU)
                    act.drain()
                    af(bx[:, :, :], bx[:, :, :], ACT.Exp, scale=1.0 / TAU)
                    af(dx[:, :, :], dx[:, :, :], ACT.Exp, scale=1.0 / TAU)
                    af(dec[:, :, :], tot[:, :, :], ACT.Exp, scale=1.0 / TAU).then_inc(s_dec, 1)
                    act.wait_ge(s_rm, it + 1 + START)
                    rr = on[:, :, :].rearrange("p t e -> p (t e)")
                    for at, bank, n in ((0, ps[4], TS), (TS, ps[6], TS), (2 * TS, ps[7], 2 * TP)):
                        af(rr[:, at:at + n], bank[:, 0:n], ACT.Exp, scale=-1.0)
                    act.drain()
                    af(rr, rr, ACT.Ln, bias=one[:, :])
                    act.drain()
                    af(rr, rr, ACT.Exp, scale=-1.0).then_inc(s_re, 1)
                    act.wait_ge(s_um, it + 1 + START)
                    us = uT[:, bass.ds(h, 1), :].rearrange("p a n -> p (a n)")
                    af(us[:, TP:T], ps[3][:, :], ACT.Copy)
                    af(us[:, 0:TP], ps[1][:, 0:TP], ACT.Copy).then_inc(s_uc, 1)
                    act.wait_ge(s_kdm, it + 1 + START)
                    af(kdT[:, 0, 1:NT, :], ps[0][:, :], ACT.Copy)
                    af(kdT[:, 1, 1:NT, :], ps[2][:, :], ACT.Copy)
                    af(kdT[:, :, 0, :], ps[1][:, 0:2 * P], ACT.Copy).then_inc(s_kd, 1)
                    hold(act, s_st, it * 9 + 2 + START)
                    for d in range(2):
                        act.dma_start(new_state[0, l, d, h], hist[:, d, 2, :]).then_inc(s_new, 16)
                    for t in range(NT):
                        if t % 2 == 0:
                            act.wait_ge(s_om, it * 3 + t // 2 + 1 + START)
                        af(on[:, t, :], ps[4 + t // 2][:, (t % 2) * DV:(t % 2 + 1) * DV], ACT.Square, accum_out=oss[:, t:t + 1])
                    act.drain()
                    af(ors[:, 0:NT], oss[:, 0:NT], ACT.Ln, bias=eps[:, :], scale=1.0 / DV)
                    act.drain()
                    af(ors[:, 0:NT], ors[:, 0:NT], ACT.Exp, scale=-0.5)
                    act.drain()
                    for t in range(NT):
                        last = af(on[:, t, :], ps[4 + t // 2][:, (t % 2) * DV:(t % 2 + 1) * DV], ACT.Copy, scale=ors[:, t:t + 1])
                    last.then_inc(s_on, 1)
                    if more:
                        copy_query(it + 1)

                copy_query(l * HEADS)
                with act.Fori(0, HEADS - 1) as h:
                    head(h, True)
                head(HEADS - 1, False)

                for i in range(2 * NT):
                    act.wait_ge(s_f1, l * (2 * NT) + i + 1 + START)
                    af(ab[:, i // 2, 2 * (i % 2):2 * (i % 2) + 2, :, :], ps[i % 8][:, :], ACT.Copy).then_inc(s_f1c, 1)
                act.wait_ge(s_f2, l + 1 + START)
                for g in range(GROUPS):
                    af(fourT[:, g, TP:T], ps[2 * g][:, :], ACT.Copy)
                    last = af(fourT[:, g, 0:TP], ps[2 * g + 1][:, 0:TP], ACT.Copy)
                last.then_inc(s_f2c, 1)
                def high_part(z, i):
                    act.wait_ge(s_slot[i], 16 * (fills_before(i, l) + MERGE_FILLS[i] + 1) + 16 * z + START)
                    af(wH[i][:, :, :], wraw[i][:, :, :], ACT.Copy).then_inc(s_wh[i], 1)

                def gates(z, more):
                    n = l * ZC + z
                    for i in (2, 3):
                        high_part(z, i)
                    act.wait_ge(s_zm, n + 1 + START)
                    act.wait_ge(s_mg, n + START)
                    for a in range(2):
                        for q in range(2):
                            last = af(sg[a][:, q * (T // 2):(q + 1) * (T // 2)], ps[2 * a + q][:, 0:T // 2], ACT.Exp, scale=-1.0)
                    last.then_inc(s_ze, 1)
                    if more:
                        for i in (0, 1):
                            high_part(z + 1, i)
                    act.drain()
                    for a in range(2):
                        af(sg[a][:, :], sg[a][:, :], ACT.Ln, bias=one[:, :])
                    act.drain()
                    for a in range(2):
                        last = af(sg[a][:, :], sg[a][:, :], ACT.Exp, scale=-1.0)
                    last.then_inc(s_sg, 1)

                for i in (0, 1):
                    high_part(0, i)
                with act.Fori(0, ZC - 1) as z:
                    gates(z, True)
                gates(ZC - 1, False)

                def high_out(chunk):
                    if chunk < OC:
                        i = chunk % 4
                        act.wait_ge(s_slot[OUT_SLOTS[i]], 16 * (fills_before(OUT_SLOTS[i], l) + OUT_FILLS[i] + chunk // 4 + 1) + START)
                        af(owH[i][:, :, :], oraw[i][:, :, :], ACT.Copy).then_inc(s_owh, 1)

                for chunk in range(4):
                    high_out(chunk)
                squares(2 * l + 1, (s_x1, l * OC), lambda k: high_out(k + 4))

                def query_copies(it):
                    act.wait_ge(s_qm, it + 1 + START)
                    act.wait_ge(s_sm, it + START)
                    for j in range(2):
                        af(qryT[:, j, TP:T], ps[2 * j][:, :], ACT.Copy)
                        last = af(qryT[:, j, 0:TP], ps[2 * j + 1][:, 0:TP], ACT.Copy)
                    last.then_inc(s_qc, 1)
                    act.wait_ge(s_kt, it + 1 + START)
                    af(skT[:, :, :], ps[7][:, 0:2 * P], ACT.Copy).then_inc(s_ktc, 1)

                def select_head(it, more):
                    act.wait_ge(s_sm, it + 1 + START)
                    act.wait_ge(s_scf, it + START)
                    af(sc[:, 0:2, :, :], ps[4][:, :], ACT.Copy)
                    af(sc[:, 2:4, :, :], ps[5][:, :], ACT.Copy)
                    af(sc[:, 4, :, :], ps[6][:, 0:2 * P], ACT.Copy).then_inc(s_sc, 1)
                    if more:
                        query_copies(it + 1)
                    act.wait_ge(s_d, it + 1 + START)
                    af(best[:, :, :], best[:, :, :], ACT.Exp).then_inc(s_e, 1)

                query_copies(l * PH)
                with act.Fori(0, PH - 1) as h:
                    select_head(l * PH + h, True)
                select_head(l * PH + PH - 1, False)
                act.wait_ge(s_tm, l + 1 + START)
                for a in range(3):
                    af(wselT[:, a, 0:TS], ps[a][:, :], ACT.Copy)
                    last = af(wselT[:, a, TS:T], ps[3][:, a * P:(a + 1) * P], ACT.Copy)
                last.then_inc(s_tc, 1)
                for t in range(NT):
                    if t >= 2:
                        hold(act, s_wst[t % 2], l * (WST[t % 2] * 16) + (t // 2) * 16 + START)
                    with act.Fori(0, P // 16) as g:
                        for b in range(4):
                            act.wait_ge(s_wm, l * NWG + t * (P // 4) + g * 4 + b + 1 + START)
                            af(wbuf[t % 2][:, :, bass.ds(g * 16 + b * 4, 4)].rearrange("p i n -> p n i"),
                               ps[4 + b][:, :].rearrange("p (n i) -> p n i", n=4), ACT.Copy).then_inc(s_wc, 1)

                hold(act, s_wst[1], (l + 1) * (WST[1] * 16) + START)
                def high_u(i, b):
                    act.wait_ge(s_utm, i + 1 + START)
                    act.wait_ge(s_um2, i - 1 + START)
                    af(uH[b][:, 0:4, :], ps[0][:, :], ACT.Copy)
                    af(uH[b][:, 4:8, :], ps[1][:, :], ACT.Copy).then_inc(s_utc, 1)

                def group(n, more):
                    i0 = l * NKEYS + n * EG
                    for g in range(EG):
                        if g + 1 < EG:
                            high_u(i0 + g + 1, (g + 1) % 2)
                        act.wait_ge(s_um2, i0 + g + 1 + START)
                        act.wait_ge(s_coef, i0 + g - 1 + START)
                        b = 2 + 2 * (g % 2)
                        af(gel[g % 2][:, 0:T // 2], ps[b][:, 0:T // 2], ACT.Gelu_apprx_tanh)
                        af(gel[g % 2][:, T // 2:T], ps[b + 1][:, 0:T // 2], ACT.Gelu_apprx_tanh).then_inc(s_gel, 1)
                        act.wait_ge(s_v[g % 2], 16 * (l * (NKEYS // 2) + n * (EG // 2) + g // 2 + 1) + START)
                        if g == 0:
                            act.wait_ge(s_vm2, (l * NG + n) * KC + START)
                        af(vH[g][:, :], vraw[g % 2][:, :], ACT.Copy).then_inc(s_vh, 1)
                    if more:
                        high_u(i0 + EG, 0)

                high_u(l * NKEYS, 0)
                with act.Fori(0, NG - 1) as n:
                    group(n, True)
                group(NG - 1, False)
                squares(2 * l + 2, (s_x2, l * KC))
            act.wait_ge(s_new, DEPTH * HEADS * 2 * 16 + START)

        @block.vector
        def _(dve):
            v = nc.vector
            tt, ts, stt = v.tensor_tensor, v.tensor_scalar, v.scalar_tensor_tensor

            def normalise(which):
                for k in which:
                    tt(hT[:, k, :], xT[:, k, :], rs[:, :], ALU.mult)

            def modulate(which, scale_of, shift_of):
                for k in which:
                    for q, columns in ((0, slice(0, TP)), (1, slice(TP, T))):
                        a, b = scale_of(k, q), shift_of(k, q)
                        if b is None:
                            last = ts(hT[:, k, columns], hT[:, k, columns], a, None, ALU.mult)
                        else:
                            last = ts(hT[:, k, columns], hT[:, k, columns], a, b, ALU.mult, ALU.add)
                    last.then_inc(s_h, 1)

            def norm(before, scale_of, shift_of):
                dve.wait_ge(s_rs, before + 1 + START)
                for first in (0, KC // 2):
                    part = range(first, first + KC // 2)
                    normalise(part)
                    dve.drain()
                    modulate(part, scale_of, shift_of)

            v.memset(ones[:, :], 1.0)
            v.memset(eps[:, :], EPS)
            v.memset(one[:, :], 1.0).then_inc(s_set, 1)
            for i in range(2 * NT):
                dve.wait_ge(s_xt, i + 1 + START)
                t, j = i // 2, i % 2
                v.tensor_copy(xT[:, 4 * j:4 * j + 4, t * P:(t + 1) * P], ps[j][:, :].rearrange("p (a n) -> p a n", a=4)).then_inc(s_xc, 1)
            dve.wait_ge(s_rowsT, 1 + START)
            v.tensor_copy(cols0[:, :], ps[7][:, 0:24]).then_inc(s_cols, 1)
            dve.wait_ge(s_econd, 1 + START)
            ts(scond[:, :, :], scond[:, :, :], 1.0, None, ALU.add)
            dve.drain()
            v.reciprocal(scond[:, :, :], scond[:, :, :])
            dve.drain()
            tt(scond[:, :, 0], scond[:, :, 0], cols0[:, 8:16], ALU.mult)
            tt(scond[:, :, 1], scond[:, :, 1], cols0[:, 0:8], ALU.mult).then_inc(s_cond, 1)

            with dve.Fori(0, DEPTH) as l:
                dve.wait_ge(s_rowsT, l + 2 + START)
                v.tensor_copy(cols[:, :], ps[7][:, 0:80]).then_inc(s_cols, 1)
                v.memset(att[:, :, :, :], 0.0)
                v.memset(hist[:, :, 0, :], 0.0)
                v.memset(wab[:, :, :], 0.0)
                dve.drain()
                v.memset(tot[:, :, :], 0.0).then_inc(s_zero, 1)
                dve.wait_ge(s_rs, 2 * l + 1 + START)
                normalise(range(KC))
                with dve.Fori(0, MOD_B) as b:
                    dve.wait_ge(s_mt, l * MOD_B + b + 1 + START)
                    tt(modT[:, bass.ds(b * (2 * SLOTS), 2 * SLOTS), :], ps[6][:, 0:4 * SLOTS].rearrange("p (n q) -> p n q", q=2),
                       cols[:, bass.ds(b * (2 * SLOTS), 2 * SLOTS)].unsqueeze(2).to_broadcast([P, 2 * SLOTS, 2]),
                       ALU.add).then_inc(s_modT, 1)
                dve.drain()
                dve.wait_ge(s_tab, 16 * l + 16 + START)
                for a in range(2):
                    stt(nscale[:, a, :, :], modT[:, 8 + 24 * a:16 + 24 * a, :], 1.0,
                        cols[:, 48 + 8 * a:56 + 8 * a].unsqueeze(2).to_broadcast([P, KC, 2]), ALU.add, ALU.mult)
                dve.drain()
                modulate(range(KC), lambda k, q: nscale[:, 0, k, q:q + 1], lambda k, q: modT[:, k, q:q + 1])

                def copy_key(it):
                    dve.wait_ge(s_qk, it + 1 + START)
                    v.tensor_copy(qk[:, 1, TP:T], ps[2][:, :])
                    v.tensor_copy(qk[:, 1, 0:TP], ps[3][:, 0:TP]).then_inc(s_k, 1)

                def head(h, more):
                    it = l * HEADS + h
                    dve.wait_ge(s_gate, it + 1 + START)
                    for d in range(2):
                        bias = cols[:, bass.ds(h + (72 + 4 * d), 1)]
                        ts(gx[:, d, TP:T], ps[4 + 2 * d][:, :], bias, None, ALU.add)
                        last = ts(gx[:, d, 0:TP], ps[5 + 2 * d][:, 0:TP], bias, None, ALU.add)
                    last.then_inc(s_gx, 1)
                    dve.wait_ge(s_rot, it + 1 + START)
                    for a in range(2):
                        tt(qk[:, a, TP:T], qk[:, a, TP:T], cos, ALU.mult)
                        tt(e2[:, a, TP:T], ps[2 * a][:, :], sin, ALU.mult)
                    dve.drain()
                    for a in range(2):
                        tt(qk[:, a, TP:T], qk[:, a, TP:T], e2[:, a, TP:T], ALU.add)
                    dve.wait_ge(s_gl, it + 1 + START)
                    stt(gx[:, :, :], gx[:, :, :], 0.0, tmp[:, :, :], ALU.min, ALU.subtract)
                    dve.drain()
                    v.tensor_tensor_scan(bx[:, 0, :], reset, gx[:, 0, :], 0.0, ALU.mult, ALU.add)
                    v.tensor_tensor_scan(tmp[:, 0, :], reset, gx[:, 1, :], 0.0, ALU.mult, ALU.add)
                    dve.drain()
                    chunks = lambda ap: ap.rearrange("p (n c) -> p n c", c=CHUNK)
                    v.tensor_copy(tot[:, 0, :], chunks(bx[:, 0, :])[:, :, CHUNK - 1])
                    v.tensor_copy(tot[:, 1, :], chunks(tmp[:, 0, :])[:, :, CHUNK - 1])
                    dve.drain()
                    spread = lambda d: tot[:, d, :].unsqueeze(2).to_broadcast([P, NCH, CHUNK])
                    tt(chunks(dx[:, 0, :]), spread(0), chunks(bx[:, 0, :]), ALU.subtract)
                    tt(chunks(tmp[:, 1, :]), spread(1), chunks(tmp[:, 0, :]), ALU.subtract)
                    tt(dx[:, 1, :], tmp[:, 0, :], gx[:, 1, :], ALU.subtract)
                    dve.drain()
                    tt(bx[:, 1, :], tmp[:, 1, :], gx[:, 1, :], ALU.add).then_inc(s_ex, 1)
                    dve.wait_ge(s_dec, it + 1 + START)
                    qb = qk[:, 0, :].unsqueeze(1).to_broadcast([P, 2, T])
                    kb = qk[:, 1, :].unsqueeze(1).to_broadcast([P, 2, T])
                    tt(dx[:, :, :], dx[:, :, :], kb, ALU.mult)
                    tt(e2[:, :, :], e2[:, :, :], kb, ALU.mult)
                    tt(bx[:, :, :], bx[:, :, :], qb, ALU.mult).then_inc(s_scal, 1)
                    rr = on[:, :, :].rearrange("p t e -> p (t e)")
                    dve.wait_ge(s_re, it + 1 + START)
                    tt(rsil[:, 0, TP:T], ps[4][:, :], rr[:, 0:TS], ALU.mult)
                    tt(rsil[:, 1, TP:T], ps[6][:, :], rr[:, TS:2 * TS], ALU.mult)
                    tt(rsil[:, :, 0:TP], ps[7][:, 0:2 * TP].rearrange("p (j n) -> p j n", j=2),
                       rr[:, 2 * TS:2 * TS + 2 * TP].rearrange("p (j n) -> p j n", j=2), ALU.mult).then_inc(s_r, 1)
                    hold(dve, s_am, it + 1 + START)
                    for d in range(2):
                        v.copy_predicated(att[:, d, 1:NT, :], mask[d].unsqueeze(1).to_broadcast([P, 4, P]),
                                          ps[4 + 2 * d][:, :].rearrange("p (t n) -> p t n", n=P))
                    for d in range(2):
                        last = v.copy_predicated(att[:, d, 0, :], mask[d], ps[5][:, d * P:(d + 1) * P])
                    last.then_inc(s_a, 1)
                    dve.wait_ge(s_init, 32 * it + 32)
                    dve.wait_ge(s_new, 32 * it + START)
                    for i in range(9):
                        dve.wait_ge(s_ds, it * 9 + i + 1 + START)
                        src = i if i < 2 else i + 1
                        for d in range(2):
                            ch = step_chunk(i, d)
                            last = stt(hist[:, d, src + 1, :], hist[:, d, src, :], dec[:, d, ch:ch + 1],
                                       ps[STEP_BANKS[i % 2][d]][:, 0:DV], ALU.mult, ALU.add)
                        last.then_inc(s_st, 1)
                        dve.drain()
                    if more:
                        copy_key(it + 1)
                    dve.wait_ge(s_ont, it + 1 + START)
                    for j in range(2):
                        gn = cols[:, bass.ds(h * 2 + (64 + j), 1)]
                        dst = oT[:, bass.ds(h * 2 + j, 1), :].rearrange("p a n -> p (a n)")
                        stt(dst[:, TP:T], ps[4 + 2 * j][:, :], gn, rsil[:, j, TP:T], ALU.mult, ALU.mult)
                        last = stt(dst[:, 0:TP], ps[5][:, j * P:(j + 1) * P], gn, rsil[:, j, 0:TP], ALU.mult, ALU.mult)
                    last.then_inc(s_o, 1)

                copy_key(l * HEADS)
                with dve.Fori(0, HEADS - 1) as h:
                    head(h, True)
                head(HEADS - 1, False)

                def split(high, low, whole):
                    v.tensor_copy(high[:, :, :], whole[:, :, :])
                    dve.drain()
                    return tt(low[:, :, :], whole[:, :, :], high[:, :, :].bitcast(F32), ALU.subtract)

                dve.drain()
                dve.wait_ge(s_new, (l * HEADS + HEADS) * 32 + START)
                dve.wait_ge(s_um, l * HEADS + HEADS + START)
                split(hmH, hL, hT).then_inc(s_hms, 1)

                def low_part(z, i):
                    dve.wait_ge(s_wh[i], l * ZC + z + 1 + START)
                    tt(wL[i][:, :, :], wraw[i][:, :, :], wH[i][:, :, :].bitcast(F32), ALU.subtract).then_inc(s_wl[i], 1)

                def low_out(chunk):
                    i = chunk % 4
                    dve.wait_ge(s_owh, l * OC + chunk + 1 + START)
                    tt(owL[i][:, :, :], oraw[i][:, :, :], owH[i][:, :, :].bitcast(F32), ALU.subtract).then_inc(s_owl, 1)

                def merge(z, more):
                    n = l * ZC + z
                    for i in (2, 3):
                        low_part(z, i)
                    if more:
                        for i in (0, 1):
                            low_part(z + 1, i)
                    else:
                        for chunk in range(2):
                            low_out(chunk)
                        dve.wait_ge(s_zm, l * ZC + ZC + START)
                        v.tensor_copy(mH[:, 0:KC - 1, :], mT[:, 0:KC - 1, :])
                        dve.drain()
                        tt(mL[:, 0:KC - 1, :], mT[:, 0:KC - 1, :], mH[:, 0:KC - 1, :].bitcast(F32), ALU.subtract).then_inc(s_ms, 1)
                    dve.wait_ge(s_sg, n + 1 + START)
                    dve.wait_ge(s_ym, n + 1 + START)
                    for a in range(2):
                        for q in range(2):
                            half = slice(q * (T // 2), (q + 1) * (T // 2))
                            tt(sg[a][:, half], sg[a][:, half], ps[4 + 2 * a + q][:, 0:T // 2], ALU.mult)
                    dve.drain()
                    tt(mT[:, bass.ds(z, 1), :].rearrange("p a n -> p (a n)"), sg[0][:, :], sg[1][:, :], ALU.add).then_inc(s_mg, 1)

                for i in (0, 1):
                    low_part(0, i)
                dve.wait_ge(s_f2, l + 1 + START)
                split(oH, oL, oT).then_inc(s_os, 1)
                dve.wait_ge(s_f2c, l + 1 + START)
                split(fourH, fourL, fourT).then_inc(s_fs, 1)
                with dve.Fori(0, ZC - 1) as z:
                    merge(z, True)
                merge(ZC - 1, False)
                dve.drain()
                v.tensor_copy(mH[:, KC - 1, :], mT[:, KC - 1, :])
                dve.drain()
                tt(mL[:, KC - 1, :], mT[:, KC - 1, :], mH[:, KC - 1, :].bitcast(F32), ALU.subtract).then_inc(s_ms, 1)
                for chunk in range(2, 4):
                    low_out(chunk)
                for chunk in range(OC):
                    dve.wait_ge(s_out, l * OC + chunk + 1 + START)
                    bank = 2 * (chunk % 4)
                    for a, lo, hi in ((0, 0, TP), (1, TP, T // 2), (1, T // 2, T)):
                        part = ps[bank][:, lo:hi] if hi <= T // 2 else ps[bank + 1][:, 0:T // 2]
                        last = stt(xT[:, chunk, lo:hi], part, modT[:, 16 + chunk, a:a + 1], xT[:, chunk, lo:hi], ALU.mult, ALU.add)
                    last.then_inc(s_x1, 1)
                    if 1 <= chunk <= 4:
                        low_out(chunk + 3)
                norm(2 * l + 1, lambda k, q: nscale[:, 1, k, q:q + 1], lambda k, q: modT[:, 24 + k, q:q + 1])

                def choose(h, more):
                    it = l * PH + h
                    hold(dve, s_sc, it + 1 + START)
                    lists = [(t, s) for t in range(NT) for s in range(2)]
                    for rank in range(2):
                        r8 = slice(8 * rank, 8 * rank + 8)
                        for t, s in lists:
                            v.max(top[:, t, s, r8], sc[:, t, s, :])
                        dve.drain()
                        for t, s in lists:
                            last = v.max_index(ti[:, t, s, r8], top[:, t, s, r8], sc[:, t, s, :])
                        if rank == 1:
                            last.then_inc(s_scf, 1)
                        dve.drain()
                        if rank == 0:
                            for t, s in lists:
                                v.match_replace(sc[:, t, s, :], top[:, t, s, r8], sc[:, t, s, :], LOWEST)
                            dve.drain()
                    for c0, a0, na, nb in ((0, 0, WIDE, TOPK), (NWIDE, WIDE, TOPK - WIDE, NARROW)):
                        tt(cand[:, :, c0:c0 + na * nb].rearrange("p t (a b) -> p t a b", b=nb),
                           top[:, :, 0, a0:a0 + na].unsqueeze(3).to_broadcast([P, NT, na, nb]),
                           top[:, :, 1, 0:nb].unsqueeze(2).to_broadcast([P, NT, na, nb]), ALU.add)
                    dve.drain()
                    for rank in range(2):
                        r8 = slice(8 * rank, 8 * rank + 8)
                        for t in range(NT):
                            v.max(best[:, t, r8], cand[:, t, :])
                        dve.drain()
                        for t in range(NT):
                            v.max_index(sel[:, t, r8], best[:, t, r8], cand[:, t, :])
                        dve.drain()
                        if rank == 0:
                            for t in range(NT):
                                v.match_replace(cand[:, t, :], best[:, t, r8], cand[:, t, :], LOWEST)
                            dve.drain()
                    v.tensor_copy(bsum[:, :], best[:, :, 0])
                    for i, (bits, op) in enumerate(((4, ALU.logical_shift_right), (TOPK - 1, ALU.bitwise_and),
                                                    (2, ALU.logical_shift_right), (NARROW - 1, ALU.bitwise_and))):
                        ts(parts_int[:, i, :, :], sel[:, :, :], bits, None, op)
                    v.tensor_copy(place_no[:, :, :], sel[:, :, :])
                    dve.drain()
                    tt(best[:, :, :], best[:, :, :], bsum[:, :].unsqueeze(2).to_broadcast([P, NT, TOPK]), ALU.subtract).then_inc(s_d, 1)
                    v.tensor_copy(parts[:, :, :, :], parts_int[:, :, :, :])
                    dve.wait_ge(s_key, it + START)
                    v.tensor_copy(tif[:, :, :, :], ti[:, :, :, :].rearrange("p t s k -> p s t k"))
                    dve.drain()
                    stt(step[:, 0, :, :], parts[:, 2, :, :], float(NWIDE // NARROW - WIDE), parts[:, 0, :, :], ALU.subtract, ALU.subtract)
                    tt(step[:, 1, :, :], parts[:, 3, :, :], parts[:, 1, :, :], ALU.subtract)
                    dve.drain()
                    for s in range(2):
                        stt(step[:, s, :, :], place_no[:, :, :], float(NWIDE), step[:, s, :, :], ALU.is_ge, ALU.mult)
                    dve.drain()
                    tt(rank_ab[:, :, :, :], parts[:, 0:2, :, :], step[:, :, :, :], ALU.add)
                    dve.drain()
                    for s in range(2):
                        last = tt(hot[:, s, :, :, :].rearrange("p t k a -> p (t k) a"),
                                  rank_ab[:, s, :, :].rearrange("p t k -> p (t k)").unsqueeze(2).to_broadcast([P, NT * TOPK, TOPK]),
                                  iota[:, 0:TOPK].unsqueeze(1).to_broadcast([P, NT * TOPK, TOPK]), ALU.is_equal)
                        if s == 1 if more else s == 0:
                            last.then_inc(s_eq, 1)
                    if not more:
                        dve.drain()
                        tt(hot[:, 1, :, :, :], hot[:, 1, :, :, :],
                           tif[:, 1, :, :].unsqueeze(2).to_broadcast([P, NT, TOPK, TOPK]), ALU.mult)
                        dve.drain()
                        v.tensor_reduce(wsel[:, 2, :, bass.ds(h * TOPK, TOPK)], hot[:, 1, :, :, :], AX_X, ALU.add)
                    dve.wait_ge(s_e, it + 1 + START)
                    v.tensor_reduce(bsum[:, :], best[:, :, :], AX_X, ALU.add)
                    dve.drain()
                    v.reciprocal(bsum[:, :], bsum[:, :])
                    dve.drain()
                    tt(wsel[:, 0, :, bass.ds(h * TOPK, TOPK)], best[:, :, :],
                       bsum[:, :].unsqueeze(2).to_broadcast([P, NT, TOPK]), ALU.mult).then_inc(s_sel, 1)
                with dve.Fori(0, PH - 1) as h:
                    choose(h, True)
                choose(PH - 1, False)
                hold(dve, s_tc, l + 1 + START)
                for t in range(NT):
                    tile = slice(t * P, (t + 1) * P)
                    dve.drain()
                    v.tensor_copy(key_int[:, :, :], wselT[:, 1:3, tile])
                    dve.drain()
                    ts(high_int[:, :, :], key_int[:, :, :], 3, None, ALU.logical_shift_right)
                    ts(low_int[:, :, :], key_int[:, :, :], 7, None, ALU.bitwise_and)
                    dve.drain()
                    v.tensor_copy(high_digit[:, :, :], high_int[:, :, :])
                    v.tensor_copy(low_digit[:, :, :], low_int[:, :, :])
                    dve.drain()
                    with dve.Fori(0, P // (4 * NB)) as g2:
                        for b in range(2):
                            g = l * (T // (2 * NB)) + (t * P // (2 * NB) + b) + g2 * 2
                            tok = g2 * (4 * NB) + b * (2 * NB)
                            dve.wait_ge(s_hotB, g * 2 - 2 + START)
                            for dst, digit, w in ((hot16, high_digit, NKEYS // 8), (hot8, low_digit, 8)):
                                last = tt(dst[:, b, :, :, :], digit[:, :, bass.ds(tok, 2 * NB)].unsqueeze(3).to_broadcast([P, 2, 2 * NB, w]),
                                          iota[:, 0:w].unsqueeze(1).unsqueeze(1).to_broadcast([P, 2, 2 * NB, w]), ALU.is_equal)
                            last.then_inc(s_digit, 1)
                            dve.drain()
                            tt(hot8[:, b, 0, :, :], hot8[:, b, 0, :, :],
                               wselT[:, 0, bass.ds(tok + t * P, 2 * NB)].unsqueeze(2).to_broadcast([P, 2 * NB, 8]), ALU.mult)
                            dve.drain()
                            for q in range(2):
                                dve.wait_ge(s_wm, g * 4 + (q * 2 - 2) + START)
                                digit_product(v, hotA, b, 0, q).then_inc(s_hotA, 1)
                hold(dve, s_wst[1], (l + 1) * (WST[1] * 16) + START)
                def split_h(part):
                    v.tensor_copy(hH[:, part, :], hT[:, part, :])
                    dve.drain()
                    tt(hL[:, part, :], hT[:, part, :], hH[:, part, :].bitcast(F32), ALU.subtract).then_inc(s_hs, 1)

                split_h(slice(0, KC // 2))

                def low_u(i, b):
                    dve.wait_ge(s_utc, i + 1 + START)
                    for q in range(2):
                        last = tt(uL[b][:, 4 * q:4 * q + 4, :], ps[q][:, :].rearrange("p (k n) -> p k n", k=4),
                                  uH[b][:, 4 * q:4 * q + 4, :].bitcast(F32), ALU.subtract)
                    last.then_inc(s_ul, 1)

                def group(n, more):
                    i0 = l * NKEYS + n * EG
                    k0 = (l * NG + n) * KC
                    for g in range(EG):
                        if g + 1 < EG:
                            low_u(i0 + g + 1, (g + 1) % 2)
                        b = g % 2
                        dve.wait_ge(s_w[b], 16 * (l * (NKEYS // 2) + n * (EG // 2) + g // 2 + 1) + START)
                        dve.wait_ge(s_gel, i0 + g + 1 + START)
                        if g == 0:
                            dve.wait_ge(s_vm2, k0 + START)
                        tt(gel[b][:, :], gel[b][:, :], wex[b][:, :], ALU.mult)
                        dve.drain()
                        v.tensor_copy(cH[g][:, :], gel[b][:, :])
                        dve.drain()
                        tt(cL[g][:, :], gel[b][:, :], cH[g][:, :].bitcast(F32), ALU.subtract).then_inc(s_coef, 1)
                        dve.wait_ge(s_vh, i0 + g + 1 + START)
                        tt(vL[g][:, :], vraw[b][:, :], vH[g][:, :].bitcast(F32), ALU.subtract).then_inc(s_vl, 1)
                    if more:
                        low_u(i0 + EG, 0)
                    for k in range(KC):
                        dve.wait_ge(s_vm2, k0 + k + 1 + START)
                        bank = OUT_BANKS[k]
                        for q in range(2):
                            half = slice(q * (T // 2), (q + 1) * (T // 2))
                            last = tt(accT[:, k, half], accT[:, k, half], ps[bank + q][:, 0:T // 2], ALU.add)
                        last.then_inc(s_acc, 1)

                low_u(l * NKEYS, 0)
                split_h(slice(KC // 2, KC))
                v.memset(accT[:, :, :], 0.0)
                with dve.Fori(0, NG - 1) as n:
                    group(n, True)
                group(NG - 1, False)
                dve.drain()
                for k in range(KC):
                    stt(xT[:, k, 0:TP], accT[:, k, 0:TP], modT[:, 40 + k, 0:1], xT[:, k, 0:TP], ALU.mult, ALU.add)
                    stt(xT[:, k, TP:T], accT[:, k, TP:T], modT[:, 40 + k, 1:2], xT[:, k, TP:T], ALU.mult, ALU.add).then_inc(s_x2, 1)
            norm(2 * DEPTH, lambda k, q: cols0[:, 16 + k:17 + k], lambda k, q: None)
            for i in range(2 * NT):
                dve.wait_ge(s_yt, i + 1 + START)
                t, j = i // 2, i % 2
                v.tensor_copy(ynat[:, t, j * 512:(j + 1) * 512], ps[4 + j][:, :]).then_inc(s_yc, 1)


WST = [3, 2]


def fills_before(s, l):
    return l * FILLS[s]


OUT_BANKS = [6, 2, 4, 6, 4, 6, 4, 6]

STEP_BANKS = [(3, 7), (1, 2)]


def step_chunk(i, d):
    if i < 2:
        return i if d == 0 else 1 - i
    return i if d == 0 else 11 - i


def prev_slot(ch, d):
    if ch < 2:
        return ch if d == 0 else 1 - ch
    return ch + 1 if d == 0 else 12 - ch


_INS = ["x_prompt", "x_sample", "state_gla", "c", "c_ctx", "w_mod", "b_mod", "norm1", "w_in", "w_af", "b_af", "w_ab",
        "b_ab", "gla_norm", "w_gla_out", "w_four_out", "w_out", "norm2", "w_query", "sub_keys", "expert_u",
        "expert_v", "final_norm"]
_OUTS = [(1, TP, D), (1, TS, D), (1, DEPTH, 2, HEADS, P, DV)]


def kernel(**inputs):
    import concourse.bacc as _bacc
    from concourse.bass_utils import run_bass_kernel_spmd as _run

    nc = _bacc.Bacc("TRN2", target_bir_lowering=False, num_devices=1)
    arrays, args = {}, []
    for name in _INS:
        a = np.ascontiguousarray(inputs[name])
        arrays[f"in_{name}"] = a
        args.append(nc.dram_tensor(f"in_{name}", a.shape, mybir.dt.from_np(a.dtype), kind="ExternalInput").ap())
    for name, a in zip(("consts", "fourier"), constants()):
        arrays[f"table_{name}"] = a
        args.append(nc.dram_tensor(f"table_{name}", a.shape, F32, kind="ExternalInput").ap())
    for i, shape in enumerate(_OUTS):
        args.append(nc.dram_tensor(f"out_{i}", shape, F32, kind="ExternalOutput").ap())
    build(nc, *args)
    r = _run(nc, [arrays], core_ids=[0])
    return tuple(r.results[0][f"out_{i}"] for i in range(len(_OUTS)))
```
